# Optimizing a Trainium2 kernel written in Bass

```python
import jax, jax.numpy as jnp
from jax import lax
import numpy as np

D_MODEL = 1024
BATCH = 1
SEQ = 512
DEPTH = 2
DEC_BATCH = 8
DEC_SEQ = 8
PAST_LEN = 4096
PAGE_SIZE = 128

H_RET = 4
DK_RET = D_MODEL // 8
DV_RET = D_MODEL // 4
D_RET_QK = H_RET * DK_RET
D_RET_V = H_RET * DV_RET
RET_CHUNK = 128
ROPE_BASE = 10000.0
D_LRU = D_MODEL
N_LRU_BLOCKS = 8
LRU_BLOCK = D_LRU // N_LRU_BLOCKS
CONV_W = 4
RG_C = 8.0
D_FF = 4 * D_MODEL
NORM_EPS = 1e-6
GN_EPS = 1e-5
D_IN = 2 * D_RET_QK + 2 * D_RET_V + 2 * D_LRU + 2 * D_MODEL

kernel_name = 'hybrid_retention_rglru_adaln_step'

def rmsnorm(x, g):
    xf = x.astype(jnp.float32)
    y = xf * lax.rsqrt(jnp.mean(xf * xf, axis=-1, keepdims=True) + NORM_EPS)
    return (y * g.astype(jnp.float32)).astype(x.dtype)

def rope(x, pos):
    half = x.shape[-1] // 2
    inv = ROPE_BASE ** (-jnp.arange(half, dtype=jnp.float32) / half)
    ang = pos.astype(jnp.float32)[:, None] * inv[None, :]
    cos = jnp.cos(ang)[None, :, None, :]
    sin = jnp.sin(ang)[None, :, None, :]
    x1, x2 = x[..., :half], x[..., half:]
    return jnp.concatenate([x1 * cos - x2 * sin, x2 * cos + x1 * sin], axis=-1)

def retention(q, k, v, s0):
    B, L = q.shape[0], q.shape[1]
    C = RET_CHUNK if L % RET_CHUNK == 0 else L
    n = L // C
    log_g = jnp.log1p(-jnp.exp2(-5.0 - jnp.arange(H_RET, dtype=jnp.float32)))
    idx = jnp.arange(C, dtype=jnp.float32)
    diff = idx[:, None] - idx[None, :]
    intra = jnp.where(diff[None] >= 0, jnp.exp(jnp.maximum(diff, 0.0)[None] * log_g[:, None, None]), 0.0)
    q_decay = jnp.exp((idx + 1.0)[None, :] * log_g[:, None])
    k_decay = jnp.exp((C - 1.0 - idx)[None, :] * log_g[:, None])
    chunk_decay = jnp.exp(C * log_g)

    def to_chunks(t):
        return t.reshape(B, n, C, H_RET, t.shape[-1]).transpose(1, 0, 3, 2, 4)

    def step(s, qkv):
        qc, kc, vc = qkv
        scores = jnp.einsum('bhqd,bhkd->bhqk', qc, kc) * intra
        o = (jnp.einsum('bhqk,bhkv->bhqv', scores, vc)
             + jnp.einsum('bhqd,bhdv->bhqv', qc, s) * q_decay[None, :, :, None])
        s = (s * chunk_decay[None, :, None, None]
             + jnp.einsum('bhkd,bhkv->bhdv', kc * k_decay[None, :, :, None], vc))
        return s, o

    s_new, o = lax.scan(step, s0, (to_chunks(q), to_chunks(k), to_chunks(v)))
    o = o.transpose(1, 0, 3, 2, 4).reshape(B, L, H_RET, DV_RET)
    return o, s_new

def rg_lru_block(xl, gl, h0, conv_buf, conv_w, conv_b, w_rg_a, b_rg_a, w_rg_x, b_rg_x, lru_lambda):
    B, L, _ = xl.shape
    f32 = jnp.float32
    xpad = jnp.concatenate([conv_buf.astype(xl.dtype), xl], axis=1)
    conv_new = xpad[:, -(CONV_W - 1):]
    xc = lax.conv_general_dilated(xpad, conv_w[:, None, :].astype(xpad.dtype), window_strides=(1,),
                                  padding='VALID', dimension_numbers=('NWC', 'WIO', 'NWC'),
                                  feature_group_count=D_LRU) + conv_b
    xc = xc.astype(f32)
    xblk = xc.reshape(B, L, N_LRU_BLOCKS, LRU_BLOCK)
    r = jax.nn.sigmoid(jnp.einsum('blni,nij->blnj', xblk, w_rg_a.astype(f32)).reshape(B, L, D_LRU) + b_rg_a.astype(f32))
    i = jax.nn.sigmoid(jnp.einsum('blni,nij->blnj', xblk, w_rg_x.astype(f32)).reshape(B, L, D_LRU) + b_rg_x.astype(f32))
    log_a = -RG_C * r * jax.nn.softplus(-lru_lambda.astype(f32))
    a = jnp.exp(log_a)
    u = jnp.sqrt(-jnp.expm1(2.0 * log_a)) * (i * xc)

    def combine(left, right):
        a1, b1 = left
        a2, b2 = right
        return a1 * a2, a2 * b1 + b2

    a_cum, b_cum = lax.associative_scan(combine, (a, u), axis=1)
    hseq = a_cum * h0.astype(f32)[:, None, :] + b_cum
    y = hseq * jax.nn.gelu(gl.astype(f32))
    return y.astype(xl.dtype), hseq[:, -1], conv_new

def mixer(h, pos, s_ret, s_lru, s_conv, w_in, w_proj_ret, w_proj_lru, w_out,
          conv_w, conv_b, w_rg_a, b_rg_a, w_rg_x, b_rg_x, lru_lambda):
    B, L, _ = h.shape
    f32 = jnp.float32
    z = h @ w_in
    sizes = (D_RET_QK, D_RET_QK, D_RET_V, D_RET_V, D_LRU, D_LRU, D_MODEL, D_MODEL)
    offs = np.cumsum(sizes)[:-1].tolist()
    q, k, v, g, xl, gl, ma, mb = jnp.split(z, offs, axis=-1)
    q = rope(q.reshape(B, L, H_RET, DK_RET).astype(f32), pos)
    k = rope(k.reshape(B, L, H_RET, DK_RET).astype(f32), pos) * (DK_RET ** -0.5)
    v = v.reshape(B, L, H_RET, DV_RET).astype(f32)
    o, s_ret_new = retention(q, k, v, s_ret.astype(f32))
    mu = jnp.mean(o, axis=-1, keepdims=True)
    var = jnp.mean(jnp.square(o - mu), axis=-1, keepdims=True)
    o = (o - mu) * lax.rsqrt(var + GN_EPS)
    o = (o.reshape(B, L, D_RET_V) * jax.nn.silu(g.astype(f32))).astype(h.dtype)
    p_ret = o @ w_proj_ret
    y_lru, s_lru_new, s_conv_new = rg_lru_block(xl, gl, s_lru, s_conv, conv_w, conv_b,
                                                w_rg_a, b_rg_a, w_rg_x, b_rg_x, lru_lambda)
    p_lru = y_lru @ w_proj_lru
    m = jax.nn.sigmoid(ma) * p_ret + jax.nn.sigmoid(mb) * p_lru
    return m @ w_out, s_ret_new, s_lru_new, s_conv_new

def trunk(x, c, pos, s_ret, s_lru, s_conv, w_ada, b_ada, norm1_g, norm2_g, w_in, w_proj_ret,
          w_proj_lru, w_out, conv_w, conv_b, w_rg_a, b_rg_a, w_rg_x, b_rg_x, lru_lambda,
          w_mlp1, w_mlp2, final_g):
    new_ret, new_lru, new_conv = [], [], []
    for l in range(DEPTH):
        ada = jax.nn.silu(c) @ w_ada[l] + b_ada[l]
        sh1, sc1, gt1, sh2, sc2, gt2 = jnp.split(ada[:, None, :], 6, axis=-1)
        h = rmsnorm(x, norm1_g[l]) * (1.0 + sc1) + sh1
        mix, sr, sl, sc = mixer(h, pos, s_ret[l], s_lru[l], s_conv[l], w_in[l], w_proj_ret[l],
                                w_proj_lru[l], w_out[l], conv_w[l], conv_b[l], w_rg_a[l], b_rg_a[l],
                                w_rg_x[l], b_rg_x[l], lru_lambda[l])
        x = x + gt1 * mix
        h2 = rmsnorm(x, norm2_g[l]) * (1.0 + sc2) + sh2
        x = x + gt2 * (jnp.square(jax.nn.relu(h2 @ w_mlp1[l])) @ w_mlp2[l])
        new_ret.append(sr)
        new_lru.append(sl)
        new_conv.append(sc)
    y = rmsnorm(x, final_g)
    return y, jnp.stack(new_ret), jnp.stack(new_lru), jnp.stack(new_conv)

def setup_inputs(seed: int = 0) -> dict:
    key = jax.random.key(seed)
    ks = jax.random.split(key, 32)
    f32 = jnp.float32

    def nrm(k, shape, scale):
        return jax.random.normal(k, shape, f32) * scale

    u = jax.random.uniform(ks[20], (DEPTH, D_LRU), f32, 0.9, 0.999)
    a0 = u ** (1.0 / RG_C)
    lru_lambda = jnp.log(a0) - jnp.log1p(-a0)
    return {
        'x_prompt': nrm(ks[0], (BATCH, SEQ, D_MODEL), 1.0),
        'x_sample': nrm(ks[1], (DEC_BATCH, DEC_SEQ, D_MODEL), 1.0),
        'c_prompt': nrm(ks[2], (BATCH, D_MODEL), 1.0),
        'c_sample': nrm(ks[3], (DEC_BATCH, D_MODEL), 1.0),
        'state_ret': nrm(ks[4], (DEPTH, DEC_BATCH, H_RET, DK_RET, DV_RET), 0.5),
        'state_lru': nrm(ks[5], (DEPTH, DEC_BATCH, D_LRU), 0.5),
        'state_conv': nrm(ks[6], (DEPTH, DEC_BATCH, CONV_W - 1, D_LRU), 1.0),
        'w_ada': nrm(ks[7], (DEPTH, D_MODEL, 6 * D_MODEL), 0.5 * D_MODEL ** -0.5),
        'b_ada': nrm(ks[8], (DEPTH, 6 * D_MODEL), 0.01),
        'norm1_g': 1.0 + nrm(ks[9], (DEPTH, D_MODEL), 0.02),
        'norm2_g': 1.0 + nrm(ks[10], (DEPTH, D_MODEL), 0.02),
        'w_in': nrm(ks[11], (DEPTH, D_MODEL, D_IN), D_MODEL ** -0.5),
        'w_proj_ret': nrm(ks[12], (DEPTH, D_RET_V, D_MODEL), D_RET_V ** -0.5),
        'w_proj_lru': nrm(ks[13], (DEPTH, D_LRU, D_MODEL), D_LRU ** -0.5),
        'w_out': nrm(ks[14], (DEPTH, D_MODEL, D_MODEL), D_MODEL ** -0.5),
        'conv_w': nrm(ks[15], (DEPTH, CONV_W, D_LRU), CONV_W ** -0.5),
        'conv_b': nrm(ks[16], (DEPTH, D_LRU), 0.01),
        'w_rg_a': nrm(ks[17], (DEPTH, N_LRU_BLOCKS, LRU_BLOCK, LRU_BLOCK), LRU_BLOCK ** -0.5),
        'b_rg_a': nrm(ks[18], (DEPTH, D_LRU), 0.01),
        'w_rg_x': nrm(ks[19], (DEPTH, N_LRU_BLOCKS, LRU_BLOCK, LRU_BLOCK), LRU_BLOCK ** -0.5),
        'b_rg_x': nrm(ks[21], (DEPTH, D_LRU), 0.01),
        'lru_lambda': lru_lambda,
        'w_mlp1': nrm(ks[22], (DEPTH, D_MODEL, D_FF), D_MODEL ** -0.5),
        'w_mlp2': nrm(ks[23], (DEPTH, D_FF, D_MODEL), D_FF ** -0.5),
        'final_g': 1.0 + nrm(ks[24], (D_MODEL,), 0.02),
    }

def reference(x_prompt, x_sample, c_prompt, c_sample, state_ret, state_lru, state_conv,
              w_ada, b_ada, norm1_g, norm2_g, w_in, w_proj_ret, w_proj_lru, w_out,
              conv_w, conv_b, w_rg_a, b_rg_a, w_rg_x, b_rg_x, lru_lambda,
              w_mlp1, w_mlp2, final_g):
    f32 = jnp.float32
    bp, lp = x_prompt.shape[0], x_prompt.shape[1]
    pos_p = jnp.arange(lp, dtype=jnp.int32)
    pos_s = PAST_LEN + jnp.arange(x_sample.shape[1], dtype=jnp.int32)
    ret0 = jnp.zeros((DEPTH, bp, H_RET, DK_RET, DV_RET), f32)
    lru0 = jnp.zeros((DEPTH, bp, D_LRU), f32)
    conv0 = jnp.zeros((DEPTH, bp, CONV_W - 1, D_LRU), x_prompt.dtype)
    y_prompt, ret_p, lru_p, conv_p = trunk(
        x_prompt, c_prompt, pos_p, ret0, lru0, conv0, w_ada, b_ada, norm1_g, norm2_g, w_in,
        w_proj_ret, w_proj_lru, w_out, conv_w, conv_b, w_rg_a, b_rg_a, w_rg_x, b_rg_x,
        lru_lambda, w_mlp1, w_mlp2, final_g)
    y_sample, ret_s, lru_s, conv_s = trunk(
        x_sample, c_sample, pos_s, state_ret, state_lru, state_conv, w_ada, b_ada, norm1_g,
        norm2_g, w_in, w_proj_ret, w_proj_lru, w_out, conv_w, conv_b, w_rg_a, b_rg_a, w_rg_x,
        b_rg_x, lru_lambda, w_mlp1, w_mlp2, final_g)
    return (y_prompt, y_sample, ret_p, lru_p, conv_p, ret_s, lru_s, conv_s)


_drawn_inputs = setup_inputs


def setup_inputs(seed=0):
    import zlib

    import numpy as np

    out = dict(_drawn_inputs(seed))
    spreads = {}
    factors = {'norm2_g': 4.523, 'b_rg_a': 38.392, 'b_rg_x': 8.0, 'final_g': 8.224}
    for name, (base, spread) in spreads.items():
        noise = np.random.default_rng([zlib.crc32(name.encode()), seed]).standard_normal(out[name].shape)
        drawn = base * np.exp(spread * noise) if base else spread * noise
        out[name] = __import__('jax').numpy.asarray(drawn.astype(out[name].dtype))
    for name, factor in factors.items():
        out[name] = (out[name] * factor).astype(out[name].dtype)
    return out
```

```python
from contextlib import ExitStack

import numpy as np
import concourse.bass as bass
from concourse import mybir

F32 = mybir.dt.float32
F32R = mybir.dt.float32r
ALU = mybir.AluOpType
ACT = mybir.ActivationFunctionType

DM, SEQ, DEPTH, DB, DS, PAST = 1024, 512, 2, 8, 8, 4096
HEADS, DK, DV, CHUNK = 4, 128, 256, 128
NORM_EPS, GN_EPS, DEC_W = 1e-6, 1e-5, 4
KT = DM // 128
HALF_P, HALF_S = SEQ // 2, DB * DS // 2
HALF = HALF_P + HALF_S
TOK = 2 * HALF
GROUPS = 1 + DB
ADA_COLS = 6 * DM
ADA_GROUPS = ADA_COLS // 512
ADA_TILES = ADA_GROUPS * 4
NB_S = DB * DS

AT_Q, AT_K, AT_V = ADA_TILES, ADA_TILES + 4, ADA_TILES + 8
AT_MA, AT_G, AT_RET, AT_XL, AT_GL, AT_LRU, AT_MB, AT_OUT = (ADA_TILES + 16 + 8 * n for n in range(8))
AT_MLP = AT_OUT + 8
QUARTERS = 4
LAYER_TILES = AT_MLP + QUARTERS * 16
ADA_SKIP = ADA_TILES - ADA_GROUPS
LAYER_GROUPS = LAYER_TILES - ADA_SKIP
STREAM = DEPTH * LAYER_TILES + 2

_off = {}
_n = 0
for _name, _w in (("cos", TOK), ("sin", TOK), ("qdec", HEADS * (CHUNK + DS)), ("mask", HEADS * CHUNK),
                  ("mask_s", HEADS * NB_S), ("kdm", HEADS * DB), ("kdec", HEADS), ("cdec", HEADS),
                  ("cdec_s", HEADS), ("ident", 128), ("mean", 128), ("sel", 96)):
    _off[_name] = (_n, _n + _w)
    _n += _w
NCONST = _n
S_BADA, S_G1, S_G2, S_CW, S_CB, S_BA, S_BX, S_LAM, NSMALL = 0, 48, 56, 64, 96, 104, 112, 120, 128


class Chain:

    def __init__(self, eng, sem, base):
        self.eng, self.sem, self.base, self.n = eng, sem, base, 0

    def link(self, ins, carry=None):
        self.n += 1
        ins.then_inc(self.sem, 1)
        self.eng.wait_ge(self.sem, self.base + self.n)
        if carry is not None:
            carry(self.eng)


def one(buf, m):
    return buf[:, bass.ds(m, 1), :].rearrange("p o (a b) -> p (o a) b", a=2)


def prompt(tile):
    return tile[:, :, 0:HALF_P]


def sample(tile):
    return tile[:, :, HALF_P:HALF]


def build(nc, stream, x_in, c_in, small_in, fg_in, h0_in, conv_in, wrg_in, state_in, const_in,
          y_out, ret_p_out, lru_out, conv_out, ret_s_out):
    ctx = ExitStack()
    with ctx:
        at = [(nc.sbuf_base + 31) // 32 * 32]

        def place(name, shape, dt=F32, offset=None):
            size = int(np.prod(shape[1:])) * 4
            if offset is None:
                offset = at[0]
                at[0] += (size + 31) // 32 * 32
                assert at[0] <= nc.sbuf_usable_end, (name, at[0])
            t = nc.alloc_sbuf_tensor_at(name, shape, dt, offset=offset)
            offs[name] = offset
            return t

        offs = {}
        raw = place("raw", [128, 4, 1024])
        weight_h = place("weight_h", [128, 2, 1024], F32R)
        weight_l = place("weight_l", [128, 2, 1024], F32R)
        x = place("x", [128, KT, TOK])
        h_hi = place("h_hi", [128, KT, TOK], F32R)
        h_lo = place("h_lo", [128, KT, TOK], F32R)
        b_hi = place("b_hi", [128, KT, TOK], F32R)
        b_lo = place("b_lo", [128, KT, TOK], F32R)
        mix = place("mix", [128, KT, TOK])
        qk = place("qk", [128, KT, TOK])
        o_t = place("o_t", [128, KT, TOK], F32, offs["b_hi"])
        tmp = place("tmp", [128, 8, TOK])
        tmp_end = at[0]
        place("tmp_tail", [128, 512])
        v_tok = place("v_tok", [128, SEQ // 128, DM], F32, offs["tmp"])
        v_s = place("v_s", [128, DM], F32, offs["tmp"] + 4 * DM * 4)
        ada_row = place("ada_row", [128, 2, 512], F32, offs["tmp"])
        del tmp_end
        lo = offs["b_lo"]
        s_p = place("s_p", [128, 2, DV], F32, lo)
        on_p = place("on_p", [128, 2, DV], F32, lo + 2048)
        p_m = place("p_m", [128, 2, CHUNK], F32, lo + 4096)
        kd_p = place("kd_p", [128, 2, DK], F32, lo + 5120)
        k_st = place("k_st", [128, 2, 2, CHUNK], F32, lo + 6144)
        q_st = place("q_st", [128, 2, 2, CHUNK], F32, lo + 8192)
        s_s = place("s_s", [128, 2, DB, DV], F32, lo)
        k_ss = place("k_ss", [128, NB_S], F32, lo + 16640)
        on_s = place("on_s", [128, DV], F32, lo + 16896)
        wrg = place("wrg", [128, 4, 256])
        kd_s = place("kd_s", [128, DB, DK], F32, offs["wrg"])
        q_sm = place("q_sm", [128, DB * 72])
        p_ms = place("p_ms", [128, 128])
        extra = place("extra", [128, TOK])
        const = place("const", [128, NCONST])
        small = place("small", [128, DEPTH, NSMALL])
        fg = place("fg", [128, KT])
        h0 = place("h0", [128, DEPTH * KT, DB])
        conv0 = place("conv0", [128, DEPTH * KT, DB, 3])
        lru_c = place("lru_c", [128, DEPTH * KT, GROUPS])
        conv_c = place("conv_c", [128, DEPTH * KT, GROUPS, 3])
        ada = place("ada", [128, 6 * KT, GROUPS])
        scale1 = place("scale1", [128, KT, GROUPS])
        scale2 = place("scale2", [128, KT, GROUPS])
        c_hl = place("c_hl", [128, KT * 18 + 110], F32R)
        sp_pos = place("sp_pos", [128, DEPTH * KT])
        sp_neg = place("sp_neg", [128, DEPTH * KT])
        half_ba = place("half_ba", [128, DEPTH * KT])
        half_bx = place("half_bx", [128, DEPTH * KT])
        bst = place("bst", [128, 2, 6])
        mv = place("mv", [128, 2, 2])
        gstd = place("gstd", [128, 2])
        grs = place("grs", [128, 2])
        eps_n = place("eps_n", [128, 1])
        eps_g = place("eps_g", [128, 1])

        def cst(name, rows=128):
            a, b = _off[name]
            return const[0:rows, a:b]

        cos = cst("cos").rearrange("p (a b) -> p a b", a=2)
        sin = cst("sin").rearrange("p (a b) -> p a b", a=2)
        qdec = cst("qdec").rearrange("p (h t) -> p h t", h=HEADS)
        mask = cst("mask").rearrange("p (h t) -> p h t", h=HEADS)
        mask_s = cst("mask_s", NB_S).rearrange("p (h t) -> p h t", h=HEADS)
        kdm = cst("kdm", NB_S).rearrange("p (h t) -> p h t", h=HEADS)
        kdec, cdec, cdec_s = cst("kdec"), cst("cdec"), cst("cdec_s")
        ident, mean_w, sel = cst("ident"), cst("mean"), cst("sel")

        acc = [ctx.enter_context(nc.psum_tensor(f"acc{n}", [128, 2, 512], F32)) for n in range(2)]
        misc = ctx.enter_context(nc.psum_tensor("misc", [128, 4, 512], F32))

        def sem(name):
            return ctx.enter_context(nc.semaphore(name))

        raw_loaded = [sem(f"raw_loaded{n}") for n in range(4)]
        h_split, l_split, tile_done, acc_free = sem("h_split"), sem("l_split"), sem("tile_done"), sem("acc_free")
        params_loaded, setup_act, setup_dve = sem("params_loaded"), sem("setup_act"), sem("setup_dve")
        ada_turned, ada_ready, scales_ready = sem("ada_turned"), sem("ada_ready"), sem("scales_ready")
        squares_ready, square_chain, mean_ready, std_ready = sem("squares_ready"), sem("square_chain"), sem("mean_ready"), sem("std_ready")
        rstd_ready, xn_ready, xn_chain, h_rounded, h_ready = sem("rstd_ready"), sem("xn_ready"), sem("xn_chain"), sem("h_rounded"), sem("h_ready")
        qk_ready, v_turned, v_ready = sem("qk_ready"), sem("v_turned"), sem("v_ready")
        ma_ready = sem("ma_ready")
        stage_ready, scores_ready, masked_ready = sem("stage_ready"), sem("scores_ready"), sem("masked_ready")
        o_ready, s_ready, mv_ready, gstd_ready, norm_chain = sem("o_ready"), sem("s_ready"), sem("mv_ready"), sem("gstd_ready"), sem("norm_chain")
        on_ready, on_turned, o_t_ready, ret_p_stored = sem("on_ready"), sem("on_turned"), sem("o_t_ready"), sem("ret_p_stored")
        state_loaded, state_stored = [sem(f"state_loaded{n}") for n in range(2)], [sem(f"state_stored{n}") for n in range(2)]
        s_stage_ready, s_scores_ready, s_masked_ready = sem("s_stage_ready"), sem("s_scores_ready"), sem("s_masked_ready")
        s_o_ready, s_update_ready, s_state_ready = sem("s_o_ready"), sem("s_update_ready"), sem("s_state_ready")
        s_mv_ready, s_gstd_ready, s_chain, s_on_ready = sem("s_mv_ready"), sem("s_gstd_ready"), sem("s_chain"), sem("s_on_ready")
        s_turned, s_o_t_ready = sem("s_turned"), sem("s_o_t_ready")
        g_sig, g_chain, g_gated, g_rounded, o_ready_hl = sem("g_sig"), sem("g_chain"), sem("g_gated"), sem("g_rounded"), sem("o_ready_hl")
        ret_mixed = sem("ret_mixed")
        conv_chain, conv_kept = sem("conv_chain"), sem("conv_kept")
        wrg_loaded = [sem(f"wrg_loaded{n}") for n in range(4)]
        gates_ready, gates_read, r_ready, a_ready, e_ready, e_root = sem("gates_ready"), sem("gates_read"), sem("r_ready"), sem("a_ready"), sem("e_ready"), sem("e_root")
        lru_chain, cube_chain, cube_ready, gelu_ready, y_ready, y_rounded, y_split = (
            sem("lru_chain"), sem("cube_chain"), sem("cube_ready"), sem("gelu_ready"), sem("y_ready"), sem("y_rounded"), sem("y_split"))
        mb_sig, mb_chain, mb_mixed, m_rounded, m_split = sem("mb_sig"), sem("mb_chain"), sem("mb_mixed"), sem("m_rounded"), sem("m_split")
        gate_chain, x_mixed, x_mlp = sem("gate_chain"), sem("x_mixed"), sem("x_mlp")
        relu_ready, u_ready, u_rounded, u_split = sem("relu_ready"), sem("u_ready"), sem("u_rounded"), sem("u_split")
        y_done, stored, waited = sem("y_done"), sem("stored"), sem("waited")

        def carry(eng):
            eng.sem_inc(waited, 1)

        block = ctx.enter_context(nc.Block())

        @block.sync
        def _(sp):
            def load(t, slot):
                sp.dma_start(raw[:, slot, :], stream[bass.ds(t, 1)].rearrange("o p n -> (o p) n")).then_inc(raw_loaded[slot], 16)

            for t in range(4):
                sp.dma_start(raw[:, t, :], stream[t]).then_inc(raw_loaded[t], 16)
            with sp.Fori(1, STREAM // 4) as i:
                for j in range(4):
                    sp.wait_ge(l_split, i * 4 + (j - 3))
                    load(i * 4 + j, j)
            for j in range(STREAM % 4):
                t = STREAM // 4 * 4 + j
                sp.wait_ge(l_split, t - 3)
                sp.dma_start(raw[:, j, :], stream[t]).then_inc(raw_loaded[j], 16)

        @block.scalar
        def _(act):
            A = nc.scalar.activation
            loads = [(small[:], small_in), (const[:], const_in), (x[:], x_in), (fg[:], fg_in), (h0[:], h0_in), (conv0[:], conv_in)]
            act.dma_start(tmp[:, 0, 0:KT * GROUPS], c_in).then_inc(params_loaded, 16)
            for dst, src in loads:
                act.dma_start(dst, src).then_inc(params_loaded, 16)
            act.wait_ge(params_loaded, 16 * 7)
            c_raw, c_sig, c_silu = (tmp[:, n, 0:KT * GROUPS] for n in range(3))
            A(c_sig, c_raw, ACT.Sigmoid).then_inc(setup_act, 1)
            lam = small[:, :, S_LAM:S_LAM + KT]
            e_abs, e_neg = tmp[:, 3, 0:16].rearrange("p (l k) -> p l k", l=2), tmp[:, 4, 0:16]
            A(e_abs, lam, ACT.Abs).then_inc(setup_act, 1)
            act.wait_ge(setup_act, 2)
            A(e_neg, tmp[:, 3, 0:16], ACT.Exp, scale=-1.0).then_inc(setup_act, 1)
            act.wait_ge(setup_dve, 2)
            c_v = c_hl[:, 0:KT * 18].rearrange("p (k s) -> p k s", s=18)
            A(c_v[:, :, 0:GROUPS], c_silu.rearrange("p (k s) -> p k s", s=GROUPS), ACT.Copy).then_inc(setup_act, 1)
            for t in range(2):
                act.wait_ge(raw_loaded[t], 16)
                A(weight_h[:, t, :], raw[:, t, :], ACT.Copy).then_inc(h_split, 1)

            def split_h(lay, off, i, j):
                act.wait_ge(tile_done, lay * LAYER_TILES + i * 4 + (off + j + 1))
                act.wait_ge(raw_loaded[(j + 2) % 4], lay * (LAYER_TILES * 4) + i * 16 + 16 * (off // 4 + (j + 2) // 4 + 1))
                A(weight_h[:, j % 2, :], raw[:, (j + 2) % 4, :], ACT.Copy).then_inc(h_split, 1)

            def copied(lay, off, i, j):
                act.wait_ge(acc_free, lay * LAYER_GROUPS + i * 4 + (off - ADA_SKIP + j + 3))

            def plain(lay, off, iters):
                with act.Fori(0, iters) as i:
                    for j in range(4):
                        split_h(lay, off, i, j)

            def norm(lay, which, scale, shift_at):
                n = lay * 2 + which
                act.wait_ge(mean_ready, n + 1)
                A(qk[:, 2, :].rearrange("p (a b) -> p a b", a=2), misc[:, 0:2, 0:HALF], ACT.Sqrt, bias=eps_n[:]).then_inc(std_ready, 1)
                with act.Fori(0, KT) as m:
                    act.wait_ge(xn_ready, n * KT + m + 1)
                    sc = scale[:, bass.ds(m, 1), 0:1].rearrange("p o a -> p (o a)")
                    sh = ada[:, bass.ds(m + shift_at, 1), 0:1].rearrange("p o a -> p (o a)")
                    A(prompt(one(mix, m)), prompt(one(tmp, m)), ACT.Identity, bias=sh, scale=sc)
                    A(prompt(one(h_hi, m)), prompt(one(tmp, m)), ACT.Identity, bias=sh, scale=sc)
                    A(sample(one(h_hi, m)), sample(one(mix, m)), ACT.Copy).then_inc(h_rounded, 1)

            with act.Fori(0, DEPTH) as lay:
                plain(lay, 0, ADA_TILES // 4)
                norm(lay, 0, scale1, 0)
                for j in range(4):
                    split_h(lay, AT_Q, 0, j)
                for j in range(4):
                    split_h(lay, AT_K, 0, j)

                with act.Fori(0, 2) as i:
                    for j in range(4):
                        split_h(lay, AT_V, i, j)
                        n, m = lay * 8 + i * 4 + j, i * 4 + j
                        act.wait_ge(v_turned, n + 1)
                        A(v_tok[:, :, bass.ds(m * 128, 128)], misc[:, 0, :].rearrange("p (c d) -> p c d", c=4), ACT.Copy)
                        A(v_s[0:NB_S, bass.ds(m * 128, 128)], misc[0:NB_S, 1, 0:128], ACT.Copy).then_inc(v_ready, 1)

                def o_evac(i, c, n):
                    act.wait_ge(on_turned, n + 1)
                    dst = o_t[:, bass.ds(i * 4, 4), (c // 2) * HALF + (c % 2) * CHUNK:(c // 2) * HALF + (c % 2) * CHUNK + CHUNK]
                    A(dst, misc[:, 3, :].rearrange("p (c d) -> p c d", c=4), ACT.Copy).then_inc(o_t_ready, 1)

                with act.Fori(0, 2) as i:
                    for c in range(4):
                        n = lay * 8 + i * 4 + c
                        if c:
                            o_evac(i, c - 1, lay * 8 + i * 4 + (c - 1))
                        split_h(lay, AT_MA, i, c)
                        copied(lay, AT_MA, i, c)
                        A(one(mix, i * 4 + c), one(mix, i * 4 + c), ACT.Sigmoid).then_inc(ma_ready, 1)
                        act.wait_ge(mv_ready, n + 1)
                        A(gstd[:], mv[:, :, 1], ACT.Sqrt, bias=eps_g[:]).then_inc(gstd_ready, 1)
                    o_evac(i, 3, n)
                    act.wait_ge(s_ready, n + 1)
                    act.dma_start(ret_p_out[bass.ds(lay * 4 + i * 2, 2)].rearrange("h p n -> p h n"), s_p[:]).then_inc(ret_p_stored, 16)

                act.wait_ge(ret_p_stored, lay * 32 + 32)
                with act.Fori(0, 2) as i:
                    for e in range(2):
                        act.wait_ge(state_stored[e], lay * 32 + i * 16)
                        act.dma_start(s_s[:, e], state_in[bass.ds(lay, 1), :, bass.ds(i * 2 + e, 1)].rearrange("l b h p n -> p (l b h) n")).then_inc(state_loaded[e], 16)
                    for e in range(2):
                        n = lay * 4 + i * 2 + e
                        act.wait_ge(s_mv_ready, n + 1)
                        A(gstd[0:NB_S, 0:1], mv[0:NB_S, 0, 1:2], ACT.Sqrt, bias=eps_g[0:NB_S]).then_inc(s_gstd_ready, 1)
                        act.wait_ge(s_turned, n + 1)
                        for half in range(2):
                            last = A(sample(one(o_t, i * 4 + (2 * e + half))), misc[:, 0, 256 + 64 * half:320 + 64 * half].rearrange("p (a b) -> p a b", a=2), ACT.Copy)
                        last.then_inc(s_o_t_ready, 1)
                        act.wait_ge(s_state_ready, n * 4 + 4)
                        act.dma_start(ret_s_out[bass.ds(lay, 1), :, bass.ds(i * 2 + e, 1)].rearrange("l b h p n -> p (l b h) n"), s_s[:, e]).then_inc(state_stored[e], 16)
                for e in range(2):
                    act.wait_ge(state_stored[e], lay * 32 + 32)

                with act.Fori(0, 2) as i:
                    for j in range(4):
                        n, m = lay * 8 + i * 4 + j, i * 4 + j
                        split_h(lay, AT_G, i, j)
                        copied(lay, AT_G, i, j)
                        A(tmp[:, 2 + j % 2, :], tmp[:, j % 2, :], ACT.Sigmoid).then_inc(g_sig, 1)
                        act.wait_ge(g_gated, n + 1)
                        A(one(b_hi, m), tmp[:, 6 + j % 2, :].rearrange("p (a b) -> p a b", a=2), ACT.Copy).then_inc(g_rounded, 1)

                plain(lay, AT_RET, 2)
                for j in range(4):
                    act.dma_start(wrg[:, j, :], wrg_in[bass.ds(lay * 8 + j, 1)].rearrange("o p n -> (o p) n")).then_inc(wrg_loaded[j], 16)
                plain(lay, AT_XL, 2)

                with act.Fori(0, 2) as i:
                    for j in range(4):
                        n, m = lay * 8 + i * 4 + j, i * 4 + j
                        lm = lay * 8 + i * 4 + j
                        col = lambda b: b[:, bass.ds(lm, 1)]
                        act.wait_ge(gates_ready, n + 1)
                        act.wait_ge(y_split, n)
                        act.wait_ge(conv_kept, lay * 8 + 8)
                        t0, t1, t2, t3, t4, t5 = (tmp[:, q, :].rearrange("p (a b) -> p a b", a=2) for q in range(6))
                        A(t0, misc[:, 0:2, 0:HALF], ACT.Tanh, bias=col(half_ba), scale=0.5)
                        A(t1, misc[:, 2:4, 0:HALF], ACT.Tanh, bias=col(half_bx), scale=0.5).then_inc(gates_read, 1)
                        act.wait_ge(r_ready, n + 1)
                        A(t2, t0, ACT.Tanh, scale=col(sp_pos))
                        A(t3, t0, ACT.Exp, scale=col(sp_neg)).then_inc(a_ready, 1)
                        act.wait_ge(e_ready, n + 1)
                        A(t5, t4, ACT.Sqrt, scale=0.25).then_inc(e_root, 1)
                        split_h(lay, AT_GL, i, j)
                        act.wait_ge(cube_ready, n + 1)
                        A(tmp[:, 5, :], extra[:], ACT.Tanh, scale=0.7978845608028654).then_inc(gelu_ready, 1)
                        act.wait_ge(y_ready, n + 1)
                        A(one(b_hi, m), t0, ACT.Copy).then_inc(y_rounded, 1)
                    for j in range(4):
                        act.dma_start(wrg[:, j, :], wrg_in[bass.ds(lay * 8 + (j + 4), 1)].rearrange("o p n -> (o p) n")).then_inc(wrg_loaded[j], 16)

                plain(lay, AT_LRU, 2)
                with act.Fori(0, 2) as i:
                    for j in range(4):
                        n, m = lay * 8 + i * 4 + j, i * 4 + j
                        split_h(lay, AT_MB, i, j)
                        copied(lay, AT_MB, i, j)
                        A(tmp[:, 2 + j % 2, :], tmp[:, j % 2, :], ACT.Sigmoid).then_inc(mb_sig, 1)
                        act.wait_ge(mb_mixed, n + 1)
                        A(one(b_hi, m), tmp[:, 6 + j % 2, :].rearrange("p (a b) -> p a b", a=2), ACT.Copy).then_inc(m_rounded, 1)
                plain(lay, AT_OUT, 2)
                norm(lay, 1, scale2, 3 * KT)
                with act.Fori(0, QUARTERS) as qt:
                    with act.Fori(0, 2) as i:
                        for j in range(4):
                            n, m = lay * 32 + qt * 8 + i * 4 + j, i * 4 + j
                            split_h(lay, AT_MLP, qt * 4 + i, j)
                            act.wait_ge(u_ready, n + 1)
                            A(one(b_hi, m), tmp[:, 2 + j % 2, :].rearrange("p (a b) -> p a b", a=2), ACT.Copy).then_inc(u_rounded, 1)
                    with act.Fori(0, 2) as i:
                        for j in range(4):
                            split_h(lay, AT_MLP + 8, qt * 4 + i, j)

            act.wait_ge(mean_ready, 2 * DEPTH + 1)
            A(qk[:, 2, :].rearrange("p (a b) -> p a b", a=2), misc[:, 0:2, 0:HALF], ACT.Sqrt, bias=eps_n[:]).then_inc(std_ready, 1)
            act.wait_ge(y_split, DEPTH * 8)
            act.wait_ge(conv_kept, DEPTH * 8)
            act.dma_start(lru_out, lru_c[:]).then_inc(stored, 16)
            act.dma_start(conv_out, conv_c[:]).then_inc(stored, 16)
            act.wait_ge(y_done, KT)
            act.dma_start(y_out, tmp[:]).then_inc(stored, 16)
            act.wait_ge(stored, 48)
            for j in range(4):
                act.wait_ge(wrg_loaded[j], 16 * 3 * DEPTH)

        @block.vector
        def _(dve):
            V = nc.vector
            dve.sem_inc(acc_free, 2)
            V.memset(eps_n[:], NORM_EPS)
            V.memset(eps_g[:], GN_EPS)
            V.memset(q_sm[:], 0.0)
            V.memset(p_ms[:], 0.0)
            V.memset(c_hl[:].bitcast(F32), 0.0).then_inc(setup_dve, 1)
            c_raw, c_sig, c_silu = (tmp[:, n, 0:KT * GROUPS] for n in range(3))
            dve.wait_ge(setup_act, 1)
            dve.wait_ge(setup_dve, 1)
            V.tensor_tensor(c_silu, c_raw, c_sig, ALU.mult).then_inc(setup_dve, 1)
            dve.wait_ge(setup_act, 4)
            c_v = c_hl[:, 0:KT * 18].rearrange("p (k s) -> p k s", s=18)
            V.tensor_tensor(c_v[:, :, GROUPS:18], c_silu.rearrange("p (k s) -> p k s", s=GROUPS), c_v[:, :, 0:GROUPS].bitcast(F32), ALU.subtract).then_inc(setup_dve, 1)
            lam = small[:, :, S_LAM:S_LAM + KT]
            e, d, s, s2, p, rl = (tmp[:, 4, 16 * n:16 * n + 16] for n in range(6))
            ch = Chain(dve, setup_dve, 3)
            ch.link(V.tensor_scalar(d, e, 2.0, None, ALU.add))
            ch.link(V.reciprocal(p, d))
            ch.link(V.tensor_tensor(s, e, p, ALU.mult))
            ch.link(V.tensor_tensor(s2, s, s, ALU.mult))
            ch.link(V.tensor_scalar(p, s2, 1.0 / 15, None, ALU.mult))
            for k in (13, 11, 9, 7, 5, 3):
                ch.link(V.scalar_tensor_tensor(p, p, 1.0 / k, s2, ALU.add, ALU.mult))
            ch.link(V.scalar_tensor_tensor(p, p, 1.0, s, ALU.add, ALU.mult))
            ch.link(V.tensor_scalar(rl.rearrange("p (l k) -> p l k", l=2), lam, -1.0, 0.0, ALU.mult, ALU.max))
            ch.link(V.scalar_tensor_tensor(s, p, 2.0, rl, ALU.mult, ALU.add))
            V.tensor_scalar(sp_pos[:], s, 8.0, None, ALU.mult)
            V.tensor_scalar(sp_neg[:], s, -8.0, None, ALU.mult)
            V.tensor_scalar(half_ba[:].rearrange("p (l k) -> p l k", l=2), small[:, :, S_BA:S_BA + KT], 0.5, None, ALU.mult)
            ch.link(V.tensor_scalar(half_bx[:].rearrange("p (l k) -> p l k", l=2), small[:, :, S_BX:S_BX + KT], 0.5, None, ALU.mult))
            for t in range(2):
                dve.wait_ge(h_split, t + 1)
                V.tensor_tensor(weight_l[:, t, :], raw[:, t, :], weight_h[:, t, :].bitcast(F32), ALU.subtract).then_inc(l_split, 1)

            def split_l(lay, off, i, j):
                dve.wait_ge(h_split, lay * LAYER_TILES + i * 4 + (off + j + 3))
                V.tensor_tensor(weight_l[:, j % 2, :], raw[:, (j + 2) % 4, :], weight_h[:, j % 2, :].bitcast(F32), ALU.subtract).then_inc(l_split, 1)

            def done(lay, off, i, j):
                dve.wait_ge(tile_done, lay * LAYER_TILES + i * 4 + (off + j + 1))

            def copied(lay, off, i, j):
                dve.wait_ge(acc_free, lay * LAYER_GROUPS + i * 4 + (off - ADA_SKIP + j + 3))

            def norm(lay, which, scale, shift_at):
                n = lay * 2 + which
                std, rstd = qk[:, 2, :], qk[:, 3, :]
                rv = rstd.rearrange("p (a b) -> p a b", a=2)
                dve.wait_ge(std_ready, n + 1)
                V.reciprocal(rstd, std).then_inc(rstd_ready, 1)
                dve.wait_ge(rstd_ready, n + 1)

                def normed(m, base):
                    ch = Chain(dve, xn_chain, base)
                    ch.link(V.tensor_tensor(one(tmp, m), one(x, m), rv, ALU.mult))
                    xs = one(tmp, m)[:, :, HALF_P:HALF].rearrange("p a (b t) -> p a b t", t=DS)
                    hs = one(mix, m)[:, :, HALF_P:HALF].rearrange("p a (b t) -> p a b t", t=DS)
                    sc = scale[:, bass.ds(m, 1), 1:GROUPS].rearrange("p o (a b) -> p (o a) b", a=2).unsqueeze(3).to_broadcast([128, 2, 4, DS])
                    sh = ada[:, bass.ds(m + shift_at, 1), 1:GROUPS].rearrange("p o (a b) -> p (o a) b", a=2).unsqueeze(3).to_broadcast([128, 2, 4, DS])
                    ch.link(V.tensor_tensor(xs, xs, sc, ALU.mult))
                    V.tensor_tensor(hs, xs, sh, ALU.add).then_inc(xn_ready, 1)

                def lower(m):
                    dve.wait_ge(h_rounded, n * KT + m + 1)
                    V.tensor_tensor(one(h_lo, m), one(mix, m), one(h_hi, m).bitcast(F32), ALU.subtract).then_inc(h_ready, 1)

                normed(0, n * 16)
                with dve.Fori(0, KT - 1) as m:
                    normed(m + 1, n * 16 + m * 2 + 2)
                    lower(m)
                lower(KT - 1)

            with dve.Fori(0, DEPTH) as lay:
                dve.wait_ge(x_mlp, lay * 32)
                carry(dve)
                with dve.Fori(0, ADA_GROUPS // 2) as i:
                    for g in range(2):
                        for j in range(4):
                            split_l(lay, 0, i * 2 + g, j)
                        n = lay * ADA_GROUPS + i * 2 + g
                        done(lay, 0, i * 2 + g, 3)
                        V.tensor_copy(ada_row[:, g, :], acc[g][:, 0, :]).then_inc(acc_free, 1)
                        dve.wait_ge(ada_turned, n + 1)
                        src = misc[:, 0, 0:384].rearrange("p (q c) -> p q c", q=4)[:, :, 0:GROUPS]
                        bias = small[:, bass.ds(lay, 1), bass.ds((i * 2 + g) * 4, 4)].rearrange("p o q -> p (o q)").unsqueeze(2).to_broadcast([128, 4, GROUPS])
                        V.tensor_tensor(ada[:, bass.ds((i * 2 + g) * 4, 4), :], src, bias, ALU.add).then_inc(ada_ready, 1)
                dve.wait_ge(ada_ready, lay * ADA_GROUPS + ADA_GROUPS)
                for scale, seg, g_at in ((scale1, 1, S_G1), (scale2, 4, S_G2)):
                    gb = small[:, bass.ds(lay, 1), g_at:g_at + KT].rearrange("p o k -> p (o k)").unsqueeze(2).to_broadcast([128, KT, GROUPS])
                    V.scalar_tensor_tensor(scale[:], ada[:, seg * KT:(seg + 1) * KT, :], 1.0, gb, ALU.add, ALU.mult).then_inc(scales_ready, 1)
                dve.wait_ge(scales_ready, lay * 2 + 2)
                norm(lay, 0, scale1, 0)

                for off, factor in ((AT_Q, 1.0), (AT_K, DK ** -0.5)):
                    for j in range(4):
                        split_l(lay, off, 0, j)
                        done(lay, off, 0, j)
                        a = acc[j % 2][:, :, 0:HALF]
                        c0 = 4 * (j % 2)
                        t1, t2 = (o_t[:, c0 + q, :].rearrange("p (a b) -> p a b", a=2) for q in range(2))
                        dve.wait_ge(qk_ready, lay * 8 + max(off - AT_Q + j - 1, 0))
                        V.scalar_tensor_tensor(t1, a, factor, cos, ALU.mult, ALU.mult)
                        V.scalar_tensor_tensor(t2[0:64], a[64:128], factor, sin[64:128], ALU.mult, ALU.mult)
                        V.scalar_tensor_tensor(t2[64:128], a[0:64], factor, sin[0:64], ALU.mult, ALU.mult).then_inc(acc_free, 1)
                        copied(lay, off, 0, j)
                        V.tensor_tensor(qk[:, off - AT_Q + j, :], o_t[:, c0, :], o_t[:, c0 + 1, :], ALU.add).then_inc(qk_ready, 1)

                with dve.Fori(0, 2) as i:
                    for j in range(4):
                        split_l(lay, AT_V, i, j)
                        done(lay, AT_V, i, j)
                        dst = o_t[:, 2 + j % 2, :]
                        V.tensor_copy(dst[:, 0:SEQ].rearrange("p (a b) -> p a b", a=2), prompt(acc[j % 2]))
                        V.tensor_copy(dst[:, SEQ:TOK].rearrange("p (a b) -> p a b", a=2), sample(acc[j % 2])).then_inc(acc_free, 1)

                with dve.Fori(0, 2) as i:
                    dve.wait_ge(ret_p_stored, lay * 32 + i * 16)
                    V.memset(s_p[:], 0.0)
                    for c in range(4):
                        n = lay * 8 + i * 4 + c
                        dve.wait_ge(scores_ready, n + 1)
                        for e in range(2):
                            h = i * 2 + e
                            V.tensor_tensor(p_m[:, e, :], misc[:, 0, e * 256:e * 256 + 128], mask[:, bass.ds(h, 1), :].rearrange("p o t -> p (o t)"), ALU.mult)
                            last = V.tensor_scalar(kd_p[:, e, :], misc[:, 0, e * 256 + 128:e * 256 + 256], kdec[:, bass.ds(h, 1)], None, ALU.mult)
                        last.then_inc(masked_ready, 1)
                        split_l(lay, AT_MA, i, c)
                        done(lay, AT_MA, i, c)
                        V.tensor_copy(one(mix, i * 4 + c), acc[c % 2][:, :, 0:HALF]).then_inc(acc_free, 1)
                        dve.wait_ge(o_ready, n + 1)
                        for e in range(2):
                            last = V.scalar_tensor_tensor(s_p[:, e, :], s_p[:, e, :], cdec[:, bass.ds(i * 2 + e, 1)], misc[:, 2, e * 256:e * 256 + 256], ALU.mult, ALU.add)
                        last.then_inc(s_ready, 1)
                        ch = Chain(dve, norm_chain, n * 2)
                        V.bn_stats(bst[:, 0, :], misc[:, 1, 0:256])
                        ch.link(V.bn_stats(bst[:, 1, :], misc[:, 1, 256:512]), carry)
                        V.bn_aggr(mv[:, 0, :], bst[:, 0, :])
                        V.bn_aggr(mv[:, 1, :], bst[:, 1, :]).then_inc(mv_ready, 1)
                        dve.wait_ge(gstd_ready, n + 1)
                        ch.link(V.reciprocal(grs[:], gstd[:]))
                        for e in range(2):
                            last = V.tensor_scalar(on_p[:, e, :], misc[:, 1, e * 256:e * 256 + 256], mv[:, e, 0:1], grs[:, e:e + 1], ALU.subtract, ALU.mult)
                        last.then_inc(on_ready, 1)

                for j in range(4):
                    dve.wait_ge(wrg_loaded[j], lay * 48)
                carry(dve)
                with dve.Fori(0, 2) as i:
                    for e in range(2):
                        h = i * 2 + e
                        n = lay * 4 + i * 2 + e
                        dve.wait_ge(s_scores_ready, n + 1)
                        V.tensor_tensor(p_ms[0:NB_S, 0:NB_S], misc[0:NB_S, 0, 0:NB_S], mask_s[:, bass.ds(h, 1), :].rearrange("p o t -> p (o t)"), ALU.mult)
                        kt = misc[0:NB_S, 0, 128:256].unsqueeze(1).to_broadcast([NB_S, DB, DK])
                        km = kdm[:, bass.ds(h, 1), :].rearrange("p o b -> p (o b)").unsqueeze(2).to_broadcast([NB_S, DB, DK])
                        V.tensor_tensor(kd_s[0:NB_S], kt, km, ALU.mult).then_inc(s_masked_ready, 1)
                        dve.wait_ge(s_o_ready, n + 1)
                        ch = Chain(dve, s_chain, n * 2)
                        o = misc[0:NB_S, 1, 0:DV]
                        ch.link(V.bn_stats(bst[0:NB_S, 0, :], o), carry)
                        V.bn_aggr(mv[0:NB_S, 0, :], bst[0:NB_S, 0, :]).then_inc(s_mv_ready, 1)
                        for pair in range(4):
                            dve.wait_ge(s_update_ready, n * 4 + (pair + 1))
                            s = s_s[:, e, 2 * pair:2 * pair + 2, :].rearrange("p b n -> p (b n)")
                            V.scalar_tensor_tensor(s, s, cdec_s[:, bass.ds(h, 1)], misc[:, 2 + pair % 2, :], ALU.mult, ALU.add).then_inc(s_state_ready, 1)
                        dve.wait_ge(s_gstd_ready, n + 1)
                        ch.link(V.reciprocal(grs[0:NB_S, 0:1], gstd[0:NB_S, 0:1]))
                        V.tensor_scalar(on_s[0:NB_S], o, mv[0:NB_S, 0, 0:1], grs[0:NB_S, 0:1], ALU.subtract, ALU.mult).then_inc(s_on_ready, 1)

                with dve.Fori(0, 2) as i:
                    for j in range(4):
                        n, m = lay * 8 + i * 4 + j, i * 4 + j
                        split_l(lay, AT_G, i, j)
                        done(lay, AT_G, i, j)
                        V.tensor_copy(tmp[:, j % 2, :].rearrange("p (a b) -> p a b", a=2), acc[j % 2][:, :, 0:HALF]).then_inc(acc_free, 1)
                        dve.wait_ge(g_sig, n + 1)
                        dve.wait_ge(s_o_t_ready, lay * 4 + 4)
                        dve.wait_ge(o_ready_hl, lay * 8 + i * 4 + max(j - 1, 0))
                        ch = Chain(dve, g_chain, n)
                        ch.link(V.tensor_tensor(tmp[:, 4 + j % 2, :], tmp[:, j % 2, :], tmp[:, 2 + j % 2, :], ALU.mult))
                        V.tensor_tensor(tmp[:, 6 + j % 2, :].rearrange("p (a b) -> p a b", a=2), tmp[:, 4 + j % 2, :].rearrange("p (a b) -> p a b", a=2), one(o_t, m), ALU.mult).then_inc(g_gated, 1)
                        dve.wait_ge(g_rounded, n + 1)
                        V.tensor_tensor(one(b_lo, m), tmp[:, 6 + j % 2, :].rearrange("p (a b) -> p a b", a=2), one(b_hi, m).bitcast(F32), ALU.subtract).then_inc(o_ready_hl, 1)

                with dve.Fori(0, 2) as i:
                    for j in range(4):
                        split_l(lay, AT_RET, i, j)
                        done(lay, AT_RET, i, j)
                        dve.wait_ge(ma_ready, lay * 8 + 8)
                        V.tensor_tensor(one(mix, i * 4 + j), acc[j % 2][:, :, 0:HALF], one(mix, i * 4 + j), ALU.mult).then_inc(acc_free, 1)

                with dve.Fori(0, 2) as i:
                    for j in range(4):
                        n, m = lay * 8 + i * 4 + j, i * 4 + j
                        a = acc[j % 2][:, :, 0:HALF]
                        pad = tmp[:, j % 2, 0:515]
                        pad_s = tmp[:, 2 + j % 2, 0:88].rearrange("p (b t) -> p b t", t=11)
                        cs = tmp[:, 4 + j % 2, 0:64]
                        w = lambda k: small[:, bass.ds(lay, 1), bass.ds(m + (S_CW + 8 * k), 1)].rearrange("p o q -> p (o q)")
                        bcol = small[:, bass.ds(lay, 1), bass.ds(m + S_CB, 1)].rearrange("p o q -> p (o q)")
                        split_l(lay, AT_XL, i, j)
                        done(lay, AT_XL, i, j)
                        dve.wait_ge(conv_kept, lay * 8 + i * 4 + max(j - 1, 0))
                        V.memset(pad[:, 0:3], 0.0)
                        V.tensor_copy(pad_s[:, :, 0:3], conv0[:, bass.ds(lay * 8 + m, 1)].rearrange("p o b t -> p (o b) t"))
                        V.tensor_copy(pad[:, 3:515].rearrange("p (a b) -> p a b", a=2), prompt(a))
                        V.tensor_copy(tmp[:, 2 + j % 2, 0:88].rearrange("p (a b t) -> p a b t", a=2, t=11)[:, :, :, 3:11], sample(a).rearrange("p a (b t) -> p a b t", t=DS)).then_inc(acc_free, 1)
                        copied(lay, AT_XL, i, j)
                        ch = Chain(dve, conv_chain, n * 4)
                        out = prompt(one(qk, m))
                        win = lambda k: pad[:, k:k + 512].rearrange("p (a b) -> p a b", a=2)
                        csv = cs.rearrange("p (b t) -> p b t", t=DS)
                        V.tensor_scalar(out, win(0), w(0), bcol, ALU.mult, ALU.add)
                        ch.link(V.tensor_scalar(csv, pad_s[:, :, 0:8], w(0), bcol, ALU.mult, ALU.add))
                        for k in range(1, 4):
                            V.scalar_tensor_tensor(out, win(k), w(k), out, ALU.mult, ALU.add)
                            ch.link(V.scalar_tensor_tensor(csv, pad_s[:, :, k:k + 8], w(k), csv, ALU.mult, ALU.add))
                        V.tensor_copy(sample(one(qk, m)), cs.rearrange("p (a b) -> p a b", a=2))
                        V.tensor_copy(conv_c[:, bass.ds(lay * 8 + m, 1), 0, :].rearrange("p o t -> p (o t)"), pad[:, 512:515])
                        V.tensor_copy(conv_c[:, bass.ds(lay * 8 + m, 1), 1:GROUPS, :].rearrange("p o b t -> p (o b) t"), pad_s[:, :, 8:11]).then_inc(conv_kept, 1)

                with dve.Fori(0, 2) as i:
                    for j in range(4):
                        n, m = lay * 8 + i * 4 + j, i * 4 + j
                        t = [tmp[:, q, :].rearrange("p (a b) -> p a b", a=2) for q in range(8)]
                        ch = Chain(dve, lru_chain, n * 8)
                        dve.wait_ge(gates_read, n + 1)
                        V.tensor_scalar(tmp[:, 0, :], tmp[:, 0, :], 0.5, 0.5, ALU.mult, ALU.add).then_inc(r_ready, 1)
                        ch.link(V.scalar_tensor_tensor(t[6], t[1], 1.0, one(qk, m), ALU.add, ALU.mult))
                        dve.wait_ge(a_ready, n + 1)
                        ch.link(V.tensor_tensor(tmp[:, 4, :], tmp[:, 3, :], tmp[:, 3, :], ALU.mult))
                        V.scalar_tensor_tensor(tmp[:, 4, :], tmp[:, 4, :], 1.0, tmp[:, 2, :], ALU.add, ALU.mult).then_inc(e_ready, 1)
                        dve.wait_ge(e_root, n + 1)
                        ch.link(V.tensor_tensor(tmp[:, 6, :], tmp[:, 6, :], tmp[:, 5, :], ALU.mult))
                        first = lambda b: sample(b).rearrange("p a (b t) -> p a b t", t=DS)[:, :, :, 0]
                        hz = tmp[:, 7, 0:8].rearrange("p (a b) -> p a b", a=2)
                        ch.link(V.tensor_tensor(hz, first(t[3]), h0[:, bass.ds(lay * 8 + m, 1), :].rearrange("p o (a b) -> p (o a) b", a=2), ALU.mult))
                        V.memset(first(t[3]), 0.0)
                        ch.link(V.tensor_tensor(first(t[6]), first(t[6]), hz, ALU.add))
                        ch.link(V.tensor_tensor_scan(t[4][:, 0, 0:HALF_P], t[3][:, 0, 0:HALF_P], t[6][:, 0, 0:HALF_P], 0.0, ALU.mult, ALU.add))
                        V.tensor_tensor_scan(t[4][:, 1, 0:HALF_P], t[3][:, 1, 0:HALF_P], t[6][:, 1, 0:HALF_P], t[4][:, 0, HALF_P - 1:HALF_P], ALU.mult, ALU.add)
                        for a in range(2):
                            last = V.tensor_tensor_scan(t[4][:, a, HALF_P:HALF], t[3][:, a, HALF_P:HALF], t[6][:, a, HALF_P:HALF], 0.0, ALU.mult, ALU.add)
                        ch.link(last)
                        V.tensor_copy(lru_c[:, bass.ds(lay * 8 + m, 1), 0:1].rearrange("p o q -> p (o q)"), t[4][:, 1, HALF_P - 1:HALF_P])
                        V.tensor_copy(lru_c[:, bass.ds(lay * 8 + m, 1), 1:GROUPS].rearrange("p o (a b) -> p (o a) b", a=2),
                                      sample(t[4]).rearrange("p a (b t) -> p a b t", t=DS)[:, :, :, DS - 1])
                        split_l(lay, AT_GL, i, j)
                        done(lay, AT_GL, i, j)
                        V.tensor_copy(t[7], acc[j % 2][:, :, 0:HALF]).then_inc(acc_free, 1)
                        dve.wait_ge(gelu_ready, n + 1)
                        ch.link(V.scalar_tensor_tensor(tmp[:, 1, :], tmp[:, 5, :], 1.0, tmp[:, 7, :], ALU.add, ALU.mult))
                        V.scalar_tensor_tensor(tmp[:, 0, :], tmp[:, 1, :], 0.5, tmp[:, 4, :], ALU.mult, ALU.mult).then_inc(y_ready, 1)
                        dve.wait_ge(y_rounded, n + 1)
                        V.tensor_tensor(one(b_lo, m), t[0], one(b_hi, m).bitcast(F32), ALU.subtract).then_inc(y_split, 1)
                        assert ch.n == 8

                with dve.Fori(0, 2) as i:
                    for j in range(4):
                        split_l(lay, AT_LRU, i, j)
                        done(lay, AT_LRU, i, j)
                        V.tensor_copy(one(qk, i * 4 + j), acc[j % 2][:, :, 0:HALF]).then_inc(acc_free, 1)

                with dve.Fori(0, 2) as i:
                    for j in range(4):
                        n, m = lay * 8 + i * 4 + j, i * 4 + j
                        split_l(lay, AT_MB, i, j)
                        done(lay, AT_MB, i, j)
                        V.tensor_copy(tmp[:, j % 2, :].rearrange("p (a b) -> p a b", a=2), acc[j % 2][:, :, 0:HALF]).then_inc(acc_free, 1)
                        dve.wait_ge(mb_sig, n + 1)
                        dve.wait_ge(m_split, lay * 8 + i * 4 + max(j - 1, 0))
                        ch = Chain(dve, mb_chain, n)
                        tv = lambda q: tmp[:, q, :].rearrange("p (a b) -> p a b", a=2)
                        ch.link(V.tensor_tensor(tv(4 + j % 2), tv(2 + j % 2), one(qk, m), ALU.mult))
                        V.tensor_tensor(tv(6 + j % 2), tv(4 + j % 2), one(mix, m), ALU.add).then_inc(mb_mixed, 1)
                        dve.wait_ge(m_rounded, n + 1)
                        V.tensor_tensor(one(b_lo, m), tv(6 + j % 2), one(b_hi, m).bitcast(F32), ALU.subtract).then_inc(m_split, 1)

                def gated_add(j, m, gate_at, base, signal, left):
                    dve.wait_ge(signal, left)
                    a = acc[j % 2][:, :, 0:HALF]
                    gate = ada[:, bass.ds(m + gate_at, 1), 0:1].rearrange("p o q -> p (o q)")
                    gs = ada[:, bass.ds(m + gate_at, 1), 1:GROUPS].rearrange("p o (a b) -> p (o a) b", a=2).unsqueeze(3).to_broadcast([128, 2, 4, DS])
                    V.scalar_tensor_tensor(prompt(one(x, m)), prompt(a), gate, prompt(one(x, m)), ALU.mult, ALU.add)
                    ts = tmp[:, 4 + j % 2, 0:64]
                    V.tensor_tensor(ts.rearrange("p (a b t) -> p a b t", a=2, t=DS), sample(a).rearrange("p a (b t) -> p a b t", t=DS), gs, ALU.mult).then_inc(acc_free, 1)
                    base()
                    xs = sample(one(x, m))
                    V.tensor_tensor(xs, xs, ts.rearrange("p (a b) -> p a b", a=2), ALU.add).then_inc(signal, 1)

                with dve.Fori(0, 2) as i:
                    for j in range(4):
                        split_l(lay, AT_OUT, i, j)
                        done(lay, AT_OUT, i, j)
                        gated_add(j, i * 4 + j, 2 * KT, lambda: copied(lay, AT_OUT, i, j), x_mixed, lay * 8 + i * 4 + max(j - 1, 0))
                norm(lay, 1, scale2, 3 * KT)
                with dve.Fori(0, QUARTERS) as qt:
                    with dve.Fori(0, 2) as i:
                        for j in range(4):
                            n, m = lay * 32 + qt * 8 + i * 4 + j, i * 4 + j
                            split_l(lay, AT_MLP, qt * 4 + i, j)
                            done(lay, AT_MLP, qt * 4 + i, j)
                            V.tensor_scalar(tmp[:, j % 2, :].rearrange("p (a b) -> p a b", a=2), acc[j % 2][:, :, 0:HALF], 0.0, None, ALU.max).then_inc(acc_free, 1)
                            dve.wait_ge(u_rounded, n + 1)
                            V.tensor_tensor(one(b_lo, m), tmp[:, 2 + j % 2, :].rearrange("p (a b) -> p a b", a=2), one(b_hi, m).bitcast(F32), ALU.subtract).then_inc(u_split, 1)
                    dve.wait_ge(squares_ready, lay * 5 + qt + 2)
                    carry(dve)
                    with dve.Fori(0, 2) as i:
                        for j in range(4):
                            split_l(lay, AT_MLP + 8, qt * 4 + i, j)
                            done(lay, AT_MLP + 8, qt * 4 + i, j)
                            gated_add(j, i * 4 + j, 5 * KT, lambda: copied(lay, AT_MLP + 8, qt * 4 + i, j), x_mlp,
                                      lay * 32 + qt * 8 + i * 4 + max(j - 1, 0))

            dve.wait_ge(std_ready, 2 * DEPTH + 1)
            V.reciprocal(qk[:, 3, :], qk[:, 2, :]).then_inc(rstd_ready, 1)
            dve.wait_ge(rstd_ready, 2 * DEPTH + 1)
            with dve.Fori(0, KT) as m:
                flat = lambda b: b[:, bass.ds(m, 1), :].rearrange("p o n -> p (o n)")
                V.scalar_tensor_tensor(flat(tmp), flat(x), fg[:, bass.ds(m, 1)], qk[:, 3, :], ALU.mult, ALU.mult).then_inc(y_done, 1)

        @block.gpsimd
        def _(pool):
            G = nc.gpsimd

            def sum_squares(wait, chain):
                with pool.Fori(0, KT) as m:
                    wait(m)
                    flat = x[:, bass.ds(m, 1), :].rearrange("p o n -> p (o n)")
                    G.tensor_tensor(qk[:, 1, :], flat, flat, ALU.mult).then_inc(square_chain, 1)
                    pool.wait_ge(square_chain, chain + m * 2 + 1)
                    G.tensor_tensor(qk[:, 0, :], qk[:, 0, :], qk[:, 1, :], ALU.add).then_inc(square_chain, 1)
                    pool.wait_ge(square_chain, chain + m * 2 + 2)
                pool.sem_inc(squares_ready, 1)

            pool.wait_ge(params_loaded, 16 * 7)
            G.memset(qk[:, 0, :], 0.0).then_inc(square_chain, 1)
            pool.wait_ge(square_chain, 1)
            sum_squares(lambda m: None, 1)
            with pool.Fori(0, DEPTH) as lay:
                with pool.Fori(0, 2) as i:
                    for c in range(4):
                        n = lay * 8 + i * 4 + c
                        pool.wait_ge(qk_ready, lay * 8 + 8)
                        pool.wait_ge(v_ready, lay * 8 + 8)
                        pool.wait_ge(o_ready, lay * 8 + i * 4 + max(c - 1, 0))
                        cols = slice((c // 2) * HALF + (c % 2) * CHUNK, (c // 2) * HALF + (c % 2) * CHUNK + CHUNK)
                        for e in range(2):
                            h = i * 2 + e
                            G.tensor_copy(k_st[:, c % 2, e, :], qk[:, bass.ds(h + 4, 1), cols].rearrange("p o t -> p (o t)"))
                            last = G.tensor_tensor(q_st[:, c % 2, e, :], qk[:, bass.ds(h, 1), cols].rearrange("p o t -> p (o t)"),
                                                   qdec[:, bass.ds(h, 1), 0:CHUNK].rearrange("p o t -> p (o t)"), ALU.mult)
                        last.then_inc(stage_ready, 1)
                with pool.Fori(0, 4) as h:
                    n = lay * 4 + h
                    pool.wait_ge(s_o_ready, n)
                    pool.wait_ge(on_ready, lay * 8 + 8)
                    pool.wait_ge(ret_p_stored, lay * 32 + 32)
                    G.tensor_copy(k_ss[:].rearrange("p (a b) -> p a b", a=2), sample(one(qk, h + 4)))
                    dst = q_sm[:].rearrange("p (a b s) -> p a b s", a=2, s=72)[:, :, :, 0:DS]
                    src = sample(one(qk, h)).rearrange("p a (b t) -> p a b t", t=DS)
                    for a in range(2):
                        dec = qdec[:, bass.ds(h, 1), CHUNK:CHUNK + DS].to_broadcast([128, 4, DS])
                        last = G.tensor_tensor(dst[:, a], src[:, a], dec, ALU.mult)
                    last.then_inc(s_stage_ready, 1)
                with pool.Fori(0, 8) as m:
                    n = lay * 8 + m
                    pool.wait_ge(acc_free, lay * LAYER_GROUPS + m + (AT_GL - ADA_SKIP + 3))
                    pool.wait_ge(gelu_ready, n)
                    g = tmp[:, 7, :]
                    G.tensor_tensor(extra[:], g, g, ALU.mult).then_inc(cube_chain, 1)
                    pool.wait_ge(cube_chain, n * 2 + 1)
                    carry(pool)
                    G.tensor_scalar(extra[:], extra[:], 0.044715, 1.0, ALU.mult, ALU.add).then_inc(cube_chain, 1)
                    pool.wait_ge(cube_chain, n * 2 + 2)
                    G.tensor_tensor(extra[:], extra[:], g, ALU.mult).then_inc(cube_ready, 1)
                base = lay * (5 * 17) + 17
                pool.wait_ge(m_split, lay * 8 + 8)
                carry(pool)
                G.memset(qk[:, 0, :], 0.0).then_inc(square_chain, 1)
                pool.wait_ge(square_chain, base + 1)
                carry(pool)
                sum_squares(lambda m: pool.wait_ge(x_mixed, lay * 8 + m + 1), base + 1)
                with pool.Fori(0, QUARTERS) as qt:
                    with pool.Fori(0, 4) as i:
                        for j in range(2):
                            n = lay * 32 + qt * 8 + i * 2 + j
                            pool.wait_ge(acc_free, lay * LAYER_GROUPS + qt * 16 + i * 2 + (AT_MLP - ADA_SKIP + j + 3))
                            G.tensor_tensor(tmp[:, 2 + j, :], tmp[:, j, :], tmp[:, j, :], ALU.mult).then_inc(u_ready, 1)
                    qbase = base + 17 + qt * 17
                    pool.wait_ge(mean_ready, lay * 2 + 2)
                    carry(pool)
                    G.memset(qk[:, 0, :], 0.0).then_inc(square_chain, 1)
                    pool.wait_ge(square_chain, qbase + 1)
                    carry(pool)
                    sum_squares(lambda m: pool.wait_ge(x_mlp, lay * 32 + qt * 8 + m + 1), qbase + 1)

        @block.tensor
        def _(pe):
            M = nc.tensor.matmul

            def stream_tile(lay, off, i, j, rhs_hi, rhs_lo, ready=None):
                pe.wait_ge(l_split, lay * LAYER_TILES + i * 4 + (off + j + 1))
                pe.wait_ge(acc_free, lay * LAYER_GROUPS + i * 4 + (off - ADA_SKIP + j + 1))
                for k in range(KT):
                    if ready is not None:
                        ready(k)
                    wh = weight_h[:, j % 2, k * 128:(k + 1) * 128]
                    wl = weight_l[:, j % 2, k * 128:(k + 1) * 128]
                    for n, (w, r) in enumerate(((wh, rhs_hi), (wh, rhs_lo), (wl, rhs_hi))):
                        for half in range(2):
                            last = M(acc[j % 2][:, half, 0:HALF], w, r[:, k, half * HALF:(half + 1) * HALF], start=(k == 0 and n == 0), stop=(k == KT - 1 and n == 2))
                last.then_inc(tile_done, 1)

            def plain(lay, off, rhs_hi, rhs_lo, ready=None):
                with pe.Fori(0, 2) as i:
                    for j in range(4):
                        stream_tile(lay, off, i, j, rhs_hi, rhs_lo, ready if j == 0 else None)

            def mean_square(n):
                pe.wait_ge(squares_ready, n)
                for half in range(2):
                    last = M(misc[:, half, 0:HALF], mean_w, qk[:, 0, half * HALF:(half + 1) * HALF], start=True, stop=True)
                last.then_inc(mean_ready, 1)

            pe.wait_ge(params_loaded, 16 * 7)
            pe.wait_ge(setup_dve, 3)
            with pe.Fori(0, DEPTH) as lay:
                with pe.Fori(0, ADA_GROUPS // 2) as i:
                    for g in range(2):
                        G_n = lay * LAYER_GROUPS + i * 2 + g
                        pe.wait_ge(acc_free, G_n + 1)
                        for j in range(4):
                            pe.wait_ge(l_split, lay * LAYER_TILES + i * 8 + (g * 4 + j + 1))
                            for kk in range(2):
                                k = 2 * j + kk
                                for n, w in enumerate((weight_h, weight_l)):
                                    last = M(acc[g][:, 0, :], c_hl[:, k * 18:k * 18 + 128], w[:, j % 2, kk * 512:(kk + 1) * 512], start=(k == 0 and n == 0), stop=(k == KT - 1 and n == 1))
                            last.then_inc(tile_done, 1)
                        pe.wait_ge(acc_free, G_n + 3)
                        pe.wait_ge(ada_ready, lay * ADA_GROUPS + i * 2 + g)
                        for q in range(4):
                            last = M(misc[:, 0, q * 96:(q + 1) * 96], ada_row[:, g, q * 128:(q + 1) * 128], sel, start=True, stop=True)
                        last.then_inc(ada_turned, 1)
                pe.wait_ge(ada_ready, lay * ADA_GROUPS + ADA_GROUPS)
                mean_square(lay * 5 + 1)
                h_parts = lambda k: pe.wait_ge(h_ready, lay * 16 + (k + 1))
                for off in (AT_Q, AT_K):
                    for j in range(4):
                        stream_tile(lay, off, 0, j, h_hi, h_lo, h_parts if off == AT_Q and j == 0 else None)

                def turn_v(n, j):
                    pe.wait_ge(acc_free, n[0] + (j + 3))
                    pe.wait_ge(v_ready, n[1] + j)
                    src = o_t[:, 2 + j % 2, :]
                    for c in range(4):
                        nc.tensor.transpose(misc[:, 0, c * 128:(c + 1) * 128], src[:, c * 128:(c + 1) * 128], ident)
                    nc.tensor.transpose(misc[0:NB_S, 1, 0:128], src[:, SEQ:TOK], ident).then_inc(v_turned, 1)

                with pe.Fori(0, 2) as i:
                    n = (lay * LAYER_GROUPS + i * 4 + (AT_V - ADA_SKIP), lay * 8 + i * 4)
                    for j in range(4):
                        stream_tile(lay, AT_V, i, j, h_hi, h_lo)
                        if j:
                            turn_v(n, j - 1)
                    turn_v(n, 3)

                def turn_o(n):
                    pe.wait_ge(on_ready, n + 1)
                    pe.wait_ge(o_t_ready, n)
                    for e in range(2):
                        for half in range(2):
                            last = nc.tensor.transpose(misc[:, 3, (2 * e + half) * 128:(2 * e + half + 1) * 128], on_p[:, e, half * 128:(half + 1) * 128], ident)
                    last.then_inc(on_turned, 1)

                with pe.Fori(0, 2) as i:
                    for c in range(4):
                        n = lay * 8 + i * 4 + c
                        pe.wait_ge(stage_ready, n + 1)
                        for e in range(2):
                            qc = qk[:, bass.ds(i * 2 + e, 1), (c // 2) * HALF + (c % 2) * CHUNK:(c // 2) * HALF + (c % 2) * CHUNK + CHUNK].rearrange("p o t -> p (o t)")
                            M(misc[:, 0, e * 256:e * 256 + 128], k_st[:, c % 2, e, :], qc, start=True, stop=True)
                            last = nc.tensor.transpose(misc[:, 0, e * 256 + 128:e * 256 + 256], k_st[:, c % 2, e, :], ident)
                        last.then_inc(scores_ready, 1)
                        stream_tile(lay, AT_MA, i, c, h_hi, h_lo)
                        if c:
                            turn_o(lay * 8 + i * 4 + (c - 1))
                        pe.wait_ge(masked_ready, n + 1)
                        pe.wait_ge(s_ready, n)
                        for e in range(2):
                            v = v_tok[:, c, bass.ds(i * 512 + e * 256, 256)]
                            M(misc[:, 1, e * 256:e * 256 + 256], p_m[:, e, :], v, start=True, stop=False)
                            M(misc[:, 1, e * 256:e * 256 + 256], q_st[:, c % 2, e, :], s_p[:, e, :], start=False, stop=True)
                            last = M(misc[:, 2, e * 256:e * 256 + 256], kd_p[:, e, :], v, start=True, stop=True)
                        last.then_inc(o_ready, 1)
                    turn_o(n)

                with pe.Fori(0, 2) as i:
                    for e in range(2):
                        n = lay * 4 + i * 2 + e
                        pe.wait_ge(s_stage_ready, n + 1)
                        pe.wait_ge(s_o_t_ready, n)
                        pe.wait_ge(o_t_ready, lay * 8 + 8)
                        M(misc[0:NB_S, 0, 0:NB_S], k_ss[:], sample(one(qk, i * 2 + e)), start=True, stop=True)
                        nc.tensor.transpose(misc[0:NB_S, 0, 128:256], k_ss[:], ident).then_inc(s_scores_ready, 1)
                        pe.wait_ge(state_loaded[e], lay * 32 + i * 16 + 16)
                        pe.wait_ge(s_masked_ready, n + 1)
                        carry(pe)
                        v = v_s[0:NB_S, bass.ds(i * 512 + e * 256, 256)]
                        o = misc[:, 1, 0:DV]
                        M(o, p_ms[0:NB_S, :], v, start=True, stop=False)
                        for b in range(DB):
                            last = M(o, q_sm[:, b * 64:b * 64 + 128], s_s[:, e, b, :], start=False, stop=(b == DB - 1))
                        last.then_inc(s_o_ready, 1)
                        for pair in range(4):
                            if pair > 1:
                                pe.wait_ge(s_state_ready, n * 4 + (pair - 1))
                                carry(pe)
                            for b in range(2):
                                last = M(misc[:, 2 + pair % 2, b * 256:(b + 1) * 256], kd_s[0:NB_S, 2 * pair + b, :], v, start=True, stop=True)
                            last.then_inc(s_update_ready, 1)
                        pe.wait_ge(s_on_ready, n + 1)
                        carry(pe)
                        for half in range(2):
                            last = nc.tensor.transpose(misc[:, 0, 256 + 64 * half:320 + 64 * half], on_s[0:NB_S, half * 128:(half + 1) * 128], ident[0:NB_S, 0:NB_S])
                        last.then_inc(s_turned, 1)

                plain(lay, AT_G, h_hi, h_lo)
                b_parts = lambda s, base: (lambda k: pe.wait_ge(s, base + (k + 1)))
                plain(lay, AT_RET, b_hi, b_lo, b_parts(o_ready_hl, lay * 8))
                plain(lay, AT_XL, h_hi, h_lo)
                with pe.Fori(0, 2) as i:
                    for j in range(4):
                        n, m = lay * 8 + i * 4 + j, i * 4 + j
                        pe.wait_ge(conv_kept, n + 1)
                        pe.wait_ge(wrg_loaded[j], lay * 48 + i * 16 + 16)
                        pe.wait_ge(gates_read, n)
                        for gate in range(2):
                            for half in range(2):
                                rhs = qk[:, bass.ds(m, 1), half * HALF:(half + 1) * HALF].rearrange("p o t -> p (o t)")
                                last = M(misc[:, 2 * gate + half, 0:HALF], wrg[:, j, gate * 128:(gate + 1) * 128], rhs, start=True, stop=True)
                        last.then_inc(gates_ready, 1)
                        stream_tile(lay, AT_GL, i, j, h_hi, h_lo)
                plain(lay, AT_LRU, b_hi, b_lo, b_parts(y_split, lay * 8))
                plain(lay, AT_MB, h_hi, h_lo)
                plain(lay, AT_OUT, b_hi, b_lo, b_parts(m_split, lay * 8))
                mean_square(lay * 5 + 2)
                h2_parts = lambda k: pe.wait_ge(h_ready, lay * 16 + (k + 9))
                with pe.Fori(0, QUARTERS) as qt:
                    with pe.Fori(0, 2) as i:
                        for j in range(4):
                            stream_tile(lay, AT_MLP, qt * 4 + i, j, h_hi, h_lo, h2_parts if j == 0 else None)
                    with pe.Fori(0, 2) as i:
                        for j in range(4):
                            stream_tile(lay, AT_MLP + 8, qt * 4 + i, j, b_hi, b_lo, b_parts(u_split, lay * 32 + qt * 8) if j == 0 else None)
            mean_square(DEPTH * 5 + 1)


def constants():
    t = np.zeros((128, NCONST), np.float32)

    def put(name, value):
        a, b = _off[name]
        value = np.asarray(value, np.float32)
        t[:value.shape[0], a:b] = value.reshape(value.shape[0], -1)

    half = DK // 2
    inv = np.float32(10000.0) ** (-np.arange(half, dtype=np.float32) / np.float32(half))
    pos_p = np.arange(SEQ, dtype=np.float32).reshape(2, HALF_P)
    pos_s = np.tile(np.float32(PAST) + np.arange(DS, dtype=np.float32), DB).reshape(2, HALF_S)
    pos = np.concatenate([pos_p, pos_s], axis=1)
    ang = (pos[None] * inv[:, None, None]).astype(np.float32).astype(np.float64)
    put("cos", np.concatenate([np.cos(ang)] * 2))
    put("sin", np.concatenate([np.sin(ang), -np.sin(ang)]))
    log_g = np.log1p(-np.exp2(-5.0 - np.arange(HEADS)))
    idx, ids = np.arange(CHUNK), np.arange(DS)
    q = np.concatenate([np.exp((idx + 1.0)[None] * log_g[:, None]), np.exp((ids + 1.0)[None] * log_g[:, None])], axis=1)
    put("qdec", np.broadcast_to(q, (128,) + q.shape))
    diff = idx[None, :] - idx[:, None]
    m = np.where(diff[:, None] >= 0, np.exp(np.maximum(diff, 0)[:, None] * log_g[None, :, None]), 0.0)
    put("mask", m)
    tok = np.arange(NB_S)
    diff = tok[None, :] - tok[:, None]
    same = (tok[None, :] // DS == tok[:, None] // DS) & (diff >= 0)
    put("mask_s", np.where(same[:, None], np.exp(np.maximum(diff, 0)[:, None] * log_g[None, :, None]), 0.0))
    own = tok[:, None] // DS == np.arange(DB)[None, :]
    put("kdm", own[:, None, :] * np.exp((DS - 1.0 - tok % DS)[:, None, None] * log_g[None, :, None]))
    put("kdec", np.exp((CHUNK - 1.0 - idx)[:, None] * log_g[None]))
    put("cdec", np.broadcast_to(np.exp(CHUNK * log_g), (128, HEADS)))
    put("cdec_s", np.broadcast_to(np.exp(DS * log_g), (128, HEADS)))
    put("ident", np.eye(128))
    put("mean", np.full((128, 128), 1.0 / DM))
    sel = np.zeros((128, 96))
    sel[np.arange(GROUPS), np.arange(GROUPS)] = 1.0
    sel[GROUPS + np.arange(GROUPS), np.arange(GROUPS)] = 1.0
    put("sel", sel)
    return t


def tiles(w):
    return w.reshape(KT, 128, -1, 128).transpose(2, 1, 0, 3).reshape(-1, 128, 1024)


def ada_tiles(w):
    return w.reshape(4, 2, 128, ADA_GROUPS, 512).transpose(3, 0, 2, 1, 4).reshape(-1, 128, 1024)


def per_feature(a):
    a = np.moveaxis(a, -1, 0)
    return np.ascontiguousarray(np.moveaxis(a.reshape((KT, 128) + a.shape[1:]), 0, 1))


def kernel(**inputs):
    import concourse.bacc as bacc
    from concourse.bass_utils import run_bass_kernel_spmd as run

    a = {k: np.asarray(v) for k, v in inputs.items()}
    w = []
    for l in range(DEPTH):
        z = a["w_in"][l]
        cut = lambda lo, hi: tiles(z[:, lo:hi])
        w += [ada_tiles(a["w_ada"][l]), cut(0, 2048), cut(5120, 6144)]
        w += [cut(2048, 3072), tiles(a["w_proj_ret"][l]), cut(3072, 4096), cut(4096, 5120), tiles(a["w_proj_lru"][l]),
              cut(6144, 7168), tiles(a["w_out"][l])]
        w1, w2 = tiles(a["w_mlp1"][l]), a["w_mlp2"][l]
        for q in range(QUARTERS):
            w += [w1[q * 8:(q + 1) * 8], tiles(w2[q * 1024:(q + 1) * 1024])]
    w.append(w[0][:STREAM - DEPTH * LAYER_TILES])
    stream = np.concatenate(w)

    xp = per_feature(a["x_prompt"][0]).reshape(128, KT, 2, HALF_P)
    xs = per_feature(a["x_sample"].reshape(NB_S, DM)).reshape(128, KT, 2, HALF_S)
    small = np.concatenate([
        a["b_ada"].reshape(DEPTH, 48, 128), a["norm1_g"].reshape(DEPTH, KT, 128), a["norm2_g"].reshape(DEPTH, KT, 128),
        a["conv_w"].reshape(DEPTH, DEC_W * KT, 128)] + [a[n].reshape(DEPTH, KT, 128) for n in ("conv_b", "b_rg_a", "b_rg_x", "lru_lambda")], axis=1)
    arrays = {
        "stream": stream,
        "x_in": np.ascontiguousarray(np.concatenate([xp, xs], axis=3).reshape(128, KT, TOK)),
        "c_in": np.ascontiguousarray(per_feature(np.concatenate([a["c_prompt"], a["c_sample"]])).reshape(128, KT * GROUPS)),
        "small_in": np.ascontiguousarray(small.transpose(2, 0, 1)),
        "fg_in": np.ascontiguousarray(a["final_g"].reshape(KT, 128).T),
        "h0_in": np.ascontiguousarray(a["state_lru"].reshape(DEPTH, DB, KT, 128).transpose(3, 0, 2, 1).reshape(128, DEPTH * KT, DB)),
        "conv_in": np.ascontiguousarray(a["state_conv"].reshape(DEPTH, DB, 3, KT, 128).transpose(4, 0, 3, 1, 2).reshape(128, DEPTH * KT, DB, 3)),
        "wrg_in": np.ascontiguousarray(np.concatenate([a["w_rg_a"], a["w_rg_x"]], axis=3).reshape(DEPTH * KT, 128, 256)),
        "state_in": a["state_ret"],
        "const_in": constants(),
    }
    outs = {
        "y_out": (128, KT, TOK), "ret_p_out": (DEPTH * HEADS, DK, DV), "lru_out": (128, DEPTH * KT, GROUPS),
        "conv_out": (128, DEPTH * KT, GROUPS, 3), "ret_s_out": (DEPTH, DB, HEADS, DK, DV),
    }
    nc = bacc.Bacc("TRN2", target_bir_lowering=False, num_devices=1)
    ins = [nc.dram_tensor(n, v.shape, F32, kind="ExternalInput").ap() for n, v in arrays.items()]
    outs_ap = [nc.dram_tensor(n, s, F32, kind="ExternalOutput").ap() for n, s in outs.items()]
    build(nc, *ins, *outs_ap)
    r = run(nc, [arrays], core_ids=[0]).results[0]

    y = np.asarray(r["y_out"]).reshape(128, KT, 2, HALF)
    rows = lambda t: t.transpose(2, 3, 1, 0).reshape(-1, DM)
    lru = np.asarray(r["lru_out"]).reshape(128, DEPTH, KT, GROUPS).transpose(1, 3, 2, 0).reshape(DEPTH, GROUPS, DM)
    conv = np.asarray(r["conv_out"]).reshape(128, DEPTH, KT, GROUPS, 3).transpose(1, 3, 4, 2, 0).reshape(DEPTH, GROUPS, 3, DM)
    return (rows(y[..., :HALF_P]).reshape(1, SEQ, DM), rows(y[..., HALF_P:]).reshape(DB, DS, DM),
            np.asarray(r["ret_p_out"]).reshape(DEPTH, 1, HEADS, DK, DV), lru[:, :1], conv[:, :1],
            np.asarray(r["ret_s_out"]), lru[:, 1:], conv[:, 1:])
```

```python
from contextlib import ExitStack

import numpy as np
import concourse.bass as bass
from concourse import mybir

F32 = mybir.dt.float32
F32R = mybir.dt.float32r
ALU = mybir.AluOpType
ACT = mybir.ActivationFunctionType

DM, SEQ, DEPTH, DB, DS, PAST = 1024, 512, 2, 8, 8, 4096
HEADS, DK, DV, CHUNK = 4, 128, 256, 128
NORM_EPS, GN_EPS, DEC_W = 1e-6, 1e-5, 4
KT = DM // 128
HALF_P, HALF_S = SEQ // 2, DB * DS // 2
HALF = HALF_P + HALF_S
TOK = 2 * HALF
GROUPS = 1 + DB
ADA_COLS = 6 * DM
ADA_GROUPS = ADA_COLS // 512
ADA_FIRST = ADA_GROUPS * 5 // 6
NB_S = DB * DS

AT_Q, AT_K, AT_V = 0, 4, 8
AT_MA, AT_G, AT_XL, AT_GL, AT_RET, AT_MB, AT_LRU, AT_OUT = (16 + 8 * n for n in range(8))
AT_MLP = AT_OUT + 8
QUARTERS = 4
LAYER_TILES = AT_MLP + QUARTERS * 16
STREAM = DEPTH * LAYER_TILES + 4

_off = {}
_n = 0
for _name, _w in (("cos", TOK), ("sin", TOK), ("qdec", HEADS * (CHUNK + DS)), ("mask", HEADS * CHUNK),
                  ("mask_s", HEADS * NB_S), ("kdm", HEADS * DB), ("kdec", HEADS), ("cdec", HEADS),
                  ("cdec_s", HEADS), ("ident", 128), ("mean", 128)):
    _off[_name] = (_n, _n + _w)
    _n += _w
NCONST = _n
S_BADA, S_G1, S_G2, S_CW, S_CB, S_BA, S_BX, S_LAM, NSMALL = 0, 48, 56, 64, 96, 104, 112, 120, 128


class Chain:

    def __init__(self, eng, sem, base):
        self.eng, self.sem, self.base, self.n = eng, sem, base, 0

    def link(self, ins, carry=None):
        self.n += 1
        ins.then_inc(self.sem, 1)
        self.eng.wait_ge(self.sem, self.base + self.n)
        if carry is not None:
            carry(self.eng)


def one(buf, m):
    return buf[:, bass.ds(m, 1), :].rearrange("p o (a b) -> p (o a) b", a=2)


def prompt(tile):
    return tile[:, :, 0:HALF_P]


def sample(tile):
    return tile[:, :, HALF_P:HALF]


def build(nc, stream, ada_in, x_in, c_in, small_in, fg_in, h0_in, conv_in, wrg_in, state_in, const_in,
          y_out, ret_p_out, lru_out, conv_out, ret_s_out):
    ctx = ExitStack()
    with ctx:
        at = [(nc.sbuf_base + 31) // 32 * 32]

        def place(name, shape, dt=F32, offset=None):
            size = int(np.prod(shape[1:])) * 4
            if offset is None:
                offset = at[0]
                at[0] += (size + 31) // 32 * 32
                assert at[0] <= nc.sbuf_usable_end, (name, at[0])
            t = nc.alloc_sbuf_tensor_at(name, shape, dt, offset=offset)
            offs[name] = offset
            return t

        offs = {}
        raw = place("raw", [128, 4, 1024])
        weight_h = place("weight_h", [128, 2, 1024], F32R)
        weight_l = place("weight_l", [128, 2, 1024], F32R)
        x = place("x", [128, KT, TOK])
        h_hi = place("h_hi", [128, KT, TOK], F32R)
        h_lo = place("h_lo", [128, KT, TOK], F32R)
        b_hi = place("b_hi", [128, KT, TOK], F32R)
        b_lo = place("b_lo", [128, KT, TOK], F32R)
        mix = place("mix", [128, KT, TOK])
        qk = place("qk", [128, KT, TOK])
        o_t = place("o_t", [128, KT, TOK], F32, offs["b_hi"])
        tmp = place("tmp", [128, 8, TOK])
        side = place("side", [128, 2, 672])
        v_tok = place("v_tok", [128, SEQ // 128, DM], F32, offs["tmp"])
        v_s = place("v_s", [128, DM], F32, offs["side"])
        lo = offs["b_lo"]
        ada_raw = [place(f"ada_raw{n}", [128, 1024], F32, at_byte) for n, at_byte in
                   enumerate((offs["qk"] + 4 * TOK * 4, offs["qk"] + 4 * TOK * 4 + 4096, offs["side"], lo))]
        ada_row = place("ada_row", [128, 512], F32, lo + 4 * 4096)
        s_p = place("s_p", [128, 2, DV], F32, lo)
        on_p = place("on_p", [128, 2, DV], F32, lo + 2048)
        p_m = place("p_m", [128, 2, CHUNK], F32, lo + 4096)
        kd_p = place("kd_p", [128, 2, DK], F32, lo + 5120)
        k_st = place("k_st", [128, 2, 2, CHUNK], F32, lo + 6144)
        q_st = place("q_st", [128, 2, 2, CHUNK], F32, lo + 8192)
        s_s = place("s_s", [128, 2, DB, DV], F32, lo)
        k_ss = place("k_ss", [128, NB_S], F32, lo + 16640)
        on_s = place("on_s", [128, DV], F32, lo + 16896)
        wrg = place("wrg", [128, 2, 256])
        kd_s = place("kd_s", [128, DB // 2, DK])
        q_sm = place("q_sm", [128, DB * 72])
        p_ms = place("p_ms", [128, 128])
        const = place("const", [128, NCONST])
        small = place("small", [128, DEPTH, NSMALL])
        fg = place("fg", [128, KT])
        h0 = place("h0", [128, DEPTH * KT, DB])
        conv0 = place("conv0", [128, DEPTH * KT, DB, 3])
        lru_c = place("lru_c", [128, DEPTH * KT, GROUPS])
        conv_c = place("conv_c", [128, DEPTH * KT, GROUPS, 3])
        ada = place("ada", [128, 6 * KT, GROUPS])
        ada_sum = place("ada_sum", [128, 2, 4, GROUPS])
        scale1 = place("scale1", [128, KT, GROUPS])
        scale2 = place("scale2", [128, KT, GROUPS])
        c_act = place("c_act", [128, KT * GROUPS])
        sp_pos = place("sp_pos", [128, DEPTH * KT])
        sp_neg = place("sp_neg", [128, DEPTH * KT])
        half_ba = place("half_ba", [128, DEPTH * KT])
        half_bx = place("half_bx", [128, DEPTH * KT])
        bst = place("bst", [128, 2, 6])
        mv = place("mv", [128, 2, 2])
        gstd = place("gstd", [128, 2])
        grs = place("grs", [128, 2])
        eps_n = place("eps_n", [128, 1])
        eps_g = place("eps_g", [128, 1])

        def cst(name, rows=128):
            a, b = _off[name]
            return const[0:rows, a:b]

        cos = cst("cos").rearrange("p (a b) -> p a b", a=2)
        sin = cst("sin").rearrange("p (a b) -> p a b", a=2)
        qdec = cst("qdec").rearrange("p (h t) -> p h t", h=HEADS)
        mask = cst("mask").rearrange("p (h t) -> p h t", h=HEADS)
        mask_s = cst("mask_s", NB_S).rearrange("p (h t) -> p h t", h=HEADS)
        kdm = cst("kdm", NB_S).rearrange("p (h t) -> p h t", h=HEADS)
        kdec, cdec, cdec_s = cst("kdec"), cst("cdec"), cst("cdec_s")
        ident, mean_w = cst("ident"), cst("mean")

        acc = [ctx.enter_context(nc.psum_tensor(f"acc{n}", [128, 2, 512], F32)) for n in range(2)]
        misc = ctx.enter_context(nc.psum_tensor("misc", [128, 4, 512], F32))

        def sem(name):
            return ctx.enter_context(nc.semaphore(name))

        raw_loaded = [sem(f"raw_loaded{n}") for n in range(4)]
        h_split, l_split, tile_done, acc_free = sem("h_split"), sem("l_split"), sem("tile_done"), sem("acc_free")
        params_loaded, setup_act, setup_dve = sem("params_loaded"), sem("setup_act"), sem("setup_dve")
        c_loaded = sem("c_loaded")
        ada_loaded = [sem(f"ada_loaded{n}") for n in range(4)]
        ada_used, ada_copied = sem("ada_used"), sem("ada_copied")
        ada_turned, ada_out_ready, ada_ready, scales_ready = sem("ada_turned"), sem("ada_out_ready"), sem("ada_ready"), sem("scales_ready")
        squares_ready, square_chain, mean_ready, std_ready = sem("squares_ready"), sem("square_chain"), sem("mean_ready"), sem("std_ready")
        rstd_ready, xn_ready, xn_chain, h_rounded, h_ready = sem("rstd_ready"), sem("xn_ready"), sem("xn_chain"), sem("h_rounded"), sem("h_ready")
        qk_ready, v_turned, v_ready = sem("qk_ready"), sem("v_turned"), sem("v_ready")
        ma_ready = sem("ma_ready")
        stage_ready, scores_ready, masked_ready = sem("stage_ready"), sem("scores_ready"), sem("masked_ready")
        o_ready, s_ready, mv_ready, gstd_ready, norm_chain = sem("o_ready"), sem("s_ready"), sem("mv_ready"), sem("gstd_ready"), sem("norm_chain")
        on_ready, on_turned, o_t_ready, ret_p_stored = sem("on_ready"), sem("on_turned"), sem("o_t_ready"), sem("ret_p_stored")
        state_loaded, state_stored = [sem(f"state_loaded{n}") for n in range(2)], [sem(f"state_stored{n}") for n in range(2)]
        s_stage_ready, s_scores_ready, s_masked_ready = sem("s_stage_ready"), sem("s_scores_ready"), sem("s_masked_ready")
        s_o_ready, s_update_ready, s_state_ready = sem("s_o_ready"), sem("s_update_ready"), sem("s_state_ready")
        s_mv_ready, s_gstd_ready, s_chain, s_on_ready = sem("s_mv_ready"), sem("s_gstd_ready"), sem("s_chain"), sem("s_on_ready")
        s_turned, s_o_t_ready = sem("s_turned"), sem("s_o_t_ready")
        g_sig, g_silu, g_gated, g_rounded, o_split = sem("g_sig"), sem("g_silu"), sem("g_gated"), sem("g_rounded"), sem("o_split")
        ret_mixed = sem("ret_mixed")
        conv_chain, conv_kept = sem("conv_chain"), sem("conv_kept")
        wrg_loaded = [sem(f"wrg_loaded{n}") for n in range(2)]
        gates_ready, gates_read, r_ready, a_ready, e_ready, e_root = sem("gates_ready"), sem("gates_read"), sem("r_ready"), sem("a_ready"), sem("e_ready"), sem("e_root")
        lru_chain, cube_chain, cube_ready, gelu_tanh, gelu_ready = (
            sem("lru_chain"), sem("cube_chain"), sem("cube_ready"), sem("gelu_tanh"), sem("gelu_ready"))
        y_ready, y_rounded = sem("y_ready"), sem("y_rounded")
        mb_sig, mb_chain, m_ready, m_rounded, m_split = sem("mb_sig"), sem("mb_chain"), sem("m_ready"), sem("m_rounded"), sem("m_split")
        gate_chain, x_mixed, x_mlp = sem("gate_chain"), sem("x_mixed"), sem("x_mlp")
        relu_ready, u_ready, u_rounded, u_split = sem("relu_ready"), sem("u_ready"), sem("u_rounded"), sem("u_split")
        y_done, stored, waited = sem("y_done"), sem("stored"), sem("waited")
        first_squares = sem("first_squares")

        def carry(eng):
            eng.sem_inc(waited, 1)

        start_at_1 = {
            "dve": (x_mlp, x_mixed, qk_ready, conv_kept, y_ready, gelu_ready, s_ready),
            "act": (v_ready, o_t_ready, s_o_t_ready, gates_read, state_stored[0], state_stored[1], ret_p_stored),
            "pe": (o_ready, s_o_ready),
            "pool": (o_split,),
        }

        block = ctx.enter_context(nc.Block())

        @block.sync
        def _(sp):
            def load(t, slot):
                sp.dma_start(raw[:, slot, :], stream[bass.ds(t, 1)].rearrange("o p n -> (o p) n")).then_inc(raw_loaded[slot], 16)

            def load_range(lay, first, count):
                with sp.Fori(0, count // 4) as i:
                    for j in range(4):
                        sp.wait_ge(l_split, lay * LAYER_TILES + i * 4 + (first + j + 1))
                        load(lay * LAYER_TILES + i * 4 + (first + j + 4), j)

            def load_ada(lay, first, groups, left, count):
                def load_tile(t, slot):
                    sp.wait_ge(ada_used, t + 1)
                    sp.dma_start(ada_raw[slot][:], ada_in[bass.ds(t, 1)].rearrange("o p n -> (o p) n")).then_inc(ada_loaded[slot], 16)

                for j in range(4):
                    if j == 3:
                        sp.wait_ge(left, count)
                        carry(sp)
                    load_tile(lay * (ADA_GROUPS * 4) + (first * 4 + j), j)
                with sp.Fori(0, groups - 1) as i:
                    for j in range(4):
                        load_tile(lay * (ADA_GROUPS * 4) + i * 4 + (first * 4 + j + 4), j)

            with sp.Fori(0, DEPTH) as lay:
                load_ada(lay, 0, ADA_FIRST, x_mlp, lay * 32 + 1)
                load_range(lay, 0, AT_MLP)
                load_ada(lay, ADA_FIRST, ADA_GROUPS - ADA_FIRST, tile_done, lay * LAYER_TILES + AT_MLP)
                load_range(lay, AT_MLP, LAYER_TILES - AT_MLP)

        @block.scalar
        def _(act):
            A = nc.scalar.activation
            for one_more in start_at_1["act"]:
                act.sem_inc(one_more, 1)
            loads = [(small[:], small_in), (const[:], const_in), (x[:], x_in), (fg[:], fg_in), (h0[:], h0_in), (conv0[:], conv_in)]
            act.dma_start(tmp[:, 0, 0:KT * GROUPS], c_in).then_inc(c_loaded, 16)
            for dst, src in loads:
                act.dma_start(dst, src).then_inc(params_loaded, 16)
            for t in range(4):
                act.dma_start(raw[:, t, :], stream[t]).then_inc(raw_loaded[t], 16)
            act.wait_ge(c_loaded, 16)
            c_raw, c_sig, c_silu = (tmp[:, n, 0:KT * GROUPS] for n in range(3))
            A(c_sig, c_raw, ACT.Sigmoid).then_inc(setup_act, 1)
            act.wait_ge(params_loaded, 16 * 6)
            lam = small[:, :, S_LAM:S_LAM + KT]
            e_abs, e_neg = tmp[:, 3, 0:16].rearrange("p (l k) -> p l k", l=2), tmp[:, 4, 0:16]
            A(e_abs, lam, ACT.Abs).then_inc(setup_act, 1)
            act.wait_ge(setup_act, 2)
            A(e_neg, tmp[:, 3, 0:16], ACT.Exp, scale=-1.0).then_inc(setup_act, 1)
            for t in range(2):
                act.dma_start(wrg[:, t, :], wrg_in[t]).then_inc(wrg_loaded[t], 16)
            for t in range(2):
                act.wait_ge(raw_loaded[t], 16)
                A(weight_h[:, t, :], raw[:, t, :], ACT.Copy).then_inc(h_split, 1)

            def split_h(lay, off, i, j):
                act.wait_ge(tile_done, lay * LAYER_TILES + i * 4 + (off + j + 1))
                act.wait_ge(raw_loaded[(j + 2) % 4], lay * (LAYER_TILES * 4) + i * 16 + 16 * (off // 4 + (j + 2) // 4 + 1))
                A(weight_h[:, j % 2, :], raw[:, (j + 2) % 4, :], ACT.Copy).then_inc(h_split, 1)

            def copied(lay, off, i, j):
                act.wait_ge(acc_free, lay * LAYER_TILES + i * 4 + (off + j + 3))

            def plain(lay, off, iters):
                with act.Fori(0, iters) as i:
                    for j in range(4):
                        split_h(lay, off, i, j)

            def ada_row_out(n, g):
                act.wait_ge(ada_used, n * 4 + 8)
                A(ada_row[0:GROUPS, :], misc[0:GROUPS, 2 + g, :], ACT.Copy).then_inc(ada_copied, 1)

            def ada_sum_out(n, g):
                act.wait_ge(ada_turned, n + 1)
                act.wait_ge(ada_ready, n + 1)
                A(ada_sum[:, g], misc[:, 2 + g, 0:384].rearrange("p (q c) -> p q c", q=4)[:, :, 0:GROUPS], ACT.Copy).then_inc(ada_out_ready, 1)

            def ada_groups(lay, first, groups):
                with act.Fori(0, groups // 2) as i:
                    for g in range(2):
                        n = lay * ADA_GROUPS + i * 2 + (first + g)
                        ada_row_out(n, g)
                        ada_sum_out(n, g)

            def norm_std(lay, which):
                act.wait_ge(mean_ready, lay * 2 + which + 1)
                A(qk[:, 2, :].rearrange("p (a b) -> p a b", a=2), misc[:, 0:2, 0:HALF], ACT.Sqrt, bias=eps_n[:]).then_inc(std_ready, 1)

            def norm_tile(lay, which, m, scale, shift_at):
                act.wait_ge(xn_ready, lay * 16 + (which * KT + 1) + m)
                sc = scale[:, bass.ds(m, 1), 0:1].rearrange("p o a -> p (o a)")
                sh = ada[:, bass.ds(m + shift_at, 1), 0:1].rearrange("p o a -> p (o a)")
                A(prompt(one(mix, m)), prompt(one(tmp, m)), ACT.Identity, bias=sh, scale=sc)
                A(prompt(one(h_hi, m)), prompt(one(tmp, m)), ACT.Identity, bias=sh, scale=sc)
                A(sample(one(h_hi, m)), sample(one(mix, m)), ACT.Copy).then_inc(h_rounded, 1)

            with act.Fori(0, DEPTH) as lay:
                ada_groups(lay, 0, 4)
                norm_std(lay, 0)
                with act.Fori(0, 2) as i:
                    for g in range(2):
                        for j in range(2):
                            norm_tile(lay, 0, i * 4 + (g * 2 + j), scale1, 0)
                        ada_row_out(lay * ADA_GROUPS + i * 2 + (4 + g), g)
                        ada_sum_out(lay * ADA_GROUPS + i * 2 + (4 + g), g)
                ada_groups(lay, 8, ADA_FIRST - 8)
                for j in range(4):
                    split_h(lay, AT_Q, 0, j)
                for j in range(4):
                    split_h(lay, AT_K, 0, j)

                with act.Fori(0, 2) as i:
                    for j in range(4):
                        split_h(lay, AT_V, i, j)
                        n, m = lay * 8 + i * 4 + j, i * 4 + j
                        act.wait_ge(v_turned, n + 1)
                        A(v_tok[:, :, bass.ds(m * 128, 128)], misc[:, 0, :].rearrange("p (c d) -> p c d", c=4), ACT.Copy)
                        A(v_s[0:NB_S, bass.ds(m * 128, 128)], misc[0:NB_S, 1, 0:128], ACT.Copy).then_inc(v_ready, 1)

                def o_evac(i, c, n):
                    act.wait_ge(on_turned, n + 1)
                    dst = o_t[:, bass.ds(i * 4, 4), (c // 2) * HALF + (c % 2) * CHUNK:(c // 2) * HALF + (c % 2) * CHUNK + CHUNK]
                    A(dst, misc[:, 3, :].rearrange("p (c d) -> p c d", c=4), ACT.Copy).then_inc(o_t_ready, 1)

                with act.Fori(0, 2) as i:
                    for c in range(4):
                        n = lay * 8 + i * 4 + c
                        if c:
                            o_evac(i, c - 1, lay * 8 + i * 4 + (c - 1))
                        split_h(lay, AT_MA, i, c)
                        copied(lay, AT_MA, i, c)
                        A(one(mix, i * 4 + c), one(mix, i * 4 + c), ACT.Sigmoid).then_inc(ma_ready, 1)
                        act.wait_ge(mv_ready, n + 1)
                        A(gstd[:], mv[:, :, 1], ACT.Sqrt, bias=eps_g[:]).then_inc(gstd_ready, 1)
                    o_evac(i, 3, n)
                    act.wait_ge(s_ready, n + 1 + 1)
                    act.dma_start(ret_p_out[bass.ds(lay * 4 + i * 2, 2)].rearrange("h p n -> p h n"), s_p[:]).then_inc(ret_p_stored, 16)

                act.wait_ge(ret_p_stored, lay * 32 + 32 + 1)

                def load_state(i, e):
                    act.wait_ge(state_stored[e], lay * 32 + i * 16 + 1)
                    act.dma_start(s_s[:, e], state_in[bass.ds(lay, 1), :, bass.ds(i * 2 + e, 1)].rearrange("l b h p n -> p (l b h) n")).then_inc(state_loaded[e], 16)

                with act.Fori(0, 2) as i:
                    for j in range(4):
                        e, m = j // 2, i * 4 + j
                        n = lay * 4 + i * 2 + e
                        if j < 2:
                            load_state(i, j)
                        split_h(lay, AT_G, i, j)
                        A(one(tmp, m), acc[j % 2][:, :, 0:HALF], ACT.Sigmoid).then_inc(g_sig, 1)
                        if j % 2 == 0:
                            act.wait_ge(s_mv_ready, n + 1)
                            A(gstd[0:NB_S, 0:1], mv[0:NB_S, 0, 1:2], ACT.Sqrt, bias=eps_g[0:NB_S]).then_inc(s_gstd_ready, 1)
                        else:
                            act.wait_ge(s_turned, n + 1)
                            for half in range(2):
                                last = A(sample(one(o_t, i * 4 + (2 * e + half))), misc[:, 1, 256 + 64 * half:320 + 64 * half].rearrange("p (a b) -> p a b", a=2), ACT.Copy)
                            last.then_inc(s_o_t_ready, 1)
                            act.wait_ge(s_state_ready, n * 4 + 4)
                            act.dma_start(ret_s_out[bass.ds(lay, 1), :, bass.ds(i * 2 + e, 1)].rearrange("l b h p n -> p (l b h) n"), s_s[:, e]).then_inc(state_stored[e], 16)

                for e in range(2):
                    act.wait_ge(state_stored[e], lay * 32 + 32 + 1)
                with act.Fori(0, 2) as i:
                    for j in range(4):
                        n, m = lay * 8 + i * 4 + j, i * 4 + j
                        split_h(lay, AT_XL, i, j)
                        act.wait_ge(g_gated, n + 1)
                        A(one(b_hi, m), one(tmp, m), ACT.Copy).then_inc(g_rounded, 1)

                def lru_gates(m, slot):
                    lm = lay * 8 + m
                    col = lambda b: b[:, bass.ds(lm, 1)]
                    t0, t1, t2, t3 = (tmp[:, q, :].rearrange("p (a b) -> p a b", a=2) for q in range(4, 8))
                    act.wait_ge(gates_ready, lm + 1)
                    act.wait_ge(y_ready, lm + 1)
                    A(t0, misc[:, 0:2, 0:HALF], ACT.Tanh, bias=col(half_ba), scale=0.5)
                    A(t1, misc[:, 2:4, 0:HALF], ACT.Tanh, bias=col(half_bx), scale=0.5).then_inc(gates_read, 1)
                    act.dma_start(wrg[:, slot, :], wrg_in[bass.ds(lm + 2, 1)].rearrange("o p n -> (o p) n")).then_inc(wrg_loaded[slot], 16)
                    act.wait_ge(r_ready, lm + 1)
                    A(t2, t0, ACT.Tanh, scale=col(sp_pos))
                    A(t3, t0, ACT.Exp, scale=col(sp_neg)).then_inc(a_ready, 1)
                    act.wait_ge(e_ready, lm + 1)
                    A(t0, t0, ACT.Sqrt, scale=0.25).then_inc(e_root, 1)

                def gelu(i, j):
                    act.wait_ge(cube_ready, lay * 8 + i * 4 + (j + 1))
                    A(side[:, j % 2, 0:TOK], side[:, j % 2, 0:TOK], ACT.Tanh, scale=0.7978845608028654).then_inc(gelu_tanh, 1)

                with act.Fori(0, 2) as i:
                    for j in range(4):
                        if j == 0:
                            act.wait_ge(g_gated, lay * 8 + 8)
                            act.wait_ge(o_split, lay * 8 + 8 + 1)
                        split_h(lay, AT_GL, i, j)
                        if j:
                            gelu(i, j - 1)
                        if j % 2 == 0:
                            lru_gates(i * 2 + j // 2, j // 2)
                    gelu(i, 3)
                with act.Fori(0, 2) as i:
                    for j in range(4):
                        split_h(lay, AT_RET, i, j)
                        if j % 2 == 0:
                            lru_gates(i * 2 + (4 + j // 2), j // 2)
                with act.Fori(0, 2) as i:
                    for j in range(4):
                        n, m = lay * 8 + i * 4 + j, i * 4 + j
                        split_h(lay, AT_MB, i, j)
                        act.wait_ge(y_ready, lay * 8 + 8 + 1)
                        A(one(tmp, m), acc[j % 2][:, :, 0:HALF], ACT.Sigmoid).then_inc(mb_sig, 1)
                        A(one(b_hi, m), one(qk, m), ACT.Copy).then_inc(y_rounded, 1)
                plain(lay, AT_LRU, 1)
                zero = lay * 0
                for j in range(3):
                    split_h(lay, AT_LRU + 4, zero, j)
                act.wait_ge(tile_done, lay * LAYER_TILES + (AT_LRU + 8))
                for m in range(KT):
                    act.wait_ge(m_ready, lay * 8 + m + 1)
                    A(one(b_hi, zero + m), one(mix, zero + m), ACT.Copy).then_inc(m_rounded, 1)
                split_h(lay, AT_LRU + 4, zero, 3)
                plain(lay, AT_OUT, 2)
                n = lay * ADA_GROUPS + ADA_FIRST
                ada_row_out(n, 0)
                norm_std(lay, 1)
                ada_sum_out(n, 0)
                for m in range(KT):
                    norm_tile(lay, 1, m, scale2, 3 * KT)
                    if m == 2:
                        ada_row_out(n + 1, 1)
                    if m == 4:
                        ada_sum_out(n + 1, 1)
                with act.Fori(0, QUARTERS) as qt:
                    with act.Fori(0, 2) as i:
                        for j in range(4):
                            n, m = lay * 32 + qt * 8 + i * 4 + j, i * 4 + j
                            split_h(lay, AT_MLP, qt * 4 + i, j)
                            act.wait_ge(u_ready, n + 1)
                            A(one(b_hi, m), tmp[:, 2 + j % 2, :].rearrange("p (a b) -> p a b", a=2), ACT.Copy).then_inc(u_rounded, 1)
                    with act.Fori(0, 2) as i:
                        for j in range(4):
                            split_h(lay, AT_MLP + 8, qt * 4 + i, j)

            act.wait_ge(mean_ready, 2 * DEPTH + 1)
            A(qk[:, 2, :].rearrange("p (a b) -> p a b", a=2), misc[:, 0:2, 0:HALF], ACT.Sqrt, bias=eps_n[:]).then_inc(std_ready, 1)
            act.wait_ge(y_ready, DEPTH * 8 + 1)
            act.wait_ge(conv_kept, DEPTH * 8 + 1)
            act.dma_start(lru_out, lru_c[:]).then_inc(stored, 16)
            act.dma_start(conv_out, conv_c[:]).then_inc(stored, 16)
            act.wait_ge(y_done, KT)
            act.dma_start(y_out, tmp[:]).then_inc(stored, 16)
            act.wait_ge(stored, 48)
            for j in range(2):
                act.wait_ge(wrg_loaded[j], 16 * (DEPTH * KT // 2 + 1))
            for j in range(4):
                act.wait_ge(raw_loaded[j], 16 * (STREAM // 4))

        @block.vector
        def _(dve):
            V = nc.vector
            dve.sem_inc(acc_free, 2)
            for one_more in start_at_1["dve"]:
                dve.sem_inc(one_more, 1)
            V.memset(eps_n[:], NORM_EPS)
            V.memset(eps_g[:], GN_EPS)
            dve.wait_ge(setup_act, 1)
            V.tensor_tensor(c_act[:], tmp[:, 0, 0:KT * GROUPS], tmp[:, 1, 0:KT * GROUPS], ALU.mult).then_inc(setup_dve, 1)
            V.memset(q_sm[:], 0.0)
            V.memset(p_ms[:], 0.0)
            dve.wait_ge(setup_act, 3)
            lam = small[:, :, S_LAM:S_LAM + KT]
            e, d, s, s2, p, rl = (tmp[:, 4, 16 * n:16 * n + 16] for n in range(6))
            ch = Chain(dve, setup_dve, 1)
            ch.link(V.tensor_scalar(d, e, 2.0, None, ALU.add))
            ch.link(V.reciprocal(p, d))
            ch.link(V.tensor_tensor(s, e, p, ALU.mult))
            ch.link(V.tensor_tensor(s2, s, s, ALU.mult))
            ch.link(V.tensor_scalar(p, s2, 1.0 / 15, None, ALU.mult))
            for k in (13, 11, 9, 7, 5, 3):
                ch.link(V.scalar_tensor_tensor(p, p, 1.0 / k, s2, ALU.add, ALU.mult))
            ch.link(V.scalar_tensor_tensor(p, p, 1.0, s, ALU.add, ALU.mult))
            ch.link(V.tensor_scalar(rl.rearrange("p (l k) -> p l k", l=2), lam, -1.0, 0.0, ALU.mult, ALU.max))
            ch.link(V.scalar_tensor_tensor(s, p, 2.0, rl, ALU.mult, ALU.add))
            V.tensor_scalar(sp_pos[:], s, 8.0, None, ALU.mult)
            V.tensor_scalar(sp_neg[:], s, -8.0, None, ALU.mult)
            V.tensor_scalar(half_ba[:].rearrange("p (l k) -> p l k", l=2), small[:, :, S_BA:S_BA + KT], 0.5, None, ALU.mult)
            ch.link(V.tensor_scalar(half_bx[:].rearrange("p (l k) -> p l k", l=2), small[:, :, S_BX:S_BX + KT], 0.5, None, ALU.mult))
            V.memset(qk[:, 0, :], 0.0).then_inc(setup_dve, 1)
            with dve.Fori(0, KT) as m:
                row = x[:, bass.ds(m, 1), :].rearrange("p o n -> p (o n)")
                V.tensor_tensor(qk[:, 1, :], row, row, ALU.mult).then_inc(first_squares, 1)
                dve.wait_ge(first_squares, m * 2 + 1)
                V.tensor_tensor(qk[:, 0, :], qk[:, 0, :], qk[:, 1, :], ALU.add).then_inc(first_squares, 1)
                dve.wait_ge(first_squares, m * 2 + 2)
            dve.sem_inc(squares_ready, 1)
            for t in range(2):
                dve.wait_ge(h_split, t + 1)
                V.tensor_tensor(weight_l[:, t, :], raw[:, t, :], weight_h[:, t, :].bitcast(F32), ALU.subtract).then_inc(l_split, 1)

            def split_l(lay, off, i, j):
                dve.wait_ge(h_split, lay * LAYER_TILES + i * 4 + (off + j + 3))
                V.tensor_tensor(weight_l[:, j % 2, :], raw[:, (j + 2) % 4, :], weight_h[:, j % 2, :].bitcast(F32), ALU.subtract).then_inc(l_split, 1)

            def done(lay, off, i, j):
                dve.wait_ge(tile_done, lay * LAYER_TILES + i * 4 + (off + j + 1))

            def copied(lay, off, i, j):
                dve.wait_ge(acc_free, lay * LAYER_TILES + i * 4 + (off + j + 3))

            def norm(lay, which, scale, shift_at):
                n = lay * 2 + which
                std, rstd = qk[:, 2, :], qk[:, 3, :]
                rv = rstd.rearrange("p (a b) -> p a b", a=2)
                dve.wait_ge(std_ready, n + 1)
                V.reciprocal(rstd, std).then_inc(rstd_ready, 1)
                dve.wait_ge(rstd_ready, n + 1)
                carry(dve)

                def normed(m, base):
                    ch = Chain(dve, xn_chain, base)
                    ch.link(V.tensor_tensor(one(tmp, m), one(x, m), rv, ALU.mult))
                    xs = one(tmp, m)[:, :, HALF_P:HALF].rearrange("p a (b t) -> p a b t", t=DS)
                    hs = one(mix, m)[:, :, HALF_P:HALF].rearrange("p a (b t) -> p a b t", t=DS)
                    sc = scale[:, bass.ds(m, 1), 1:GROUPS].rearrange("p o (a b) -> p (o a) b", a=2).unsqueeze(3).to_broadcast([128, 2, 4, DS])
                    sh = ada[:, bass.ds(m + shift_at, 1), 1:GROUPS].rearrange("p o (a b) -> p (o a) b", a=2).unsqueeze(3).to_broadcast([128, 2, 4, DS])
                    ch.link(V.tensor_tensor(xs, xs, sc, ALU.mult))
                    V.tensor_tensor(hs, xs, sh, ALU.add).then_inc(xn_ready, 1)

                with dve.Fori(0, KT) as m:
                    normed(m, n * 16 + m * 2)

            with dve.Fori(0, DEPTH) as lay:
                dve.wait_ge(x_mlp, lay * 32 + 1)
                carry(dve)

                def gains(scale, seg, g_at):
                    gb = small[:, bass.ds(lay, 1), g_at:g_at + KT].rearrange("p o k -> p (o k)").unsqueeze(2).to_broadcast([128, KT, GROUPS])
                    V.scalar_tensor_tensor(scale[:], ada[:, seg * KT:(seg + 1) * KT, :], 1.0, gb, ALU.add, ALU.mult).then_inc(scales_ready, 1)

                dve.wait_ge(ada_ready, lay * ADA_GROUPS + 4 + 2)
                gains(scale1, 1, S_G1)
                dve.wait_ge(scales_ready, lay * 2 + 1)
                norm(lay, 0, scale1, 0)

                for off, factor in ((AT_Q, 1.0), (AT_K, DK ** -0.5)):
                    for j in range(4):
                        split_l(lay, off, 0, j)
                        done(lay, off, 0, j)
                        a = acc[j % 2][:, :, 0:HALF]
                        c0 = 4 * (j % 2)
                        t1, t2 = (o_t[:, c0 + q, :].rearrange("p (a b) -> p a b", a=2) for q in range(2))
                        dve.wait_ge(qk_ready, lay * 8 + max(off - AT_Q + j - 1, 0) + 1)
                        V.scalar_tensor_tensor(t1, a, factor, cos, ALU.mult, ALU.mult)
                        V.scalar_tensor_tensor(t2[0:64], a[64:128], factor, sin[64:128], ALU.mult, ALU.mult)
                        V.scalar_tensor_tensor(t2[64:128], a[0:64], factor, sin[0:64], ALU.mult, ALU.mult).then_inc(acc_free, 1)
                        copied(lay, off, 0, j)
                        V.tensor_tensor(qk[:, off - AT_Q + j, :], o_t[:, c0, :], o_t[:, c0 + 1, :], ALU.add).then_inc(qk_ready, 1)

                with dve.Fori(0, 2) as i:
                    for j in range(4):
                        done(lay, AT_V, i, j)
                        dst = o_t[:, 2 + j % 2, :]
                        V.tensor_copy(dst[:, 0:SEQ].rearrange("p (a b) -> p a b", a=2), prompt(acc[j % 2]))
                        V.tensor_copy(dst[:, SEQ:TOK].rearrange("p (a b) -> p a b", a=2), sample(acc[j % 2])).then_inc(acc_free, 1)
                        split_l(lay, AT_V, i, j)

                with dve.Fori(0, 2) as i:
                    dve.wait_ge(ret_p_stored, lay * 32 + i * 16 + 1)
                    V.memset(s_p[:], 0.0)
                    for c in range(4):
                        n = lay * 8 + i * 4 + c
                        dve.wait_ge(scores_ready, n + 1)
                        for e in range(2):
                            h = i * 2 + e
                            V.tensor_tensor(p_m[:, e, :], misc[:, 0, e * 256:e * 256 + 128], mask[:, bass.ds(h, 1), :].rearrange("p o t -> p (o t)"), ALU.mult)
                            last = V.tensor_scalar(kd_p[:, e, :], misc[:, 0, e * 256 + 128:e * 256 + 256], kdec[:, bass.ds(h, 1)], None, ALU.mult)
                        last.then_inc(masked_ready, 1)
                        done(lay, AT_MA, i, c)
                        V.tensor_copy(one(mix, i * 4 + c), acc[c % 2][:, :, 0:HALF]).then_inc(acc_free, 1)
                        split_l(lay, AT_MA, i, c)
                        dve.wait_ge(o_ready, n + 1 + 1)
                        for e in range(2):
                            last = V.scalar_tensor_tensor(s_p[:, e, :], s_p[:, e, :], cdec[:, bass.ds(i * 2 + e, 1)], misc[:, 2, e * 256:e * 256 + 256], ALU.mult, ALU.add)
                        last.then_inc(s_ready, 1)
                        ch = Chain(dve, norm_chain, n * 2)
                        V.bn_stats(bst[:, 0, :], misc[:, 1, 0:256])
                        ch.link(V.bn_stats(bst[:, 1, :], misc[:, 1, 256:512]), carry)
                        V.bn_aggr(mv[:, 0, :], bst[:, 0, :])
                        V.bn_aggr(mv[:, 1, :], bst[:, 1, :]).then_inc(mv_ready, 1)
                        dve.wait_ge(gstd_ready, n + 1)
                        ch.link(V.reciprocal(grs[:], gstd[:]))
                        for e in range(2):
                            last = V.tensor_scalar(on_p[:, e, :], misc[:, 1, e * 256:e * 256 + 256], mv[:, e, 0:1], grs[:, e:e + 1], ALU.subtract, ALU.mult)
                        last.then_inc(on_ready, 1)

                with dve.Fori(0, 2) as i:
                    for j in range(4):
                        e = j // 2
                        h, m = i * 2 + e, i * 4 + j
                        n = lay * 4 + i * 2 + e
                        o = misc[0:NB_S, 1, 0:DV]
                        if j % 2 == 0:
                            dve.wait_ge(s_scores_ready, n + 1)
                            V.tensor_tensor(p_ms[0:NB_S, 0:NB_S], misc[0:NB_S, 0, 0:NB_S], mask_s[:, bass.ds(h, 1), :].rearrange("p o t -> p (o t)"), ALU.mult)
                        kt = misc[0:NB_S, 0, 128:256].unsqueeze(1).to_broadcast([NB_S, DB // 2, DK])
                        km = kdm[:, bass.ds(h, 1), 4 * (j % 2):4 * (j % 2) + 4].rearrange("p o b -> p (o b)").unsqueeze(2).to_broadcast([NB_S, DB // 2, DK])
                        V.tensor_tensor(kd_s[0:NB_S], kt, km, ALU.mult).then_inc(s_masked_ready, 1)
                        split_l(lay, AT_G, i, j)
                        dve.wait_ge(g_sig, lay * 8 + i * 4 + (j + 1))
                        V.tensor_tensor(one(tmp, m), acc[j % 2][:, :, 0:HALF], one(tmp, m), ALU.mult).then_inc(acc_free, 1)
                        ch = Chain(dve, s_chain, n * 2)
                        if j % 2 == 0:
                            dve.wait_ge(s_o_ready, n + 1 + 1)
                            ch.link(V.bn_stats(bst[0:NB_S, 0, :], o), carry)
                            V.bn_aggr(mv[0:NB_S, 0, :], bst[0:NB_S, 0, :]).then_inc(s_mv_ready, 1)
                        for pair in (0, 1) if j % 2 == 0 else (2, 3):
                            dve.wait_ge(s_update_ready, n * 4 + (pair + 1))
                            s = s_s[:, e, 2 * pair:2 * pair + 2, :].rearrange("p b n -> p (b n)")
                            V.scalar_tensor_tensor(s, s, cdec_s[:, bass.ds(h, 1)], misc[:, 2 + pair % 2, :], ALU.mult, ALU.add).then_inc(s_state_ready, 1)
                        if j % 2 == 0:
                            dve.wait_ge(s_gstd_ready, n + 1)
                            ch.link(V.reciprocal(grs[0:NB_S, 0:1], gstd[0:NB_S, 0:1]))
                            V.tensor_scalar(on_s[0:NB_S], o, mv[0:NB_S, 0, 0:1], grs[0:NB_S, 0:1], ALU.subtract, ALU.mult).then_inc(s_on_ready, 1)

                with dve.Fori(0, 2) as i:
                    for j in range(4):
                        n, m = lay * 8 + i * 4 + j, i * 4 + j
                        a = acc[j % 2][:, :, 0:HALF]
                        pad = side[:, j % 2, 0:515]
                        flat_s = side[:, j % 2, 516:604]
                        pad_s = flat_s.rearrange("p (b t) -> p b t", t=11)
                        cs = side[:, j % 2, 604:668]
                        w = lambda k: small[:, bass.ds(lay, 1), bass.ds(m + (S_CW + 8 * k), 1)].rearrange("p o q -> p (o q)")
                        bcol = small[:, bass.ds(lay, 1), bass.ds(m + S_CB, 1)].rearrange("p o q -> p (o q)")
                        split_l(lay, AT_XL, i, j)
                        done(lay, AT_XL, i, j)
                        dve.wait_ge(conv_kept, lay * 8 + i * 4 + max(j - 1, 0) + 1)
                        V.memset(pad[:, 0:3], 0.0)
                        V.tensor_copy(pad_s[:, :, 0:3], conv0[:, bass.ds(lay * 8 + m, 1)].rearrange("p o b t -> p (o b) t"))
                        V.tensor_copy(pad[:, 3:515].rearrange("p (a b) -> p a b", a=2), prompt(a))
                        V.tensor_copy(flat_s.rearrange("p (a b t) -> p a b t", a=2, t=11)[:, :, :, 3:11], sample(a).rearrange("p a (b t) -> p a b t", t=DS)).then_inc(acc_free, 1)
                        copied(lay, AT_XL, i, j)
                        ch = Chain(dve, conv_chain, n * 4)
                        out = prompt(one(qk, m))
                        win = lambda k: pad[:, k:k + 512].rearrange("p (a b) -> p a b", a=2)
                        csv = cs.rearrange("p (b t) -> p b t", t=DS)
                        V.tensor_scalar(out, win(0), w(0), bcol, ALU.mult, ALU.add)
                        ch.link(V.tensor_scalar(csv, pad_s[:, :, 0:8], w(0), bcol, ALU.mult, ALU.add))
                        for k in range(1, 4):
                            V.scalar_tensor_tensor(out, win(k), w(k), out, ALU.mult, ALU.add)
                            ch.link(V.scalar_tensor_tensor(csv, pad_s[:, :, k:k + 8], w(k), csv, ALU.mult, ALU.add))
                        V.tensor_copy(sample(one(qk, m)), cs.rearrange("p (a b) -> p a b", a=2))
                        V.tensor_copy(conv_c[:, bass.ds(lay * 8 + m, 1), 0, :].rearrange("p o t -> p (o t)"), pad[:, 512:515])
                        V.tensor_copy(conv_c[:, bass.ds(lay * 8 + m, 1), 1:GROUPS, :].rearrange("p o b t -> p (o b) t"), pad_s[:, :, 8:11]).then_inc(conv_kept, 1)

                t = [tmp[:, q, :].rearrange("p (a b) -> p a b", a=2) for q in range(4, 8)]
                flat = [tmp[:, q, :] for q in range(4, 8)]

                def lru_first(m):
                    n = lay * 8 + m
                    ch = Chain(dve, lru_chain, n * 6)
                    dve.wait_ge(gates_read, n + 1 + 1)
                    V.tensor_scalar(flat[0], flat[0], 0.5, 0.5, ALU.mult, ALU.add).then_inc(r_ready, 1)
                    V.scalar_tensor_tensor(t[1], t[1], 1.0, one(qk, m), ALU.add, ALU.mult)
                    dve.wait_ge(a_ready, n + 1)
                    ch.link(V.tensor_tensor(flat[0], flat[3], flat[3], ALU.mult))
                    V.scalar_tensor_tensor(flat[0], flat[0], 1.0, flat[2], ALU.add, ALU.mult).then_inc(e_ready, 1)

                def lru_rest(m, slot):
                    n = lay * 8 + m
                    ch = Chain(dve, lru_chain, n * 6 + 1)
                    dve.wait_ge(e_root, n + 1)
                    ch.link(V.tensor_tensor(flat[1], flat[1], flat[0], ALU.mult))
                    first = lambda b: sample(b).rearrange("p a (b t) -> p a b t", t=DS)[:, :, :, 0]
                    hz = tmp[:, 4, 0:8].rearrange("p (a b) -> p a b", a=2)
                    ch.link(V.tensor_tensor(hz, first(t[3]), h0[:, bass.ds(lay * 8 + m, 1), :].rearrange("p o (a b) -> p (o a) b", a=2), ALU.mult))
                    V.memset(first(t[3]), 0.0)
                    ch.link(V.tensor_tensor(first(t[1]), first(t[1]), hz, ALU.add))
                    ch.link(V.tensor_tensor_scan(t[2][:, 0, 0:HALF_P], t[3][:, 0, 0:HALF_P], t[1][:, 0, 0:HALF_P], 0.0, ALU.mult, ALU.add))
                    V.tensor_tensor_scan(t[2][:, 1, 0:HALF_P], t[3][:, 1, 0:HALF_P], t[1][:, 1, 0:HALF_P], t[2][:, 0, HALF_P - 1:HALF_P], ALU.mult, ALU.add)
                    for a in range(2):
                        last = V.tensor_tensor_scan(t[2][:, a, HALF_P:HALF], t[3][:, a, HALF_P:HALF], t[1][:, a, HALF_P:HALF], 0.0, ALU.mult, ALU.add)
                    ch.link(last)
                    V.tensor_copy(lru_c[:, bass.ds(lay * 8 + m, 1), 0:1].rearrange("p o q -> p (o q)"), t[2][:, 1, HALF_P - 1:HALF_P])
                    V.tensor_copy(lru_c[:, bass.ds(lay * 8 + m, 1), 1:GROUPS].rearrange("p o (a b) -> p (o a) b", a=2),
                                  sample(t[2]).rearrange("p a (b t) -> p a b t", t=DS)[:, :, :, DS - 1])
                    dve.wait_ge(gelu_ready, slot + 1)
                    V.scalar_tensor_tensor(one(qk, m), one(tmp, slot_of(m)), 0.5, t[2], ALU.mult, ALU.mult).then_inc(y_ready, 1)

                def gelu(i, j):
                    n = lay * 8 + i * 4 + j
                    dve.wait_ge(gelu_tanh, n + 1)
                    V.scalar_tensor_tensor(tmp[:, j, :], side[:, j % 2, 0:TOK], 1.0, tmp[:, j, :], ALU.add, ALU.mult).then_inc(gelu_ready, 1)

                with dve.Fori(0, 2) as i:
                    slot_of = lambda m: m
                    for j in range(4):
                        if j == 3:
                            split_l(lay, AT_GL, i, j)
                            gelu(i, j - 1)
                            lru_rest(i * 2 + j // 2, lay * 8 + i * 2 + (j // 2 + 1))
                        done(lay, AT_GL, i, j)
                        dve.wait_ge(y_ready, lay * 8 + i * 2 + (j // 2 + j // 3) + 1)
                        V.tensor_copy(tmp[:, j, :].rearrange("p (a b) -> p a b", a=2), acc[j % 2][:, :, 0:HALF]).then_inc(acc_free, 1)
                        if j != 3:
                            split_l(lay, AT_GL, i, j)
                        if j in (1, 2):
                            gelu(i, j - 1)
                        if j % 2 == 0:
                            lru_first(i * 2 + j // 2)
                        elif j == 1:
                            lru_rest(i * 2 + j // 2, lay * 8 + i * 2 + (j // 2 + 1))
                    gelu(i, 3)
                with dve.Fori(0, 2) as i:
                    slot_of = lambda m: i * 2 + j // 2
                    for j in range(4):
                        split_l(lay, AT_RET, i, j)
                        done(lay, AT_RET, i, j)
                        dve.wait_ge(ma_ready, lay * 8 + 8)
                        V.tensor_tensor(one(mix, i * 4 + j), acc[j % 2][:, :, 0:HALF], one(mix, i * 4 + j), ALU.mult).then_inc(acc_free, 1)
                        if j % 2 == 0:
                            lru_first(i * 2 + (4 + j // 2))
                        else:
                            lru_rest(i * 2 + (4 + j // 2), lay * 8 + 8)

                with dve.Fori(0, 2) as i:
                    for j in range(4):
                        n, m = lay * 8 + i * 4 + j, i * 4 + j
                        split_l(lay, AT_MB, i, j)
                        dve.wait_ge(mb_sig, n + 1)
                        dve.wait_ge(y_rounded, n + 1)
                        V.tensor_tensor(one(b_lo, m), one(qk, m), one(b_hi, m).bitcast(F32), ALU.subtract).then_inc(acc_free, 1)

                def merge(i, j):
                    m = i * 4 + j
                    done(lay, AT_LRU, i, j)
                    V.tensor_tensor(one(tmp, m), acc[j % 2][:, :, 0:HALF], one(tmp, m), ALU.mult).then_inc(acc_free, 1)
                    copied(lay, AT_LRU, i, j)
                    V.tensor_tensor(one(mix, m), one(mix, m), one(tmp, m), ALU.add).then_inc(m_ready, 1)

                def split_merged(m):
                    dve.wait_ge(m_rounded, lay * 8 + m + 1)
                    V.tensor_tensor(one(b_lo, zero + m), one(mix, zero + m), one(b_hi, zero + m).bitcast(F32), ALU.subtract).then_inc(m_split, 1)

                with dve.Fori(0, 1) as i:
                    for j in range(4):
                        merge(i, j)
                        split_l(lay, AT_LRU, i, j)
                zero = lay * 0
                for j in range(4):
                    merge(zero + 1, j)
                    if j < 3:
                        split_l(lay, AT_LRU + 4, zero, j)
                for m in range(KT):
                    split_merged(m)
                split_l(lay, AT_LRU + 4, zero, 3)

                def gated_add(j, m, gate_at, base, signal, left):
                    dve.wait_ge(signal, left + 1)
                    a = acc[j % 2][:, :, 0:HALF]
                    gate = ada[:, bass.ds(m + gate_at, 1), 0:1].rearrange("p o q -> p (o q)")
                    gs = ada[:, bass.ds(m + gate_at, 1), 1:GROUPS].rearrange("p o (a b) -> p (o a) b", a=2).unsqueeze(3).to_broadcast([128, 2, 4, DS])
                    V.scalar_tensor_tensor(prompt(one(x, m)), prompt(a), gate, prompt(one(x, m)), ALU.mult, ALU.add)
                    ts = tmp[:, 4 + j % 2, 0:64]
                    V.tensor_tensor(ts.rearrange("p (a b t) -> p a b t", a=2, t=DS), sample(a).rearrange("p a (b t) -> p a b t", t=DS), gs, ALU.mult).then_inc(acc_free, 1)
                    base()
                    xs = sample(one(x, m))
                    V.tensor_tensor(xs, xs, ts.rearrange("p (a b) -> p a b", a=2), ALU.add).then_inc(signal, 1)

                with dve.Fori(0, 2) as i:
                    for j in range(4):
                        done(lay, AT_OUT, i, j)
                        gated_add(j, i * 4 + j, 2 * KT, lambda: copied(lay, AT_OUT, i, j), x_mixed, lay * 8 + i * 4 + max(j - 1, 0))
                        split_l(lay, AT_OUT, i, j)
                dve.wait_ge(ada_ready, lay * ADA_GROUPS + ADA_FIRST + 2)
                gains(scale2, 4, S_G2)
                dve.wait_ge(scales_ready, lay * 2 + 2)
                norm(lay, 1, scale2, 3 * KT)
                with dve.Fori(0, QUARTERS) as qt:
                    with dve.Fori(0, 2) as i:
                        for j in range(4):
                            n, m = lay * 32 + qt * 8 + i * 4 + j, i * 4 + j
                            done(lay, AT_MLP, qt * 4 + i, j)
                            V.tensor_scalar(tmp[:, j % 2, :].rearrange("p (a b) -> p a b", a=2), acc[j % 2][:, :, 0:HALF], 0.0, None, ALU.max).then_inc(acc_free, 1)
                            split_l(lay, AT_MLP, qt * 4 + i, j)
                            dve.wait_ge(u_rounded, n + 1)
                            V.tensor_tensor(one(b_lo, m), tmp[:, 2 + j % 2, :].rearrange("p (a b) -> p a b", a=2), one(b_hi, m).bitcast(F32), ALU.subtract).then_inc(u_split, 1)
                    dve.wait_ge(squares_ready, lay * 5 + qt + 2)
                    carry(dve)
                    with dve.Fori(0, 2) as i:
                        for j in range(4):
                            done(lay, AT_MLP + 8, qt * 4 + i, j)
                            dve.wait_ge(ada_ready, lay * ADA_GROUPS + ADA_GROUPS + 2)
                            gated_add(j, i * 4 + j, 5 * KT, lambda: copied(lay, AT_MLP + 8, qt * 4 + i, j), x_mlp,
                                      lay * 32 + qt * 8 + i * 4 + max(j - 1, 0))
                            split_l(lay, AT_MLP + 8, qt * 4 + i, j)

            dve.wait_ge(std_ready, 2 * DEPTH + 1)
            V.reciprocal(qk[:, 3, :], qk[:, 2, :]).then_inc(rstd_ready, 1)
            dve.wait_ge(rstd_ready, 2 * DEPTH + 1)
            with dve.Fori(0, KT) as m:
                flat = lambda b: b[:, bass.ds(m, 1), :].rearrange("p o n -> p (o n)")
                V.scalar_tensor_tensor(flat(tmp), flat(x), fg[:, bass.ds(m, 1)], qk[:, 3, :], ALU.mult, ALU.mult).then_inc(y_done, 1)

        @block.gpsimd
        def _(pool):
            G = nc.gpsimd

            def sum_squares(wait, chain):
                with pool.Fori(0, KT) as m:
                    wait(m)
                    flat = x[:, bass.ds(m, 1), :].rearrange("p o n -> p (o n)")
                    G.tensor_tensor(qk[:, 1, :], flat, flat, ALU.mult).then_inc(square_chain, 1)
                    pool.wait_ge(square_chain, chain + m * 2 + 1)
                    G.tensor_tensor(qk[:, 0, :], qk[:, 0, :], qk[:, 1, :], ALU.add).then_inc(square_chain, 1)
                    pool.wait_ge(square_chain, chain + m * 2 + 2)
                pool.sem_inc(squares_ready, 1)

            def add_bias(n, at_q, g):
                pool.wait_ge(ada_out_ready, n + 1)
                bias = small[:, bass.ds(lay, 1), bass.ds(at_q, 4)].rearrange("p o q -> p (o q)").unsqueeze(2).to_broadcast([128, 4, GROUPS])
                G.tensor_tensor(ada[:, bass.ds(at_q, 4), :], ada_sum[:, g], bias, ALU.add).then_inc(ada_ready, 1)

            def add_biases(first, groups):
                with pool.Fori(0, groups // 2) as i:
                    for g in range(2):
                        add_bias(lay * ADA_GROUPS + i * 2 + (first + g), i * 8 + (first + g) * 4, g)

            def lower(which, m):
                pool.wait_ge(h_rounded, lay * 16 + (which * KT + 1) + m)
                carry(pool)
                G.tensor_tensor(one(h_lo, m), one(mix, m), one(h_hi, m).bitcast(F32), ALU.subtract).then_inc(h_ready, 1)

            pool.sem_inc(ada_ready, 2)
            for one_more in start_at_1["pool"]:
                pool.sem_inc(one_more, 1)
            pool.wait_ge(params_loaded, 16 * 6)
            with pool.Fori(0, DEPTH) as lay:
                add_biases(0, 4)
                with pool.Fori(0, 2) as i:
                    for g in range(2):
                        for j in range(2):
                            lower(0, i * 4 + (g * 2 + j))
                        add_bias(lay * ADA_GROUPS + i * 2 + (4 + g), i * 8 + (4 + g) * 4, g)
                add_biases(8, ADA_FIRST - 8)
                with pool.Fori(0, 2) as i:
                    for c in range(4):
                        n = lay * 8 + i * 4 + c
                        pool.wait_ge(qk_ready, lay * 8 + 8 + 1)
                        pool.wait_ge(o_ready, lay * 8 + i * 4 + max(c - 1, 0) + 1)
                        cols = slice((c // 2) * HALF + (c % 2) * CHUNK, (c // 2) * HALF + (c % 2) * CHUNK + CHUNK)
                        for e in range(2):
                            h = i * 2 + e
                            G.tensor_copy(k_st[:, c % 2, e, :], qk[:, bass.ds(h + 4, 1), cols].rearrange("p o t -> p (o t)"))
                            last = G.tensor_tensor(q_st[:, c % 2, e, :], qk[:, bass.ds(h, 1), cols].rearrange("p o t -> p (o t)"),
                                                   qdec[:, bass.ds(h, 1), 0:CHUNK].rearrange("p o t -> p (o t)"), ALU.mult)
                        last.then_inc(stage_ready, 1)
                with pool.Fori(0, 4) as h:
                    n = lay * 4 + h
                    pool.wait_ge(s_o_ready, n + 1)
                    G.tensor_copy(k_ss[:].rearrange("p (a b) -> p a b", a=2), sample(one(qk, h + 4)))
                    dst = q_sm[:].rearrange("p (a b s) -> p a b s", a=2, s=72)[:, :, :, 0:DS]
                    src = sample(one(qk, h)).rearrange("p a (b t) -> p a b t", t=DS)
                    for a in range(2):
                        dec = qdec[:, bass.ds(h, 1), CHUNK:CHUNK + DS].to_broadcast([128, 4, DS])
                        last = G.tensor_tensor(dst[:, a], src[:, a], dec, ALU.mult)
                    last.then_inc(s_stage_ready, 1)
                with pool.Fori(0, KT) as m:
                    n = lay * 8 + m
                    pool.wait_ge(s_o_t_ready, lay * 4 + 4 + 1)
                    pool.wait_ge(acc_free, lay * LAYER_TILES + (AT_XL + 2))
                    G.tensor_tensor(one(tmp, m), one(tmp, m), one(o_t, m), ALU.mult).then_inc(g_gated, 1)
                    pool.wait_ge(g_rounded, n + 1)
                    carry(pool)
                    G.tensor_tensor(one(b_lo, m), one(tmp, m), one(b_hi, m).bitcast(F32), ALU.subtract).then_inc(o_split, 1)
                with pool.Fori(0, 2) as i:
                    for j in range(4):
                        n = lay * 8 + i * 4 + j
                        arg, g = side[:, j % 2, 0:TOK], tmp[:, j, :]
                        pool.wait_ge(acc_free, lay * LAYER_TILES + i * 4 + (AT_GL + j + 3))
                        pool.wait_ge(gelu_ready, lay * 8 + i * 4 + max(j - 1, 0) + 1)
                        pool.wait_ge(conv_kept, lay * 8 + 8 + 1)
                        G.tensor_tensor(arg, g, g, ALU.mult).then_inc(cube_chain, 1)
                        pool.wait_ge(cube_chain, n * 2 + 1)
                        carry(pool)
                        G.tensor_scalar(arg, arg, 0.044715, 1.0, ALU.mult, ALU.add).then_inc(cube_chain, 1)
                        pool.wait_ge(cube_chain, n * 2 + 2)
                        G.tensor_tensor(arg, arg, g, ALU.mult).then_inc(cube_ready, 1)
                base = lay * (5 * 17)
                pool.wait_ge(acc_free, lay * LAYER_TILES + (AT_LRU + 2))
                carry(pool)
                G.memset(qk[:, 0, :], 0.0).then_inc(square_chain, 1)
                pool.wait_ge(square_chain, base + 1)
                carry(pool)
                sum_squares(lambda m: pool.wait_ge(x_mixed, lay * 8 + m + 1 + 1), base + 1)
                n_ada = lay * ADA_GROUPS + ADA_FIRST
                zero = lay * 0
                add_bias(n_ada, zero + ADA_FIRST * 4, 0)
                for m in range(KT):
                    lower(1, zero + m)
                    if m == 4:
                        add_bias(n_ada + 1, zero + (ADA_FIRST + 1) * 4, 1)
                with pool.Fori(0, QUARTERS) as qt:
                    with pool.Fori(0, 4) as i:
                        for j in range(2):
                            n = lay * 32 + qt * 8 + i * 2 + j
                            pool.wait_ge(acc_free, lay * LAYER_TILES + qt * 16 + i * 2 + (AT_MLP + j + 3))
                            G.tensor_tensor(tmp[:, 2 + j, :], tmp[:, j, :], tmp[:, j, :], ALU.mult).then_inc(u_ready, 1)
                    qbase = base + 17 + qt * 17
                    pool.wait_ge(mean_ready, lay * 2 + 2)
                    carry(pool)
                    G.memset(qk[:, 0, :], 0.0).then_inc(square_chain, 1)
                    pool.wait_ge(square_chain, qbase + 1)
                    carry(pool)
                    sum_squares(lambda m: pool.wait_ge(x_mlp, lay * 32 + qt * 8 + m + 1 + 1), qbase + 1)

        @block.tensor
        def _(pe):
            M = nc.tensor.matmul
            pe.sem_inc(ada_used, 4)
            for one_more in start_at_1["pe"]:
                pe.sem_inc(one_more, 1)

            def stream_tile(lay, off, i, j, rhs_hi, rhs_lo, ready=None):
                pe.wait_ge(l_split, lay * LAYER_TILES + i * 4 + (off + j + 1))
                pe.wait_ge(acc_free, lay * LAYER_TILES + i * 4 + (off + j + 1))
                for k in range(KT):
                    if ready is not None:
                        ready(k)
                    wh = weight_h[:, j % 2, k * 128:(k + 1) * 128]
                    wl = weight_l[:, j % 2, k * 128:(k + 1) * 128]
                    for n, (w, r) in enumerate(((wh, rhs_hi), (wh, rhs_lo), (wl, rhs_hi))):
                        for half in range(2):
                            last = M(acc[j % 2][:, half, 0:HALF], w, r[:, k, half * HALF:(half + 1) * HALF], start=(k == 0 and n == 0), stop=(k == KT - 1 and n == 2))
                last.then_inc(tile_done, 1)

            def plain(lay, off, rhs_hi, rhs_lo, ready=None):
                with pe.Fori(0, 2) as i:
                    for j in range(4):
                        stream_tile(lay, off, i, j, rhs_hi, rhs_lo, ready if j == 0 else None)

            def mean_square(n):
                pe.wait_ge(squares_ready, n)
                for half in range(2):
                    last = M(misc[:, half, 0:HALF], mean_w, qk[:, 0, half * HALF:(half + 1) * HALF], start=True, stop=True)
                last.then_inc(mean_ready, 1)

            pe.wait_ge(setup_dve, 1)
            with pe.Fori(0, DEPTH) as lay:
                def ada_group(n, g, between=None):
                    pe.wait_ge(ada_ready, n + 1)
                    for j in range(4):
                        pe.wait_ge(ada_loaded[j], n * 16 + 16)
                        for kk in range(2):
                            k = 2 * j + kk
                            last = M(misc[0:GROUPS, 2 + g, :], c_act[:, k * GROUPS:(k + 1) * GROUPS], ada_raw[j][:, kk * 512:(kk + 1) * 512], start=(k == 0), stop=(k == KT - 1))
                        last.then_inc(ada_used, 1)
                        if j == 0 and between is not None:
                            between()

                def ada_groups(first, groups):
                    with pe.Fori(0, groups // 2) as i:
                        n = lay * ADA_GROUPS + i * 2 + first
                        ada_group(n, 0)
                        ada_group(n + 1, 1, lambda: turn(n, 0))
                        turn(n + 1, 1)

                def turn(n, g):
                    pe.wait_ge(ada_copied, n + 1)
                    for q in range(4):
                        last = M(misc[:, 2 + g, q * 96:(q + 1) * 96], ada_row[0:GROUPS, q * 128:(q + 1) * 128], ident[0:GROUPS, 0:96], start=True, stop=True)
                    last.then_inc(ada_turned, 1)

                ada_groups(0, 4)
                mean_square(lay * 5 + 1)
                ada_groups(4, ADA_FIRST - 4)
                h_parts = lambda k: pe.wait_ge(h_ready, lay * 16 + (k + 1))
                for off in (AT_Q, AT_K):
                    for j in range(4):
                        stream_tile(lay, off, 0, j, h_hi, h_lo, h_parts if off == AT_Q and j == 0 else None)

                def turn_v(n, j):
                    pe.wait_ge(acc_free, n[0] + (j + 3))
                    pe.wait_ge(v_ready, n[1] + j + 1)
                    src = o_t[:, 2 + j % 2, :]
                    for c in range(4):
                        nc.tensor.transpose(misc[:, 0, c * 128:(c + 1) * 128], src[:, c * 128:(c + 1) * 128], ident)
                    nc.tensor.transpose(misc[0:NB_S, 1, 0:128], src[:, SEQ:TOK], ident).then_inc(v_turned, 1)

                with pe.Fori(0, 2) as i:
                    n = (lay * LAYER_TILES + i * 4 + (AT_V), lay * 8 + i * 4)
                    for j in range(4):
                        stream_tile(lay, AT_V, i, j, h_hi, h_lo)
                        if j:
                            turn_v(n, j - 1)
                    turn_v(n, 3)

                def turn_o(n):
                    pe.wait_ge(on_ready, n + 1)
                    pe.wait_ge(o_t_ready, n + 1)
                    for e in range(2):
                        for half in range(2):
                            last = nc.tensor.transpose(misc[:, 3, (2 * e + half) * 128:(2 * e + half + 1) * 128], on_p[:, e, half * 128:(half + 1) * 128], ident)
                    last.then_inc(on_turned, 1)

                with pe.Fori(0, 2) as i:
                    for c in range(4):
                        n = lay * 8 + i * 4 + c
                        pe.wait_ge(stage_ready, n + 1)
                        pe.wait_ge(v_ready, lay * 8 + 8 + 1)
                        for e in range(2):
                            qc = qk[:, bass.ds(i * 2 + e, 1), (c // 2) * HALF + (c % 2) * CHUNK:(c // 2) * HALF + (c % 2) * CHUNK + CHUNK].rearrange("p o t -> p (o t)")
                            M(misc[:, 0, e * 256:e * 256 + 128], k_st[:, c % 2, e, :], qc, start=True, stop=True)
                            last = nc.tensor.transpose(misc[:, 0, e * 256 + 128:e * 256 + 256], k_st[:, c % 2, e, :], ident)
                        last.then_inc(scores_ready, 1)
                        stream_tile(lay, AT_MA, i, c, h_hi, h_lo)
                        if c:
                            turn_o(lay * 8 + i * 4 + (c - 1))
                        pe.wait_ge(masked_ready, n + 1)
                        pe.wait_ge(s_ready, n + 1)
                        for e in range(2):
                            v = v_tok[:, c, bass.ds(i * 512 + e * 256, 256)]
                            M(misc[:, 1, e * 256:e * 256 + 256], p_m[:, e, :], v, start=True, stop=False)
                            M(misc[:, 1, e * 256:e * 256 + 256], q_st[:, c % 2, e, :], s_p[:, e, :], start=False, stop=True)
                            last = M(misc[:, 2, e * 256:e * 256 + 256], kd_p[:, e, :], v, start=True, stop=True)
                        last.then_inc(o_ready, 1)
                    turn_o(n)

                def sample_scores(n, h):
                    pe.wait_ge(s_stage_ready, n + 1)
                    pe.wait_ge(o_t_ready, lay * 8 + 8 + 1)
                    M(misc[0:NB_S, 0, 0:NB_S], k_ss[:], sample(one(qk, h)), start=True, stop=True)
                    nc.tensor.transpose(misc[0:NB_S, 0, 128:256], k_ss[:], ident).then_inc(s_scores_ready, 1)

                def sample_o(n, v):
                    pe.wait_ge(s_masked_ready, n * 2 + 1)
                    pe.wait_ge(s_o_t_ready, n + 1)
                    carry(pe)
                    o = misc[:, 1, 0:DV]
                    M(o, p_ms[0:NB_S, :], v, start=True, stop=False)
                    for b in range(DB):
                        last = M(o, q_sm[:, b * 64:b * 64 + 128], s_s[:, e, b, :], start=False, stop=(b == DB - 1))
                    last.then_inc(s_o_ready, 1)

                def sample_updates(n, pairs, v):
                    for pair in pairs:
                        if pair > 1:
                            pe.wait_ge(s_state_ready, n * 4 + (pair - 1))
                            carry(pe)
                        for b in range(2):
                            last = M(misc[:, 2 + pair % 2, b * 256:(b + 1) * 256], kd_s[0:NB_S, 2 * (pair % 2) + b, :], v, start=True, stop=True)
                        last.then_inc(s_update_ready, 1)

                with pe.Fori(0, 2) as i:
                    for j in range(4):
                        e = j // 2
                        n = lay * 4 + i * 2 + e
                        v = v_s[0:NB_S, bass.ds(i * 512 + e * 256, 256)]
                        if j % 2 == 0:
                            sample_scores(n, i * 2 + e)
                        stream_tile(lay, AT_G, i, j, h_hi, h_lo)
                        if j % 2 == 0:
                            pe.wait_ge(state_loaded[e], lay * 32 + i * 16 + 16)
                            sample_o(n, v)
                            sample_updates(n, (0, 1), v)
                        else:
                            pe.wait_ge(s_masked_ready, n * 2 + 2)
                            sample_updates(n, (2, 3), v)
                            pe.wait_ge(s_on_ready, n + 1)
                            carry(pe)
                            for half in range(2):
                                last = nc.tensor.transpose(misc[:, 1, 256 + 64 * half:320 + 64 * half], on_s[0:NB_S, half * 128:(half + 1) * 128], ident[0:NB_S, 0:NB_S])
                            last.then_inc(s_turned, 1)

                b_parts = lambda s, base: (lambda k: pe.wait_ge(s, base + (k + 1)))
                plain(lay, AT_XL, h_hi, h_lo)

                def gates(m, slot, turn):
                    n = lay * 8 + m
                    pe.wait_ge(conv_kept, n + 1 + 1)
                    pe.wait_ge(wrg_loaded[slot], lay * 64 + i * 16 + 16 * turn)
                    pe.wait_ge(gates_read, n + 1)
                    pe.wait_ge(s_o_t_ready, lay * 4 + 4 + 1)
                    for gate in range(2):
                        for half in range(2):
                            rhs = qk[:, bass.ds(m, 1), half * HALF:(half + 1) * HALF].rearrange("p o t -> p (o t)")
                            last = M(misc[:, 2 * gate + half, 0:HALF], wrg[:, slot, gate * 128:(gate + 1) * 128], rhs, start=True, stop=True)
                    last.then_inc(gates_ready, 1)

                with pe.Fori(0, 2) as i:
                    for j in range(4):
                        if j % 2 == 0:
                            gates(i * 2 + j // 2, j // 2, 1)
                        stream_tile(lay, AT_GL, i, j, h_hi, h_lo)
                with pe.Fori(0, 2) as i:
                    for j in range(4):
                        if j % 2 == 0:
                            gates(i * 2 + (4 + j // 2), j // 2, 3)
                        stream_tile(lay, AT_RET, i, j, b_hi, b_lo, b_parts(o_split, lay * 8 + 1) if j == 0 else None)
                plain(lay, AT_MB, h_hi, h_lo)
                plain(lay, AT_LRU, b_hi, b_lo, b_parts(acc_free, lay * LAYER_TILES + (AT_MB + 2)))
                plain(lay, AT_OUT, b_hi, b_lo, b_parts(m_split, lay * 8))
                n = lay * ADA_GROUPS + ADA_FIRST
                ada_group(n, 0)
                mean_square(lay * 5 + 2)
                turn(n, 0)
                ada_group(n + 1, 1)
                turn(n + 1, 1)
                h2_parts = lambda k: pe.wait_ge(h_ready, lay * 16 + (k + 9))
                with pe.Fori(0, QUARTERS) as qt:
                    with pe.Fori(0, 2) as i:
                        for j in range(4):
                            stream_tile(lay, AT_MLP, qt * 4 + i, j, h_hi, h_lo, h2_parts if j == 0 else None)
                    with pe.Fori(0, 2) as i:
                        for j in range(4):
                            stream_tile(lay, AT_MLP + 8, qt * 4 + i, j, b_hi, b_lo, b_parts(u_split, lay * 32 + qt * 8) if j == 0 else None)
            mean_square(DEPTH * 5 + 1)


def constants():
    t = np.zeros((128, NCONST), np.float32)

    def put(name, value):
        a, b = _off[name]
        value = np.asarray(value, np.float32)
        t[:value.shape[0], a:b] = value.reshape(value.shape[0], -1)

    half = DK // 2
    inv = np.float32(10000.0) ** (-np.arange(half, dtype=np.float32) / np.float32(half))
    pos_p = np.arange(SEQ, dtype=np.float32).reshape(2, HALF_P)
    pos_s = np.tile(np.float32(PAST) + np.arange(DS, dtype=np.float32), DB).reshape(2, HALF_S)
    pos = np.concatenate([pos_p, pos_s], axis=1)
    ang = (pos[None] * inv[:, None, None]).astype(np.float32).astype(np.float64)
    put("cos", np.concatenate([np.cos(ang)] * 2))
    put("sin", np.concatenate([np.sin(ang), -np.sin(ang)]))
    log_g = np.log1p(-np.exp2(-5.0 - np.arange(HEADS)))
    idx, ids = np.arange(CHUNK), np.arange(DS)
    q = np.concatenate([np.exp((idx + 1.0)[None] * log_g[:, None]), np.exp((ids + 1.0)[None] * log_g[:, None])], axis=1)
    put("qdec", np.broadcast_to(q, (128,) + q.shape))
    diff = idx[None, :] - idx[:, None]
    m = np.where(diff[:, None] >= 0, np.exp(np.maximum(diff, 0)[:, None] * log_g[None, :, None]), 0.0)
    put("mask", m)
    tok = np.arange(NB_S)
    diff = tok[None, :] - tok[:, None]
    same = (tok[None, :] // DS == tok[:, None] // DS) & (diff >= 0)
    put("mask_s", np.where(same[:, None], np.exp(np.maximum(diff, 0)[:, None] * log_g[None, :, None]), 0.0))
    own = tok[:, None] // DS == np.arange(DB)[None, :]
    put("kdm", own[:, None, :] * np.exp((DS - 1.0 - tok % DS)[:, None, None] * log_g[None, :, None]))
    put("kdec", np.exp((CHUNK - 1.0 - idx)[:, None] * log_g[None]))
    put("cdec", np.broadcast_to(np.exp(CHUNK * log_g), (128, HEADS)))
    put("cdec_s", np.broadcast_to(np.exp(DS * log_g), (128, HEADS)))
    put("ident", np.eye(128))
    put("mean", np.full((128, 128), 1.0 / DM))
    return t


def tiles(w):
    return w.reshape(KT, 128, -1, 128).transpose(2, 1, 0, 3).reshape(-1, 128, 1024)


def ada_tiles(w):
    return w.reshape(4, 2, 128, ADA_GROUPS, 512).transpose(3, 0, 2, 1, 4).reshape(-1, 128, 1024)


def per_feature(a):
    a = np.moveaxis(a, -1, 0)
    return np.ascontiguousarray(np.moveaxis(a.reshape((KT, 128) + a.shape[1:]), 0, 1))


def kernel(**inputs):
    import concourse.bacc as bacc
    from concourse.bass_utils import run_bass_kernel_spmd as run

    a = {k: np.asarray(v) for k, v in inputs.items()}
    w = []
    for l in range(DEPTH):
        z = a["w_in"][l]
        cut = lambda lo, hi: tiles(z[:, lo:hi])
        w += [cut(0, 2048), cut(5120, 6144), cut(2048, 3072), cut(3072, 4096), cut(4096, 5120),
              tiles(a["w_proj_ret"][l]), cut(6144, 7168), tiles(a["w_proj_lru"][l]), tiles(a["w_out"][l])]
        w1, w2 = tiles(a["w_mlp1"][l]), a["w_mlp2"][l]
        for q in range(QUARTERS):
            w += [w1[q * 8:(q + 1) * 8], tiles(w2[q * 1024:(q + 1) * 1024])]
    w.append(w[0][:STREAM - DEPTH * LAYER_TILES])
    w_ada = np.concatenate([ada_tiles(a["w_ada"][l]) for l in range(DEPTH)])
    stream = np.concatenate(w)

    xp = per_feature(a["x_prompt"][0]).reshape(128, KT, 2, HALF_P)
    xs = per_feature(a["x_sample"].reshape(NB_S, DM)).reshape(128, KT, 2, HALF_S)
    small = np.concatenate([
        a["b_ada"].reshape(DEPTH, 48, 128), a["norm1_g"].reshape(DEPTH, KT, 128), a["norm2_g"].reshape(DEPTH, KT, 128),
        a["conv_w"].reshape(DEPTH, DEC_W * KT, 128)] + [a[n].reshape(DEPTH, KT, 128) for n in ("conv_b", "b_rg_a", "b_rg_x", "lru_lambda")], axis=1)
    w_rg = np.concatenate([a["w_rg_a"], a["w_rg_x"]], axis=3).reshape(DEPTH * KT, 128, 256)
    arrays = {
        "stream": stream,
        "ada_in": w_ada,
        "x_in": np.ascontiguousarray(np.concatenate([xp, xs], axis=3).reshape(128, KT, TOK)),
        "c_in": np.ascontiguousarray(per_feature(np.concatenate([a["c_prompt"], a["c_sample"]])).reshape(128, KT * GROUPS)),
        "small_in": np.ascontiguousarray(small.transpose(2, 0, 1)),
        "fg_in": np.ascontiguousarray(a["final_g"].reshape(KT, 128).T),
        "h0_in": np.ascontiguousarray(a["state_lru"].reshape(DEPTH, DB, KT, 128).transpose(3, 0, 2, 1).reshape(128, DEPTH * KT, DB)),
        "conv_in": np.ascontiguousarray(a["state_conv"].reshape(DEPTH, DB, 3, KT, 128).transpose(4, 0, 3, 1, 2).reshape(128, DEPTH * KT, DB, 3)),
        "wrg_in": np.concatenate([w_rg, w_rg[:2]]),
        "state_in": a["state_ret"],
        "const_in": constants(),
    }
    outs = {
        "y_out": (128, KT, TOK), "ret_p_out": (DEPTH * HEADS, DK, DV), "lru_out": (128, DEPTH * KT, GROUPS),
        "conv_out": (128, DEPTH * KT, GROUPS, 3), "ret_s_out": (DEPTH, DB, HEADS, DK, DV),
    }
    nc = bacc.Bacc("TRN2", target_bir_lowering=False, num_devices=1)
    ins = [nc.dram_tensor(n, v.shape, F32, kind="ExternalInput").ap() for n, v in arrays.items()]
    outs_ap = [nc.dram_tensor(n, s, F32, kind="ExternalOutput").ap() for n, s in outs.items()]
    build(nc, *ins, *outs_ap)
    r = run(nc, [arrays], core_ids=[0]).results[0]

    y = np.asarray(r["y_out"]).reshape(128, KT, 2, HALF)
    rows = lambda t: t.transpose(2, 3, 1, 0).reshape(-1, DM)
    lru = np.asarray(r["lru_out"]).reshape(128, DEPTH, KT, GROUPS).transpose(1, 3, 2, 0).reshape(DEPTH, GROUPS, DM)
    conv = np.asarray(r["conv_out"]).reshape(128, DEPTH, KT, GROUPS, 3).transpose(1, 3, 4, 2, 0).reshape(DEPTH, GROUPS, 3, DM)
    return (rows(y[..., :HALF_P]).reshape(1, SEQ, DM), rows(y[..., HALF_P:]).reshape(DB, DS, DM),
            np.asarray(r["ret_p_out"]).reshape(DEPTH, 1, HEADS, DK, DV), lru[:, :1], conv[:, :1],
            np.asarray(r["ret_s_out"]), lru[:, 1:], conv[:, 1:])
```

```python
from contextlib import ExitStack

import numpy as np
import concourse.bass as bass
from concourse import mybir

F32 = mybir.dt.float32
F32R = mybir.dt.float32r
ALU = mybir.AluOpType
ACT = mybir.ActivationFunctionType

DM, SEQ, DEPTH, DB, DS, PAST = 1024, 512, 2, 8, 8, 4096
HEADS, DK, DV, CHUNK = 4, 128, 256, 128
NORM_EPS, GN_EPS, DEC_W = 1e-6, 1e-5, 4
KT = DM // 128
HALF_P, HALF_S = SEQ // 2, DB * DS // 2
HALF = HALF_P + HALF_S
TOK = 2 * HALF
GROUPS = 1 + DB
ADA_COLS = 6 * DM
ADA_GROUPS = ADA_COLS // 512
ADA_FIRST = ADA_GROUPS * 5 // 6
NB_S = DB * DS

AT_Q, AT_K, AT_V = 0, 4, 8
AT_MA, AT_G, AT_XL, AT_GL, AT_RET, AT_MB, AT_LRU, AT_OUT = (16 + 8 * n for n in range(8))
AT_MLP = AT_OUT + 8
QUARTERS = 4
LAYER_TILES = AT_MLP + QUARTERS * 16
STREAM = DEPTH * LAYER_TILES + 4

_off = {}
_n = 0
for _name, _w in (("cos", TOK), ("sin", TOK), ("qdec", HEADS * (CHUNK + DS)), ("mask", HEADS * CHUNK),
                  ("mask_s", HEADS * NB_S), ("kdm", HEADS * DB), ("kdec", HEADS), ("cdec", HEADS),
                  ("cdec_s", HEADS), ("ident", 128), ("mean", 128)):
    _off[_name] = (_n, _n + _w)
    _n += _w
NCONST = _n
S_BADA, S_G1, S_G2, S_CW, S_CB, S_BA, S_BX, S_LAM, NSMALL = 0, 48, 56, 64, 96, 104, 112, 120, 128


class Chain:

    def __init__(self, eng, sem, base):
        self.eng, self.sem, self.base, self.n = eng, sem, base, 0

    def link(self, ins, carry=None):
        self.n += 1
        ins.then_inc(self.sem, 1)
        self.eng.wait_ge(self.sem, self.base + self.n)
        if carry is not None:
            carry(self.eng)


def one(buf, m):
    return buf[:, bass.ds(m, 1), :].rearrange("p o (a b) -> p (o a) b", a=2)


def prompt(tile):
    return tile[:, :, 0:HALF_P]


def sample(tile):
    return tile[:, :, HALF_P:HALF]


def build(nc, stream, ada_in, x_in, c_in, small_in, fg_in, h0_in, conv_in, wrg_in, state_in, const_in,
          y_out, ret_p_out, lru_out, conv_out, ret_s_out):
    ctx = ExitStack()
    with ctx:
        at = [(nc.sbuf_base + 31) // 32 * 32]

        def place(name, shape, dt=F32, offset=None):
            size = int(np.prod(shape[1:])) * 4
            if offset is None:
                offset = at[0]
                at[0] += (size + 31) // 32 * 32
                assert at[0] <= nc.sbuf_usable_end, (name, at[0])
            t = nc.alloc_sbuf_tensor_at(name, shape, dt, offset=offset)
            offs[name] = offset
            return t

        offs = {}
        raw = place("raw", [128, 4, 1024])
        weight_h = place("weight_h", [128, 2, 1024], F32R)
        weight_l = place("weight_l", [128, 2, 1024], F32R)
        x = place("x", [128, KT, TOK])
        h_hi = place("h_hi", [128, KT, TOK], F32R)
        h_lo = place("h_lo", [128, KT, TOK], F32R)
        b_hi = place("b_hi", [128, KT, TOK], F32R)
        b_lo = place("b_lo", [128, KT, TOK], F32R)
        mix = place("mix", [128, KT, TOK])
        qk = place("qk", [128, KT, TOK])
        o_t = place("o_t", [128, KT, TOK], F32, offs["b_hi"])
        tmp = place("tmp", [128, 8, TOK])
        side = place("side", [128, 2, 672])
        v_tok = place("v_tok", [128, SEQ // 128, DM], F32, offs["tmp"])
        v_s = place("v_s", [128, DM], F32, offs["side"])
        lo = offs["b_lo"]
        ada_raw = [place(f"ada_raw{n}", [128, 1024], F32, at_byte) for n, at_byte in
                   enumerate((offs["qk"] + 4 * TOK * 4, offs["qk"] + 4 * TOK * 4 + 4096, offs["side"], lo))]
        ada_row = place("ada_row", [128, 512], F32, lo + 4 * 4096)
        s_p = place("s_p", [128, 2, DV], F32, lo)
        on_p = place("on_p", [128, 2, DV], F32, lo + 2048)
        p_m = place("p_m", [128, 2, CHUNK], F32, lo + 4096)
        kd_p = place("kd_p", [128, 2, DK], F32, lo + 5120)
        k_st = place("k_st", [128, 2, 2, CHUNK], F32, lo + 6144)
        q_st = place("q_st", [128, 2, 2, CHUNK], F32, lo + 8192)
        s_s = place("s_s", [128, 2, DB, DV], F32, lo)
        k_ss = place("k_ss", [128, NB_S], F32, lo + 16640)
        on_s = place("on_s", [128, DV], F32, lo + 16896)
        wrg = place("wrg", [128, 2, 256])
        kd_s = place("kd_s", [128, DB // 2, DK])
        q_sm = place("q_sm", [128, DB * 72])
        p_ms = place("p_ms", [128, 128])
        const = place("const", [128, NCONST])
        small = place("small", [128, DEPTH, NSMALL])
        fg = place("fg", [128, KT])
        h0 = place("h0", [128, DEPTH * KT, DB])
        conv0 = place("conv0", [128, DEPTH * KT, DB, 3])
        lru_c = place("lru_c", [128, DEPTH * KT, GROUPS])
        conv_c = place("conv_c", [128, DEPTH * KT, GROUPS, 3])
        ada = place("ada", [128, 6 * KT, GROUPS])
        ada_sum = place("ada_sum", [128, 2, 4, GROUPS])
        scale1 = place("scale1", [128, KT, GROUPS])
        scale2 = place("scale2", [128, KT, GROUPS])
        c_act = place("c_act", [128, KT * GROUPS])
        sp_pos = place("sp_pos", [128, DEPTH * KT])
        sp_neg = place("sp_neg", [128, DEPTH * KT])
        half_ba = place("half_ba", [128, DEPTH * KT])
        half_bx = place("half_bx", [128, DEPTH * KT])
        bst = place("bst", [128, 2, 6])
        mv = place("mv", [128, 2, 2])
        gstd = place("gstd", [128, 2])
        grs = place("grs", [128, 2])
        eps_n = place("eps_n", [128, 1])
        eps_g = place("eps_g", [128, 1])

        def cst(name, rows=128):
            a, b = _off[name]
            return const[0:rows, a:b]

        cos = cst("cos").rearrange("p (a b) -> p a b", a=2)
        sin = cst("sin").rearrange("p (a b) -> p a b", a=2)
        qdec = cst("qdec").rearrange("p (h t) -> p h t", h=HEADS)
        mask = cst("mask").rearrange("p (h t) -> p h t", h=HEADS)
        mask_s = cst("mask_s", NB_S).rearrange("p (h t) -> p h t", h=HEADS)
        kdm = cst("kdm", NB_S).rearrange("p (h t) -> p h t", h=HEADS)
        kdec, cdec, cdec_s = cst("kdec"), cst("cdec"), cst("cdec_s")
        ident, mean_w = cst("ident"), cst("mean")

        acc = [ctx.enter_context(nc.psum_tensor(f"acc{n}", [128, 2, 512], F32)) for n in range(2)]
        misc = ctx.enter_context(nc.psum_tensor("misc", [128, 4, 512], F32))

        def sem(name):
            return ctx.enter_context(nc.semaphore(name))

        raw_loaded = [sem(f"raw_loaded{n}") for n in range(4)]
        h_split, l_split, tile_done, acc_free = sem("h_split"), sem("l_split"), sem("tile_done"), sem("acc_free")
        small_loaded, const_loaded = sem("small_loaded"), sem("const_loaded")
        params_loaded, setup_act, setup_dve = sem("params_loaded"), sem("setup_act"), sem("setup_dve")
        c_loaded = sem("c_loaded")
        ada_loaded = [sem(f"ada_loaded{n}") for n in range(4)]
        ada_used, ada_copied = sem("ada_used"), sem("ada_copied")
        ada_turned, ada_out_ready, ada_ready, scales_ready = sem("ada_turned"), sem("ada_out_ready"), sem("ada_ready"), sem("scales_ready")
        squares_ready, square_chain, mean_ready, std_ready = sem("squares_ready"), sem("square_chain"), sem("mean_ready"), sem("std_ready")
        rstd_ready, xn_ready, xn_chain, h_rounded, h_ready = sem("rstd_ready"), sem("xn_ready"), sem("xn_chain"), sem("h_rounded"), sem("h_ready")
        qk_ready, v_turned, v_ready = sem("qk_ready"), sem("v_turned"), sem("v_ready")
        ma_ready = sem("ma_ready")
        stage_ready, scores_ready, masked_ready = sem("stage_ready"), sem("scores_ready"), sem("masked_ready")
        o_ready, s_ready, mv_ready, gstd_ready, norm_chain = sem("o_ready"), sem("s_ready"), sem("mv_ready"), sem("gstd_ready"), sem("norm_chain")
        on_ready, on_turned, o_t_ready, ret_p_stored = sem("on_ready"), sem("on_turned"), sem("o_t_ready"), sem("ret_p_stored")
        state_loaded, state_stored = [sem(f"state_loaded{n}") for n in range(2)], [sem(f"state_stored{n}") for n in range(2)]
        s_stage_ready, s_scores_ready, s_masked_ready = sem("s_stage_ready"), sem("s_scores_ready"), sem("s_masked_ready")
        s_o_ready, s_update_ready, s_state_ready = sem("s_o_ready"), sem("s_update_ready"), sem("s_state_ready")
        s_mv_ready, s_gstd_ready, s_chain, s_on_ready = sem("s_mv_ready"), sem("s_gstd_ready"), sem("s_chain"), sem("s_on_ready")
        s_turned, s_o_t_ready = sem("s_turned"), sem("s_o_t_ready")
        g_sig, g_gated, g_rounded, o_split = sem("g_sig"), sem("g_gated"), sem("g_rounded"), sem("o_split")
        ret_mixed = sem("ret_mixed")
        conv_chain, conv_kept = sem("conv_chain"), sem("conv_kept")
        wrg_loaded = [sem(f"wrg_loaded{n}") for n in range(2)]
        gates_ready, gates_read, r_ready, a_ready, e_ready, e_root = sem("gates_ready"), sem("gates_read"), sem("r_ready"), sem("a_ready"), sem("e_ready"), sem("e_root")
        lru_chain, cube_chain, cube_ready, gelu_tanh, gelu_ready = (
            sem("lru_chain"), sem("cube_chain"), sem("cube_ready"), sem("gelu_tanh"), sem("gelu_ready"))
        lru_u_ready, scans_done, y_ready, y_rounded = sem("lru_u_ready"), sem("scans_done"), sem("y_ready"), sem("y_rounded")
        mb_sig, m_ready, m_rounded, m_split = sem("mb_sig"), sem("m_ready"), sem("m_rounded"), sem("m_split")
        gate_chain, x_mixed, x_mlp = sem("gate_chain"), sem("x_mixed"), sem("x_mlp")
        u_ready, u_rounded, u_split = sem("u_ready"), sem("u_rounded"), sem("u_split")
        y_done, stored, waited = sem("y_done"), sem("stored"), sem("waited")
        first_squares = sem("first_squares")

        def carry(eng):
            eng.sem_inc(waited, 1)

        start_at_1 = {
            "dve": (x_mlp, x_mixed, qk_ready, conv_kept, lru_u_ready, scans_done, y_ready, gelu_ready, s_ready),
            "act": (v_ready, o_t_ready, s_o_t_ready, gates_read, state_stored[0], state_stored[1], ret_p_stored),
            "pe": (o_ready, s_o_ready),
            "pool": (o_split,),
        }

        block = ctx.enter_context(nc.Block())

        @block.sync
        def _(sp):
            def load(t, slot):
                sp.dma_start(raw[:, slot, :], stream[bass.ds(t, 1)].rearrange("o p n -> (o p) n")).then_inc(raw_loaded[slot], 16)

            def load_range(lay, first, count):
                with sp.Fori(0, count // 4) as i:
                    for j in range(4):
                        sp.wait_ge(l_split, lay * LAYER_TILES + i * 4 + (first + j + 1))
                        load(lay * LAYER_TILES + i * 4 + (first + j + 4), j)

            def load_ada(lay, first, groups, left, count):
                def load_tile(t, slot):
                    sp.wait_ge(ada_used, t + 1)
                    sp.dma_start(ada_raw[slot][:], ada_in[bass.ds(t, 1)].rearrange("o p n -> (o p) n")).then_inc(ada_loaded[slot], 16)

                for j in range(4):
                    if j == 3:
                        sp.wait_ge(left, count)
                        carry(sp)
                    load_tile(lay * (ADA_GROUPS * 4) + (first * 4 + j), j)
                with sp.Fori(0, groups - 1) as i:
                    for j in range(4):
                        load_tile(lay * (ADA_GROUPS * 4) + i * 4 + (first * 4 + j + 4), j)

            with sp.Fori(0, DEPTH) as lay:
                load_ada(lay, 0, ADA_FIRST, x_mlp, lay * 32 + 1)
                load_range(lay, 0, AT_MLP)
                load_ada(lay, ADA_FIRST, ADA_GROUPS - ADA_FIRST, tile_done, lay * LAYER_TILES + AT_MLP)
                load_range(lay, AT_MLP, LAYER_TILES - AT_MLP)

        @block.scalar
        def _(act):
            A = nc.scalar.activation
            for one_more in start_at_1["act"]:
                act.sem_inc(one_more, 1)
            act.dma_start(tmp[:, 0, 0:KT * GROUPS], c_in).then_inc(c_loaded, 16)
            act.dma_start(small[:], small_in).then_inc(small_loaded, 16)
            act.dma_start(const[:], const_in).then_inc(const_loaded, 16)
            for dst, src in [(x[:], x_in), (fg[:], fg_in), (h0[:], h0_in), (conv0[:], conv_in)]:
                act.dma_start(dst, src).then_inc(params_loaded, 16)
            act.wait_ge(c_loaded, 16)
            c_raw, c_sig, c_silu = (tmp[:, n, 0:KT * GROUPS] for n in range(3))
            A(c_sig, c_raw, ACT.Sigmoid).then_inc(setup_act, 1)
            act.wait_ge(small_loaded, 16)
            lam = small[:, :, S_LAM:S_LAM + KT]
            e_abs, e_neg = tmp[:, 3, 0:16].rearrange("p (l k) -> p l k", l=2), tmp[:, 4, 0:16]
            A(e_abs, lam, ACT.Abs).then_inc(setup_act, 1)
            act.wait_ge(setup_act, 2)
            A(e_neg, tmp[:, 3, 0:16], ACT.Exp, scale=-1.0).then_inc(setup_act, 1)
            for t in range(2):
                act.dma_start(wrg[:, t, :], wrg_in[t]).then_inc(wrg_loaded[t], 16)
            for t in range(4):
                act.wait_ge(ada_used, t + 5)
                act.dma_start(raw[:, t, :], stream[t]).then_inc(raw_loaded[t], 16)

            def split_h(lay, off, i, j):
                act.wait_ge(tile_done, lay * LAYER_TILES + i * 4 + (off + j + 1))
                act.wait_ge(raw_loaded[(j + 2) % 4], lay * (LAYER_TILES * 4) + i * 16 + 16 * (off // 4 + (j + 2) // 4 + 1))
                A(weight_h[:, j % 2, :], raw[:, (j + 2) % 4, :], ACT.Copy).then_inc(h_split, 1)

            def copied(lay, off, i, j):
                act.wait_ge(acc_free, lay * LAYER_TILES + i * 4 + (off + j + 3))

            def plain(lay, off, iters):
                with act.Fori(0, iters) as i:
                    for j in range(4):
                        split_h(lay, off, i, j)

            def ada_row_out(n, g):
                act.wait_ge(ada_used, n * 4 + 8)
                A(ada_row[0:GROUPS, :], misc[0:GROUPS, 2 + g, :], ACT.Copy).then_inc(ada_copied, 1)

            def ada_sum_out(n, g):
                act.wait_ge(ada_turned, n + 1)
                act.wait_ge(ada_ready, n + 1)
                A(ada_sum[:, g], misc[:, 2 + g, 0:384].rearrange("p (q c) -> p q c", q=4)[:, :, 0:GROUPS], ACT.Copy).then_inc(ada_out_ready, 1)

            def ada_groups(lay, first, groups):
                with act.Fori(0, groups // 2) as i:
                    for g in range(2):
                        n = lay * ADA_GROUPS + i * 2 + (first + g)
                        ada_row_out(n, g)
                        ada_sum_out(n, g)

            def norm_std(lay, which):
                act.wait_ge(mean_ready, lay * 2 + which + 1)
                A(qk[:, 2, :].rearrange("p (a b) -> p a b", a=2), misc[:, 0:2, 0:HALF], ACT.Sqrt, bias=eps_n[:]).then_inc(std_ready, 1)

            def norm_tile(lay, which, m, scale, shift_at):
                act.wait_ge(xn_ready, lay * 16 + (which * KT + 1) + m)
                sc = scale[:, bass.ds(m, 1), 0:1].rearrange("p o a -> p (o a)")
                sh = ada[:, bass.ds(m + shift_at, 1), 0:1].rearrange("p o a -> p (o a)")
                A(prompt(one(mix, m)), prompt(one(tmp, m)), ACT.Identity, bias=sh, scale=sc)
                A(prompt(one(h_hi, m)), prompt(one(tmp, m)), ACT.Identity, bias=sh, scale=sc)
                A(sample(one(h_hi, m)), sample(one(mix, m)), ACT.Copy).then_inc(h_rounded, 1)

            with act.Fori(0, DEPTH) as lay:
                ada_groups(lay, 0, 4)
                norm_std(lay, 0)
                with act.Fori(0, 2) as i:
                    for g in range(2):
                        for j in range(2):
                            norm_tile(lay, 0, i * 4 + (g * 2 + j), scale1, 0)
                        ada_row_out(lay * ADA_GROUPS + i * 2 + (4 + g), g)
                        ada_sum_out(lay * ADA_GROUPS + i * 2 + (4 + g), g)
                ada_groups(lay, 8, ADA_FIRST - 8)
                for j in range(4):
                    split_h(lay, AT_Q, 0, j)
                for j in range(4):
                    split_h(lay, AT_K, 0, j)

                with act.Fori(0, 2) as i:
                    for j in range(4):
                        split_h(lay, AT_V, i, j)
                        n, m = lay * 8 + i * 4 + j, i * 4 + j
                        act.wait_ge(v_turned, n + 1)
                        A(v_tok[:, :, bass.ds(m * 128, 128)], misc[:, 0, :].rearrange("p (c d) -> p c d", c=4), ACT.Copy)
                        A(v_s[0:NB_S, bass.ds(m * 128, 128)], misc[0:NB_S, 1, 0:128], ACT.Copy).then_inc(v_ready, 1)

                def o_evac(i, c, n):
                    act.wait_ge(on_turned, n + 1)
                    dst = o_t[:, bass.ds(i * 4, 4), (c // 2) * HALF + (c % 2) * CHUNK:(c // 2) * HALF + (c % 2) * CHUNK + CHUNK]
                    A(dst, misc[:, 3, :].rearrange("p (c d) -> p c d", c=4), ACT.Copy).then_inc(o_t_ready, 1)

                def store_state(i):
                    act.wait_ge(s_ready, lay * 8 + (i * 4 + 4) + 1)
                    act.dma_start(ret_p_out[bass.ds(lay * 4 + i * 2, 2)].rearrange("h p n -> p h n"), s_p[:]).then_inc(ret_p_stored, 16)

                zero = lay * 0
                for t in range(8):
                    i, c = t // 4, t % 4
                    n = lay * 8 + t
                    if t == 4:
                        split_h(lay, AT_MA, zero, t)
                    if t:
                        o_evac(zero + (t - 1) // 4, (t - 1) % 4, lay * 8 + (t - 1))
                    if t != 4:
                        split_h(lay, AT_MA, zero, t)
                    copied(lay, AT_MA, zero, t)
                    A(one(mix, zero + t), one(mix, zero + t), ACT.Sigmoid).then_inc(ma_ready, 1)
                    act.wait_ge(mv_ready, n + 1)
                    A(gstd[:], mv[:, :, 1], ACT.Sqrt, bias=eps_g[:]).then_inc(gstd_ready, 1)
                    if t == 3:
                        store_state(0)
                o_evac(zero + 1, 3, n)
                store_state(1)

                act.wait_ge(ret_p_stored, lay * 32 + 32 + 1)

                def load_state(i, e):
                    act.wait_ge(state_stored[e], lay * 32 + i * 16 + 1)
                    act.dma_start(s_s[:, e], state_in[bass.ds(lay, 1), :, bass.ds(i * 2 + e, 1)].rearrange("l b h p n -> p (l b h) n")).then_inc(state_loaded[e], 16)

                load_state(0, 0)
                load_state(0, 1)
                for i in range(2):
                    for j in range(4):
                        e, m = j // 2, i * 4 + j
                        n = lay * 4 + i * 2 + e
                        split_h(lay, AT_G, zero + i, j)
                        if i == 0 and j == 3:
                            load_state(1, 0)
                        if i == 1 and j == 1:
                            load_state(1, 1)
                        A(one(tmp, zero + m), acc[j % 2][:, :, 0:HALF], ACT.Sigmoid).then_inc(g_sig, 1)
                        if j % 2 == 0:
                            act.wait_ge(s_mv_ready, n + 1)
                            A(gstd[0:NB_S, 0:1], mv[0:NB_S, 0, 1:2], ACT.Sqrt, bias=eps_g[0:NB_S]).then_inc(s_gstd_ready, 1)
                        else:
                            act.wait_ge(s_turned, n + 1)
                            for half in range(2):
                                last = A(sample(one(o_t, zero + i * 4 + (2 * e + half))), misc[:, 1, 256 + 64 * half:320 + 64 * half].rearrange("p (a b) -> p a b", a=2), ACT.Copy)
                            last.then_inc(s_o_t_ready, 1)
                            act.wait_ge(s_state_ready, n * 4 + 4)
                            act.dma_start(ret_s_out[bass.ds(lay, 1), :, bass.ds(i * 2 + e, 1)].rearrange("l b h p n -> p (l b h) n"), s_s[:, e]).then_inc(state_stored[e], 16)

                for e in range(2):
                    act.wait_ge(state_stored[e], lay * 32 + 32 + 1)
                with act.Fori(0, 2) as i:
                    for j in range(4):
                        n, m = lay * 8 + i * 4 + j, i * 4 + j
                        split_h(lay, AT_XL, i, j)
                        act.wait_ge(g_gated, n + 1)
                        A(one(b_hi, m), one(tmp, m), ACT.Copy).then_inc(g_rounded, 1)

                def lru_gates(m, slot):
                    lm = lay * 8 + m
                    col = lambda b: b[:, bass.ds(lm, 1)]
                    t0, t1, t2, t3 = (tmp[:, q, :].rearrange("p (a b) -> p a b", a=2) for q in (4, 5 + slot, 6 - slot, 7))
                    act.wait_ge(lru_u_ready, lm + 1)
                    act.wait_ge(gates_ready, lm + 1)
                    A(t0, misc[:, 0:2, 0:HALF], ACT.Tanh, bias=col(half_ba), scale=0.5)
                    A(t1, misc[:, 2:4, 0:HALF], ACT.Tanh, bias=col(half_bx), scale=0.5).then_inc(gates_read, 1)
                    act.dma_start(wrg[:, slot, :], wrg_in[bass.ds(lm + 2, 1)].rearrange("o p n -> (o p) n")).then_inc(wrg_loaded[slot], 16)
                    act.wait_ge(r_ready, lm + 1)
                    act.wait_ge(scans_done, lm + 1)
                    A(t2, t0, ACT.Tanh, scale=col(sp_pos))
                    A(t3, t0, ACT.Exp, scale=col(sp_neg)).then_inc(a_ready, 1)
                    act.wait_ge(e_ready, lm + 1)
                    A(t0, t0, ACT.Sqrt, scale=0.25).then_inc(e_root, 1)

                def gelu(t):
                    act.wait_ge(cube_ready, lay * 8 + (t + 1))
                    A(side[:, t % 2, 0:TOK], side[:, t % 2, 0:TOK], ACT.Tanh, scale=0.7978845608028654).then_inc(gelu_tanh, 1)

                for t in range(16):
                    split_h(lay, AT_GL, lay * 0, t)
                    if t == 0:
                        act.wait_ge(g_gated, lay * 8 + 8)
                        act.wait_ge(o_split, lay * 8 + 8 + 1)
                    if 0 < t < 8 or t == 9:
                        gelu(min(t - 1, 7))
                    if t % 2 == 0:
                        lru_gates(lay * 0 + t // 2, t // 2 % 2)
                with act.Fori(0, 2) as i:
                    for j in range(4):
                        n, m = lay * 8 + i * 4 + j, i * 4 + j
                        split_h(lay, AT_MB, i, j)
                        act.wait_ge(y_ready, lay * 8 + 8 + 1)
                        A(one(tmp, m), acc[j % 2][:, :, 0:HALF], ACT.Sigmoid).then_inc(mb_sig, 1)
                        A(one(b_hi, m), one(qk, m), ACT.Copy).then_inc(y_rounded, 1)
                plain(lay, AT_LRU, 1)
                zero = lay * 0
                for j in range(3):
                    split_h(lay, AT_LRU + 4, zero, j)
                act.wait_ge(tile_done, lay * LAYER_TILES + (AT_LRU + 8))
                for m in range(KT):
                    act.wait_ge(m_ready, lay * 8 + m + 1)
                    A(one(b_hi, zero + m), one(mix, zero + m), ACT.Copy).then_inc(m_rounded, 1)
                split_h(lay, AT_LRU + 4, zero, 3)
                plain(lay, AT_OUT, 2)
                n = lay * ADA_GROUPS + ADA_FIRST
                ada_row_out(n, 0)
                norm_std(lay, 1)
                ada_sum_out(n, 0)
                for m in range(KT):
                    norm_tile(lay, 1, m, scale2, 3 * KT)
                    if m == 2:
                        ada_row_out(n + 1, 1)
                    if m == 4:
                        ada_sum_out(n + 1, 1)
                with act.Fori(0, QUARTERS) as qt:
                    with act.Fori(0, 2) as i:
                        for j in range(4):
                            n, m = lay * 32 + qt * 8 + i * 4 + j, i * 4 + j
                            split_h(lay, AT_MLP, qt * 4 + i, j)
                            act.wait_ge(u_ready, n + 1)
                            A(one(b_hi, m), tmp[:, 2 + j % 2, :].rearrange("p (a b) -> p a b", a=2), ACT.Copy).then_inc(u_rounded, 1)
                    with act.Fori(0, 2) as i:
                        for j in range(4):
                            split_h(lay, AT_MLP + 8, qt * 4 + i, j)

            act.wait_ge(mean_ready, 2 * DEPTH + 1)
            A(qk[:, 2, :].rearrange("p (a b) -> p a b", a=2), misc[:, 0:2, 0:HALF], ACT.Sqrt, bias=eps_n[:]).then_inc(std_ready, 1)
            act.wait_ge(y_ready, DEPTH * 8 + 1)
            act.wait_ge(conv_kept, DEPTH * 8 + 1)
            act.dma_start(lru_out, lru_c[:]).then_inc(stored, 16)
            act.dma_start(conv_out, conv_c[:]).then_inc(stored, 16)
            act.wait_ge(y_done, KT)
            act.dma_start(y_out, tmp[:]).then_inc(stored, 16)
            act.wait_ge(stored, 48)
            for j in range(2):
                act.wait_ge(wrg_loaded[j], 16 * (DEPTH * KT // 2 + 1))
            for j in range(4):
                act.wait_ge(raw_loaded[j], 16 * (STREAM // 4))

        @block.vector
        def _(dve):
            V = nc.vector
            dve.sem_inc(acc_free, 2)
            for one_more in start_at_1["dve"]:
                dve.sem_inc(one_more, 1)
            V.memset(eps_n[:], NORM_EPS)
            V.memset(eps_g[:], GN_EPS)
            dve.wait_ge(setup_act, 1)
            V.tensor_tensor(c_act[:], tmp[:, 0, 0:KT * GROUPS], tmp[:, 1, 0:KT * GROUPS], ALU.mult).then_inc(setup_dve, 1)
            V.memset(q_sm[:], 0.0)
            V.memset(p_ms[:], 0.0)
            dve.wait_ge(setup_act, 3)
            lam = small[:, :, S_LAM:S_LAM + KT]
            e, d, s, s2, p, rl = (tmp[:, 4, 16 * n:16 * n + 16] for n in range(6))
            ch = Chain(dve, setup_dve, 1)
            ch.link(V.tensor_scalar(d, e, 2.0, None, ALU.add))
            ch.link(V.reciprocal(p, d))
            ch.link(V.tensor_tensor(s, e, p, ALU.mult))
            ch.link(V.tensor_tensor(s2, s, s, ALU.mult))
            ch.link(V.tensor_scalar(p, s2, 1.0 / 15, None, ALU.mult))
            for k in (13, 11, 9, 7, 5, 3):
                ch.link(V.scalar_tensor_tensor(p, p, 1.0 / k, s2, ALU.add, ALU.mult))
            ch.link(V.scalar_tensor_tensor(p, p, 1.0, s, ALU.add, ALU.mult))
            ch.link(V.tensor_scalar(rl.rearrange("p (l k) -> p l k", l=2), lam, -1.0, 0.0, ALU.mult, ALU.max))
            ch.link(V.scalar_tensor_tensor(s, p, 2.0, rl, ALU.mult, ALU.add))
            V.tensor_scalar(sp_pos[:], s, 8.0, None, ALU.mult)
            V.tensor_scalar(sp_neg[:], s, -8.0, None, ALU.mult)
            V.tensor_scalar(half_ba[:].rearrange("p (l k) -> p l k", l=2), small[:, :, S_BA:S_BA + KT], 0.5, None, ALU.mult)
            ch.link(V.tensor_scalar(half_bx[:].rearrange("p (l k) -> p l k", l=2), small[:, :, S_BX:S_BX + KT], 0.5, None, ALU.mult))
            dve.wait_ge(params_loaded, 16 * 4)
            dve.wait_ge(const_loaded, 16)
            V.memset(qk[:, 0, :], 0.0).then_inc(setup_dve, 1)
            with dve.Fori(0, KT) as m:
                row = x[:, bass.ds(m, 1), :].rearrange("p o n -> p (o n)")
                V.tensor_tensor(qk[:, 1, :], row, row, ALU.mult).then_inc(first_squares, 1)
                dve.wait_ge(first_squares, m * 2 + 1)
                V.tensor_tensor(qk[:, 0, :], qk[:, 0, :], qk[:, 1, :], ALU.add).then_inc(first_squares, 1)
                dve.wait_ge(first_squares, m * 2 + 2)
            dve.sem_inc(squares_ready, 1)
            for t in range(2):
                dve.wait_ge(raw_loaded[t], 16)
                V.tensor_copy(weight_h[:, t, :], raw[:, t, :]).then_inc(h_split, 1)
                dve.wait_ge(h_split, t + 1)
                V.tensor_tensor(weight_l[:, t, :], raw[:, t, :], weight_h[:, t, :].bitcast(F32), ALU.subtract).then_inc(l_split, 1)

            def split_l(lay, off, i, j):
                dve.wait_ge(h_split, lay * LAYER_TILES + i * 4 + (off + j + 3))
                V.tensor_tensor(weight_l[:, j % 2, :], raw[:, (j + 2) % 4, :], weight_h[:, j % 2, :].bitcast(F32), ALU.subtract).then_inc(l_split, 1)

            def done(lay, off, i, j):
                dve.wait_ge(tile_done, lay * LAYER_TILES + i * 4 + (off + j + 1))

            def copied(lay, off, i, j):
                dve.wait_ge(acc_free, lay * LAYER_TILES + i * 4 + (off + j + 3))

            def norm(lay, which, scale, shift_at):
                n = lay * 2 + which
                std, rstd = qk[:, 2, :], qk[:, 3, :]
                rv = rstd.rearrange("p (a b) -> p a b", a=2)
                dve.wait_ge(std_ready, n + 1)
                V.reciprocal(rstd, std).then_inc(rstd_ready, 1)
                dve.wait_ge(rstd_ready, n + 1)
                carry(dve)

                def normed(m, base):
                    ch = Chain(dve, xn_chain, base)
                    ch.link(V.tensor_tensor(one(tmp, m), one(x, m), rv, ALU.mult))
                    xs = one(tmp, m)[:, :, HALF_P:HALF].rearrange("p a (b t) -> p a b t", t=DS)
                    hs = one(mix, m)[:, :, HALF_P:HALF].rearrange("p a (b t) -> p a b t", t=DS)
                    sc = scale[:, bass.ds(m, 1), 1:GROUPS].rearrange("p o (a b) -> p (o a) b", a=2).unsqueeze(3).to_broadcast([128, 2, 4, DS])
                    sh = ada[:, bass.ds(m + shift_at, 1), 1:GROUPS].rearrange("p o (a b) -> p (o a) b", a=2).unsqueeze(3).to_broadcast([128, 2, 4, DS])
                    ch.link(V.tensor_tensor(xs, xs, sc, ALU.mult))
                    V.tensor_tensor(hs, xs, sh, ALU.add).then_inc(xn_ready, 1)

                with dve.Fori(0, KT) as m:
                    normed(m, n * 16 + m * 2)

            with dve.Fori(0, DEPTH) as lay:
                dve.wait_ge(x_mlp, lay * 32 + 1)
                carry(dve)

                def gains(scale, seg, g_at):
                    gb = small[:, bass.ds(lay, 1), g_at:g_at + KT].rearrange("p o k -> p (o k)").unsqueeze(2).to_broadcast([128, KT, GROUPS])
                    V.scalar_tensor_tensor(scale[:], ada[:, seg * KT:(seg + 1) * KT, :], 1.0, gb, ALU.add, ALU.mult).then_inc(scales_ready, 1)

                dve.wait_ge(ada_ready, lay * ADA_GROUPS + 4 + 2)
                gains(scale1, 1, S_G1)
                dve.wait_ge(scales_ready, lay * 2 + 1)
                norm(lay, 0, scale1, 0)

                for off, factor in ((AT_Q, 1.0), (AT_K, DK ** -0.5)):
                    for j in range(4):
                        split_l(lay, off, 0, j)
                        done(lay, off, 0, j)
                        a = acc[j % 2][:, :, 0:HALF]
                        c0 = 4 * (j % 2)
                        t1, t2 = (o_t[:, c0 + q, :].rearrange("p (a b) -> p a b", a=2) for q in range(2))
                        dve.wait_ge(qk_ready, lay * 8 + max(off - AT_Q + j - 1, 0) + 1)
                        V.scalar_tensor_tensor(t1, a, factor, cos, ALU.mult, ALU.mult)
                        V.scalar_tensor_tensor(t2[0:64], a[64:128], factor, sin[64:128], ALU.mult, ALU.mult)
                        V.scalar_tensor_tensor(t2[64:128], a[0:64], factor, sin[0:64], ALU.mult, ALU.mult).then_inc(acc_free, 1)
                        copied(lay, off, 0, j)
                        V.tensor_tensor(qk[:, off - AT_Q + j, :], o_t[:, c0, :], o_t[:, c0 + 1, :], ALU.add).then_inc(qk_ready, 1)

                with dve.Fori(0, 2) as i:
                    for j in range(4):
                        done(lay, AT_V, i, j)
                        dst = o_t[:, 2 + j % 2, :]
                        V.tensor_copy(dst[:, 0:SEQ].rearrange("p (a b) -> p a b", a=2), prompt(acc[j % 2]))
                        V.tensor_copy(dst[:, SEQ:TOK].rearrange("p (a b) -> p a b", a=2), sample(acc[j % 2])).then_inc(acc_free, 1)
                        split_l(lay, AT_V, i, j)

                with dve.Fori(0, 2) as i:
                    dve.wait_ge(ret_p_stored, lay * 32 + i * 16 + 1)
                    V.memset(s_p[:], 0.0)
                    for c in range(4):
                        n = lay * 8 + i * 4 + c
                        dve.wait_ge(scores_ready, n + 1)
                        for e in range(2):
                            h = i * 2 + e
                            V.tensor_tensor(p_m[:, e, :], misc[:, 0, e * 256:e * 256 + 128], mask[:, bass.ds(h, 1), :].rearrange("p o t -> p (o t)"), ALU.mult)
                            last = V.tensor_scalar(kd_p[:, e, :], misc[:, 0, e * 256 + 128:e * 256 + 256], kdec[:, bass.ds(h, 1)], None, ALU.mult)
                        last.then_inc(masked_ready, 1)
                        done(lay, AT_MA, i, c)
                        V.tensor_copy(one(mix, i * 4 + c), acc[c % 2][:, :, 0:HALF]).then_inc(acc_free, 1)
                        split_l(lay, AT_MA, i, c)
                        dve.wait_ge(o_ready, n + 1 + 1)
                        for e in range(2):
                            last = V.scalar_tensor_tensor(s_p[:, e, :], s_p[:, e, :], cdec[:, bass.ds(i * 2 + e, 1)], misc[:, 2, e * 256:e * 256 + 256], ALU.mult, ALU.add)
                        last.then_inc(s_ready, 1)
                        ch = Chain(dve, norm_chain, n * 2)
                        V.bn_stats(bst[:, 0, :], misc[:, 1, 0:256])
                        ch.link(V.bn_stats(bst[:, 1, :], misc[:, 1, 256:512]), carry)
                        V.bn_aggr(mv[:, 0, :], bst[:, 0, :])
                        V.bn_aggr(mv[:, 1, :], bst[:, 1, :]).then_inc(mv_ready, 1)
                        dve.wait_ge(gstd_ready, n + 1)
                        ch.link(V.reciprocal(grs[:], gstd[:]))
                        for e in range(2):
                            last = V.tensor_scalar(on_p[:, e, :], misc[:, 1, e * 256:e * 256 + 256], mv[:, e, 0:1], grs[:, e:e + 1], ALU.subtract, ALU.mult)
                        last.then_inc(on_ready, 1)

                with dve.Fori(0, 2) as i:
                    for j in range(4):
                        e = j // 2
                        h, m = i * 2 + e, i * 4 + j
                        n = lay * 4 + i * 2 + e
                        o = misc[0:NB_S, 1, 0:DV]
                        if j % 2 == 0:
                            dve.wait_ge(s_scores_ready, n + 1)
                            V.tensor_tensor(p_ms[0:NB_S, 0:NB_S], misc[0:NB_S, 0, 0:NB_S], mask_s[:, bass.ds(h, 1), :].rearrange("p o t -> p (o t)"), ALU.mult)
                        kt = misc[0:NB_S, 0, 128:256].unsqueeze(1).to_broadcast([NB_S, DB // 2, DK])
                        km = kdm[:, bass.ds(h, 1), 4 * (j % 2):4 * (j % 2) + 4].rearrange("p o b -> p (o b)").unsqueeze(2).to_broadcast([NB_S, DB // 2, DK])
                        V.tensor_tensor(kd_s[0:NB_S], kt, km, ALU.mult).then_inc(s_masked_ready, 1)
                        split_l(lay, AT_G, i, j)
                        dve.wait_ge(g_sig, lay * 8 + i * 4 + (j + 1))
                        V.tensor_tensor(one(tmp, m), acc[j % 2][:, :, 0:HALF], one(tmp, m), ALU.mult).then_inc(acc_free, 1)
                        ch = Chain(dve, s_chain, n * 2)
                        if j % 2 == 0:
                            dve.wait_ge(s_o_ready, n + 1 + 1)
                            ch.link(V.bn_stats(bst[0:NB_S, 0, :], o), carry)
                            V.bn_aggr(mv[0:NB_S, 0, :], bst[0:NB_S, 0, :]).then_inc(s_mv_ready, 1)
                        for pair in (0, 1) if j % 2 == 0 else (2, 3):
                            dve.wait_ge(s_update_ready, n * 4 + (pair + 1))
                            s = s_s[:, e, 2 * pair:2 * pair + 2, :].rearrange("p b n -> p (b n)")
                            V.scalar_tensor_tensor(s, s, cdec_s[:, bass.ds(h, 1)], misc[:, 2 + pair % 2, :], ALU.mult, ALU.add).then_inc(s_state_ready, 1)
                        if j % 2 == 0:
                            dve.wait_ge(s_gstd_ready, n + 1)
                            ch.link(V.reciprocal(grs[0:NB_S, 0:1], gstd[0:NB_S, 0:1]))
                            V.tensor_scalar(on_s[0:NB_S], o, mv[0:NB_S, 0, 0:1], grs[0:NB_S, 0:1], ALU.subtract, ALU.mult).then_inc(s_on_ready, 1)

                with dve.Fori(0, 2) as i:
                    for j in range(4):
                        n, m = lay * 8 + i * 4 + j, i * 4 + j
                        a = acc[j % 2][:, :, 0:HALF]
                        pad = side[:, j % 2, 0:515]
                        flat_s = side[:, j % 2, 516:604]
                        pad_s = flat_s.rearrange("p (b t) -> p b t", t=11)
                        cs = side[:, j % 2, 604:668]
                        w = lambda k: small[:, bass.ds(lay, 1), bass.ds(m + (S_CW + 8 * k), 1)].rearrange("p o q -> p (o q)")
                        bcol = small[:, bass.ds(lay, 1), bass.ds(m + S_CB, 1)].rearrange("p o q -> p (o q)")
                        split_l(lay, AT_XL, i, j)
                        done(lay, AT_XL, i, j)
                        dve.wait_ge(conv_kept, lay * 8 + i * 4 + max(j - 1, 0) + 1)
                        V.memset(pad[:, 0:3], 0.0)
                        V.tensor_copy(pad_s[:, :, 0:3], conv0[:, bass.ds(lay * 8 + m, 1)].rearrange("p o b t -> p (o b) t"))
                        V.tensor_copy(pad[:, 3:515].rearrange("p (a b) -> p a b", a=2), prompt(a))
                        V.tensor_copy(flat_s.rearrange("p (a b t) -> p a b t", a=2, t=11)[:, :, :, 3:11], sample(a).rearrange("p a (b t) -> p a b t", t=DS)).then_inc(acc_free, 1)
                        copied(lay, AT_XL, i, j)
                        ch = Chain(dve, conv_chain, n * 4)
                        out = prompt(one(qk, m))
                        win = lambda k: pad[:, k:k + 512].rearrange("p (a b) -> p a b", a=2)
                        csv = cs.rearrange("p (b t) -> p b t", t=DS)
                        V.tensor_scalar(out, win(0), w(0), bcol, ALU.mult, ALU.add)
                        ch.link(V.tensor_scalar(csv, pad_s[:, :, 0:8], w(0), bcol, ALU.mult, ALU.add))
                        for k in range(1, 4):
                            V.scalar_tensor_tensor(out, win(k), w(k), out, ALU.mult, ALU.add)
                            ch.link(V.scalar_tensor_tensor(csv, pad_s[:, :, k:k + 8], w(k), csv, ALU.mult, ALU.add))
                        V.tensor_copy(sample(one(qk, m)), cs.rearrange("p (a b) -> p a b", a=2))
                        V.tensor_copy(conv_c[:, bass.ds(lay * 8 + m, 1), 0, :].rearrange("p o t -> p (o t)"), pad[:, 512:515])
                        V.tensor_copy(conv_c[:, bass.ds(lay * 8 + m, 1), 1:GROUPS, :].rearrange("p o b t -> p (o b) t"), pad_s[:, :, 8:11]).then_inc(conv_kept, 1)

                def lru_first(m, slot):
                    n = lay * 8 + m
                    t0, t1, t2, t3 = (tmp[:, q, :] for q in (4, 5 + slot, 6 - slot, 7))
                    t1v = t1.rearrange("p (a b) -> p a b", a=2)
                    dve.wait_ge(gates_read, n + 1 + 1)
                    V.tensor_scalar(t0, t0, 0.5, 0.5, ALU.mult, ALU.add).then_inc(r_ready, 1)
                    V.scalar_tensor_tensor(t1v, t1v, 1.0, one(qk, m), ALU.add, ALU.mult)
                    dve.wait_ge(a_ready, n + 1)
                    Chain(dve, lru_chain, n * 5).link(V.tensor_tensor(t0, t3, t3, ALU.mult))
                    V.scalar_tensor_tensor(t0, t0, 1.0, t2, ALU.add, ALU.mult).then_inc(e_ready, 1)

                def lru_rest(m, slot, gelus, at_slot):
                    n = lay * 8 + m
                    t0, t1, t3 = (tmp[:, q, :] for q in (4, 5 + slot, 7))
                    a, u = (v.rearrange("p (a b) -> p a b", a=2) for v in (t3, t1))
                    h = one(qk, m)
                    ch = Chain(dve, lru_chain, n * 5 + 1)
                    dve.wait_ge(e_root, n + 1)
                    V.tensor_tensor(t1, t1, t0, ALU.mult).then_inc(lru_u_ready, 1)
                    first = lambda b: sample(b).rearrange("p a (b t) -> p a b t", t=DS)[:, :, :, 0]
                    hz = bst[:, :, 0:4]
                    ch.link(V.tensor_tensor(hz, first(a), h0[:, bass.ds(lay * 8 + m, 1), :].rearrange("p o (a b) -> p (o a) b", a=2), ALU.mult))
                    V.memset(first(a), 0.0)
                    ch.link(V.tensor_tensor(first(u), first(u), hz, ALU.add))
                    ch.link(V.tensor_tensor_scan(h[:, 0, 0:HALF_P], a[:, 0, 0:HALF_P], u[:, 0, 0:HALF_P], 0.0, ALU.mult, ALU.add))
                    V.tensor_tensor_scan(h[:, 1, 0:HALF_P], a[:, 1, 0:HALF_P], u[:, 1, 0:HALF_P], h[:, 0, HALF_P - 1:HALF_P], ALU.mult, ALU.add)
                    for q in range(2):
                        last = V.tensor_tensor_scan(h[:, q, HALF_P:HALF], a[:, q, HALF_P:HALF], u[:, q, HALF_P:HALF], 0.0, ALU.mult, ALU.add)
                    ch.link(last)
                    V.tensor_copy(lru_c[:, bass.ds(lay * 8 + m, 1), 0:1].rearrange("p o q -> p (o q)"), h[:, 1, HALF_P - 1:HALF_P])
                    V.tensor_copy(lru_c[:, bass.ds(lay * 8 + m, 1), 1:GROUPS].rearrange("p o (a b) -> p (o a) b", a=2),
                                  sample(h).rearrange("p a (b t) -> p a b t", t=DS)[:, :, :, DS - 1]).then_inc(scans_done, 1)
                    dve.wait_ge(scans_done, n + 1 + 1)
                    dve.wait_ge(gelu_ready, gelus + 1)
                    V.scalar_tensor_tensor(h, one(tmp, at_slot), 0.5, h, ALU.mult, ALU.mult).then_inc(y_ready, 1)

                def gelu(t):
                    dve.wait_ge(gelu_tanh, lay * 8 + (t + 1))
                    V.scalar_tensor_tensor(tmp[:, t % 4, :], side[:, t % 2, 0:TOK], 1.0, tmp[:, t % 4, :], ALU.add, ALU.mult).then_inc(gelu_ready, 1)

                def lru_step(t):
                    if t % 2 == 0:
                        lru_first(zero + t // 2, t // 2 % 2)
                    else:
                        lru_rest(zero + t // 2, t // 2 % 2, lay * 8 + (t // 2 + 1), zero + t // 2 % 4)

                zero = lay * 0
                for t in range(16):
                    done(lay, AT_GL, zero, t)
                    if t == 7:
                        split_l(lay, AT_GL, zero, t)
                        gelu(t - 1)
                        lru_step(t)
                    if t < 8:
                        dve.wait_ge(y_ready, lay * 8 + (t // 2 + t // 7) + 1)
                        V.tensor_copy(tmp[:, t % 4, :].rearrange("p (a b) -> p a b", a=2), acc[t % 2][:, :, 0:HALF]).then_inc(acc_free, 1)
                    else:
                        dve.wait_ge(ma_ready, lay * 8 + 8)
                        V.tensor_tensor(one(mix, zero + t - 8), acc[t % 2][:, :, 0:HALF], one(mix, zero + t - 8), ALU.mult).then_inc(acc_free, 1)
                    if t != 7:
                        split_l(lay, AT_GL, zero, t)
                        if 0 < t < 8 or t == 9:
                            gelu(min(t - 1, 7))
                        lru_step(t)

                with dve.Fori(0, 2) as i:
                    for j in range(4):
                        n, m = lay * 8 + i * 4 + j, i * 4 + j
                        split_l(lay, AT_MB, i, j)
                        dve.wait_ge(mb_sig, n + 1)
                        dve.wait_ge(y_rounded, n + 1)
                        V.tensor_tensor(one(b_lo, m), one(qk, m), one(b_hi, m).bitcast(F32), ALU.subtract).then_inc(acc_free, 1)

                def merge(i, j):
                    m = i * 4 + j
                    done(lay, AT_LRU, i, j)
                    V.tensor_tensor(one(tmp, m), acc[j % 2][:, :, 0:HALF], one(tmp, m), ALU.mult).then_inc(acc_free, 1)
                    copied(lay, AT_LRU, i, j)
                    V.tensor_tensor(one(mix, m), one(mix, m), one(tmp, m), ALU.add).then_inc(m_ready, 1)

                def split_merged(m):
                    dve.wait_ge(m_rounded, lay * 8 + m + 1)
                    V.tensor_tensor(one(b_lo, zero + m), one(mix, zero + m), one(b_hi, zero + m).bitcast(F32), ALU.subtract).then_inc(m_split, 1)

                with dve.Fori(0, 1) as i:
                    for j in range(4):
                        merge(i, j)
                        split_l(lay, AT_LRU, i, j)
                zero = lay * 0
                for j in range(4):
                    merge(zero + 1, j)
                    if j < 3:
                        split_l(lay, AT_LRU + 4, zero, j)
                for m in range(KT):
                    split_merged(m)
                split_l(lay, AT_LRU + 4, zero, 3)

                def gated_add(j, m, gate_at, base, signal, left):
                    dve.wait_ge(signal, left + 1)
                    a = acc[j % 2][:, :, 0:HALF]
                    gate = ada[:, bass.ds(m + gate_at, 1), 0:1].rearrange("p o q -> p (o q)")
                    gs = ada[:, bass.ds(m + gate_at, 1), 1:GROUPS].rearrange("p o (a b) -> p (o a) b", a=2).unsqueeze(3).to_broadcast([128, 2, 4, DS])
                    V.scalar_tensor_tensor(prompt(one(x, m)), prompt(a), gate, prompt(one(x, m)), ALU.mult, ALU.add)
                    ts = tmp[:, 4 + j % 2, 0:64]
                    V.tensor_tensor(ts.rearrange("p (a b t) -> p a b t", a=2, t=DS), sample(a).rearrange("p a (b t) -> p a b t", t=DS), gs, ALU.mult).then_inc(acc_free, 1)
                    base()
                    xs = sample(one(x, m))
                    V.tensor_tensor(xs, xs, ts.rearrange("p (a b) -> p a b", a=2), ALU.add).then_inc(signal, 1)

                with dve.Fori(0, 2) as i:
                    for j in range(4):
                        done(lay, AT_OUT, i, j)
                        gated_add(j, i * 4 + j, 2 * KT, lambda: copied(lay, AT_OUT, i, j), x_mixed, lay * 8 + i * 4 + max(j - 1, 0))
                        split_l(lay, AT_OUT, i, j)
                dve.wait_ge(ada_ready, lay * ADA_GROUPS + ADA_FIRST + 2)
                gains(scale2, 4, S_G2)
                dve.wait_ge(scales_ready, lay * 2 + 2)
                norm(lay, 1, scale2, 3 * KT)
                with dve.Fori(0, QUARTERS) as qt:
                    with dve.Fori(0, 2) as i:
                        for j in range(4):
                            n, m = lay * 32 + qt * 8 + i * 4 + j, i * 4 + j
                            done(lay, AT_MLP, qt * 4 + i, j)
                            V.tensor_scalar(tmp[:, j % 2, :].rearrange("p (a b) -> p a b", a=2), acc[j % 2][:, :, 0:HALF], 0.0, None, ALU.max).then_inc(acc_free, 1)
                            split_l(lay, AT_MLP, qt * 4 + i, j)
                            dve.wait_ge(u_rounded, n + 1)
                            V.tensor_tensor(one(b_lo, m), tmp[:, 2 + j % 2, :].rearrange("p (a b) -> p a b", a=2), one(b_hi, m).bitcast(F32), ALU.subtract).then_inc(u_split, 1)
                    dve.wait_ge(squares_ready, lay * 5 + qt + 2)
                    carry(dve)
                    with dve.Fori(0, 2) as i:
                        for j in range(4):
                            done(lay, AT_MLP + 8, qt * 4 + i, j)
                            dve.wait_ge(ada_ready, lay * ADA_GROUPS + ADA_GROUPS + 2)
                            gated_add(j, i * 4 + j, 5 * KT, lambda: copied(lay, AT_MLP + 8, qt * 4 + i, j), x_mlp,
                                      lay * 32 + qt * 8 + i * 4 + max(j - 1, 0))
                            split_l(lay, AT_MLP + 8, qt * 4 + i, j)

            dve.wait_ge(std_ready, 2 * DEPTH + 1)
            V.reciprocal(qk[:, 3, :], qk[:, 2, :]).then_inc(rstd_ready, 1)
            dve.wait_ge(rstd_ready, 2 * DEPTH + 1)
            with dve.Fori(0, KT) as m:
                flat = lambda b: b[:, bass.ds(m, 1), :].rearrange("p o n -> p (o n)")
                V.scalar_tensor_tensor(flat(tmp), flat(x), fg[:, bass.ds(m, 1)], qk[:, 3, :], ALU.mult, ALU.mult).then_inc(y_done, 1)

        @block.gpsimd
        def _(pool):
            G = nc.gpsimd

            def sum_squares(wait, chain):
                with pool.Fori(0, KT) as m:
                    wait(m)
                    flat = x[:, bass.ds(m, 1), :].rearrange("p o n -> p (o n)")
                    G.tensor_tensor(qk[:, 1, :], flat, flat, ALU.mult).then_inc(square_chain, 1)
                    pool.wait_ge(square_chain, chain + m * 2 + 1)
                    G.tensor_tensor(qk[:, 0, :], qk[:, 0, :], qk[:, 1, :], ALU.add).then_inc(square_chain, 1)
                    pool.wait_ge(square_chain, chain + m * 2 + 2)
                pool.sem_inc(squares_ready, 1)

            def add_bias(n, at_q, g):
                pool.wait_ge(ada_out_ready, n + 1)
                bias = small[:, bass.ds(lay, 1), bass.ds(at_q, 4)].rearrange("p o q -> p (o q)").unsqueeze(2).to_broadcast([128, 4, GROUPS])
                G.tensor_tensor(ada[:, bass.ds(at_q, 4), :], ada_sum[:, g], bias, ALU.add).then_inc(ada_ready, 1)

            def add_biases(first, groups):
                with pool.Fori(0, groups // 2) as i:
                    for g in range(2):
                        add_bias(lay * ADA_GROUPS + i * 2 + (first + g), i * 8 + (first + g) * 4, g)

            def lower(which, m):
                pool.wait_ge(h_rounded, lay * 16 + (which * KT + 1) + m)
                carry(pool)
                G.tensor_tensor(one(h_lo, m), one(mix, m), one(h_hi, m).bitcast(F32), ALU.subtract).then_inc(h_ready, 1)

            pool.sem_inc(ada_ready, 2)
            for one_more in start_at_1["pool"]:
                pool.sem_inc(one_more, 1)
            pool.wait_ge(params_loaded, 16 * 4)
            pool.wait_ge(small_loaded, 16)
            pool.wait_ge(const_loaded, 16)
            with pool.Fori(0, DEPTH) as lay:
                add_biases(0, 4)
                with pool.Fori(0, 2) as i:
                    for g in range(2):
                        for j in range(2):
                            lower(0, i * 4 + (g * 2 + j))
                        add_bias(lay * ADA_GROUPS + i * 2 + (4 + g), i * 8 + (4 + g) * 4, g)
                add_biases(8, ADA_FIRST - 8)
                with pool.Fori(0, 2) as i:
                    for c in range(4):
                        n = lay * 8 + i * 4 + c
                        pool.wait_ge(qk_ready, lay * 8 + 8 + 1)
                        pool.wait_ge(o_ready, lay * 8 + i * 4 + max(c - 1, 0) + 1)
                        cols = slice((c // 2) * HALF + (c % 2) * CHUNK, (c // 2) * HALF + (c % 2) * CHUNK + CHUNK)
                        for e in range(2):
                            h = i * 2 + e
                            G.tensor_copy(k_st[:, c % 2, e, :], qk[:, bass.ds(h + 4, 1), cols].rearrange("p o t -> p (o t)"))
                            last = G.tensor_tensor(q_st[:, c % 2, e, :], qk[:, bass.ds(h, 1), cols].rearrange("p o t -> p (o t)"),
                                                   qdec[:, bass.ds(h, 1), 0:CHUNK].rearrange("p o t -> p (o t)"), ALU.mult)
                        last.then_inc(stage_ready, 1)
                with pool.Fori(0, 4) as h:
                    n = lay * 4 + h
                    pool.wait_ge(s_o_ready, n + 1)
                    G.tensor_copy(k_ss[:].rearrange("p (a b) -> p a b", a=2), sample(one(qk, h + 4)))
                    dst = q_sm[:].rearrange("p (a b s) -> p a b s", a=2, s=72)[:, :, :, 0:DS]
                    src = sample(one(qk, h)).rearrange("p a (b t) -> p a b t", t=DS)
                    for a in range(2):
                        dec = qdec[:, bass.ds(h, 1), CHUNK:CHUNK + DS].to_broadcast([128, 4, DS])
                        last = G.tensor_tensor(dst[:, a], src[:, a], dec, ALU.mult)
                    last.then_inc(s_stage_ready, 1)
                with pool.Fori(0, KT) as m:
                    n = lay * 8 + m
                    pool.wait_ge(s_o_t_ready, lay * 4 + 4 + 1)
                    pool.wait_ge(acc_free, lay * LAYER_TILES + (AT_XL + 2))
                    G.tensor_tensor(one(tmp, m), one(tmp, m), one(o_t, m), ALU.mult).then_inc(g_gated, 1)
                    pool.wait_ge(g_rounded, n + 1)
                    carry(pool)
                    G.tensor_tensor(one(b_lo, m), one(tmp, m), one(b_hi, m).bitcast(F32), ALU.subtract).then_inc(o_split, 1)
                with pool.Fori(0, 2) as i:
                    for j in range(4):
                        n = lay * 8 + i * 4 + j
                        arg, g = side[:, j % 2, 0:TOK], tmp[:, j, :]
                        pool.wait_ge(acc_free, lay * LAYER_TILES + i * 4 + (AT_GL + j + 3))
                        pool.wait_ge(gelu_ready, lay * 8 + i * 4 + max(j - 1, 0) + 1)
                        pool.wait_ge(conv_kept, lay * 8 + 8 + 1)
                        G.tensor_tensor(arg, g, g, ALU.mult).then_inc(cube_chain, 1)
                        pool.wait_ge(cube_chain, n * 2 + 1)
                        carry(pool)
                        G.tensor_scalar(arg, arg, 0.044715, 1.0, ALU.mult, ALU.add).then_inc(cube_chain, 1)
                        pool.wait_ge(cube_chain, n * 2 + 2)
                        G.tensor_tensor(arg, arg, g, ALU.mult).then_inc(cube_ready, 1)
                base = lay * (5 * 17)
                pool.wait_ge(acc_free, lay * LAYER_TILES + (AT_LRU + 2))
                carry(pool)
                G.memset(qk[:, 0, :], 0.0).then_inc(square_chain, 1)
                pool.wait_ge(square_chain, base + 1)
                carry(pool)
                sum_squares(lambda m: pool.wait_ge(x_mixed, lay * 8 + m + 1 + 1), base + 1)
                n_ada = lay * ADA_GROUPS + ADA_FIRST
                zero = lay * 0
                add_bias(n_ada, zero + ADA_FIRST * 4, 0)
                for m in range(KT):
                    lower(1, zero + m)
                    if m == 4:
                        add_bias(n_ada + 1, zero + (ADA_FIRST + 1) * 4, 1)
                with pool.Fori(0, QUARTERS) as qt:
                    with pool.Fori(0, 4) as i:
                        for j in range(2):
                            n = lay * 32 + qt * 8 + i * 2 + j
                            pool.wait_ge(acc_free, lay * LAYER_TILES + qt * 16 + i * 2 + (AT_MLP + j + 3))
                            G.tensor_tensor(tmp[:, 2 + j, :], tmp[:, j, :], tmp[:, j, :], ALU.mult).then_inc(u_ready, 1)
                    qbase = base + 17 + qt * 17
                    pool.wait_ge(mean_ready, lay * 2 + 2)
                    carry(pool)
                    G.memset(qk[:, 0, :], 0.0).then_inc(square_chain, 1)
                    pool.wait_ge(square_chain, qbase + 1)
                    carry(pool)
                    sum_squares(lambda m: pool.wait_ge(x_mlp, lay * 32 + qt * 8 + m + 1 + 1), qbase + 1)

        @block.tensor
        def _(pe):
            M = nc.tensor.matmul
            pe.sem_inc(ada_used, 4)
            for one_more in start_at_1["pe"]:
                pe.sem_inc(one_more, 1)

            def stream_tile(lay, off, i, j, rhs_hi, rhs_lo, ready=None):
                pe.wait_ge(l_split, lay * LAYER_TILES + i * 4 + (off + j + 1))
                pe.wait_ge(acc_free, lay * LAYER_TILES + i * 4 + (off + j + 1))
                for k in range(KT):
                    if ready is not None:
                        ready(k)
                    wh = weight_h[:, j % 2, k * 128:(k + 1) * 128]
                    wl = weight_l[:, j % 2, k * 128:(k + 1) * 128]
                    for n, (w, r) in enumerate(((wh, rhs_hi), (wh, rhs_lo), (wl, rhs_hi))):
                        for half in range(2):
                            last = M(acc[j % 2][:, half, 0:HALF], w, r[:, k, half * HALF:(half + 1) * HALF], start=(k == 0 and n == 0), stop=(k == KT - 1 and n == 2))
                last.then_inc(tile_done, 1)

            def plain(lay, off, rhs_hi, rhs_lo, ready=None):
                with pe.Fori(0, 2) as i:
                    for j in range(4):
                        stream_tile(lay, off, i, j, rhs_hi, rhs_lo, ready if j == 0 else None)

            def mean_square(n):
                pe.wait_ge(squares_ready, n)
                for half in range(2):
                    last = M(misc[:, half, 0:HALF], mean_w, qk[:, 0, half * HALF:(half + 1) * HALF], start=True, stop=True)
                last.then_inc(mean_ready, 1)

            pe.wait_ge(setup_dve, 1)
            with pe.Fori(0, DEPTH) as lay:
                def ada_group(n, g, between=None):
                    pe.wait_ge(ada_ready, n + 1)
                    for j in range(4):
                        pe.wait_ge(ada_loaded[j], n * 16 + 16)
                        for kk in range(2):
                            k = 2 * j + kk
                            last = M(misc[0:GROUPS, 2 + g, :], c_act[:, k * GROUPS:(k + 1) * GROUPS], ada_raw[j][:, kk * 512:(kk + 1) * 512], start=(k == 0), stop=(k == KT - 1))
                        last.then_inc(ada_used, 1)
                        if j == 0 and between is not None:
                            between()

                def ada_groups(first, groups):
                    with pe.Fori(0, groups // 2) as i:
                        n = lay * ADA_GROUPS + i * 2 + first
                        ada_group(n, 0)
                        ada_group(n + 1, 1, lambda: turn(n, 0))
                        turn(n + 1, 1)

                def turn(n, g):
                    pe.wait_ge(ada_copied, n + 1)
                    pe.wait_ge(const_loaded, 16)
                    for q in range(4):
                        last = M(misc[:, 2 + g, q * 96:(q + 1) * 96], ada_row[0:GROUPS, q * 128:(q + 1) * 128], ident[0:GROUPS, 0:96], start=True, stop=True)
                    last.then_inc(ada_turned, 1)

                ada_groups(0, 4)
                mean_square(lay * 5 + 1)
                ada_groups(4, ADA_FIRST - 4)
                h_parts = lambda k: pe.wait_ge(h_ready, lay * 16 + (k + 1))
                for off in (AT_Q, AT_K):
                    for j in range(4):
                        stream_tile(lay, off, 0, j, h_hi, h_lo, h_parts if off == AT_Q and j == 0 else None)

                def turn_v(n, j):
                    pe.wait_ge(acc_free, n[0] + (j + 3))
                    pe.wait_ge(v_ready, n[1] + j + 1)
                    src = o_t[:, 2 + j % 2, :]
                    for c in range(4):
                        nc.tensor.transpose(misc[:, 0, c * 128:(c + 1) * 128], src[:, c * 128:(c + 1) * 128], ident)
                    nc.tensor.transpose(misc[0:NB_S, 1, 0:128], src[:, SEQ:TOK], ident).then_inc(v_turned, 1)

                with pe.Fori(0, 2) as i:
                    n = (lay * LAYER_TILES + i * 4 + (AT_V), lay * 8 + i * 4)
                    for j in range(4):
                        stream_tile(lay, AT_V, i, j, h_hi, h_lo)
                        if j:
                            turn_v(n, j - 1)
                    turn_v(n, 3)

                def turn_o(n):
                    pe.wait_ge(on_ready, n + 1)
                    pe.wait_ge(o_t_ready, n + 1)
                    for e in range(2):
                        for half in range(2):
                            last = nc.tensor.transpose(misc[:, 3, (2 * e + half) * 128:(2 * e + half + 1) * 128], on_p[:, e, half * 128:(half + 1) * 128], ident)
                    last.then_inc(on_turned, 1)

                pe.wait_ge(v_ready, lay * 8 + 8 + 1)
                carry(pe)
                for i in range(2):
                    for c in range(4):
                        n = lay * 8 + (i * 4 + c)
                        pe.wait_ge(stage_ready, n + 1)
                        for e in range(2):
                            qc = qk[:, bass.ds(lay * 0 + (i * 2 + e), 1), (c // 2) * HALF + (c % 2) * CHUNK:(c // 2) * HALF + (c % 2) * CHUNK + CHUNK].rearrange("p o t -> p (o t)")
                            M(misc[:, 0, e * 256:e * 256 + 128], k_st[:, c % 2, e, :], qc, start=True, stop=True)
                            last = nc.tensor.transpose(misc[:, 0, e * 256 + 128:e * 256 + 256], k_st[:, c % 2, e, :], ident)
                        last.then_inc(scores_ready, 1)
                        stream_tile(lay, AT_MA, lay * 0, 4 * i + c, h_hi, h_lo)
                        if i or c:
                            turn_o(lay * 8 + (i * 4 + c - 1))
                        pe.wait_ge(masked_ready, n + 1)
                        pe.wait_ge(s_ready, n + 1)
                        for e in range(2):
                            v = v_tok[:, c, bass.ds(lay * 0 + (i * 512 + e * 256), 256)]
                            M(misc[:, 1, e * 256:e * 256 + 256], p_m[:, e, :], v, start=True, stop=False)
                            M(misc[:, 1, e * 256:e * 256 + 256], q_st[:, c % 2, e, :], s_p[:, e, :], start=False, stop=True)
                            last = M(misc[:, 2, e * 256:e * 256 + 256], kd_p[:, e, :], v, start=True, stop=True)
                        last.then_inc(o_ready, 1)
                turn_o(n)

                def sample_scores(n, h):
                    pe.wait_ge(s_stage_ready, n + 1)
                    pe.wait_ge(o_t_ready, lay * 8 + 8 + 1)
                    M(misc[0:NB_S, 0, 0:NB_S], k_ss[:], sample(one(qk, h)), start=True, stop=True)
                    nc.tensor.transpose(misc[0:NB_S, 0, 128:256], k_ss[:], ident).then_inc(s_scores_ready, 1)

                def sample_o(n, v):
                    pe.wait_ge(s_masked_ready, n * 2 + 1)
                    pe.wait_ge(s_o_t_ready, n + 1)
                    carry(pe)
                    o = misc[:, 1, 0:DV]
                    M(o, p_ms[0:NB_S, :], v, start=True, stop=False)
                    for b in range(DB):
                        last = M(o, q_sm[:, b * 64:b * 64 + 128], s_s[:, e, b, :], start=False, stop=(b == DB - 1))
                    last.then_inc(s_o_ready, 1)

                def sample_updates(n, pairs, v):
                    for pair in pairs:
                        if pair > 1:
                            pe.wait_ge(s_state_ready, n * 4 + (pair - 1))
                            carry(pe)
                        for b in range(2):
                            last = M(misc[:, 2 + pair % 2, b * 256:(b + 1) * 256], kd_s[0:NB_S, 2 * (pair % 2) + b, :], v, start=True, stop=True)
                        last.then_inc(s_update_ready, 1)

                with pe.Fori(0, 2) as i:
                    for j in range(4):
                        e = j // 2
                        n = lay * 4 + i * 2 + e
                        v = v_s[0:NB_S, bass.ds(i * 512 + e * 256, 256)]
                        if j % 2 == 0:
                            sample_scores(n, i * 2 + e)
                        stream_tile(lay, AT_G, i, j, h_hi, h_lo)
                        if j % 2 == 0:
                            pe.wait_ge(state_loaded[e], lay * 32 + i * 16 + 16)
                            sample_o(n, v)
                            sample_updates(n, (0, 1), v)
                        else:
                            pe.wait_ge(s_masked_ready, n * 2 + 2)
                            sample_updates(n, (2, 3), v)
                            pe.wait_ge(s_on_ready, n + 1)
                            carry(pe)
                            for half in range(2):
                                last = nc.tensor.transpose(misc[:, 1, 256 + 64 * half:320 + 64 * half], on_s[0:NB_S, half * 128:(half + 1) * 128], ident[0:NB_S, 0:NB_S])
                            last.then_inc(s_turned, 1)

                b_parts = lambda s, base: (lambda k: pe.wait_ge(s, base + (k + 1)))
                plain(lay, AT_XL, h_hi, h_lo)

                def gates(m, slot, turn):
                    n = lay * 8 + m
                    if turn == 1:
                        pe.wait_ge(conv_kept, n + 1 + 1)
                    pe.wait_ge(wrg_loaded[slot], lay * 64 + i * 16 + 16 * turn)
                    pe.wait_ge(gates_read, n + 1)
                    for gate in range(2):
                        for half in range(2):
                            rhs = qk[:, bass.ds(m, 1), half * HALF:(half + 1) * HALF].rearrange("p o t -> p (o t)")
                            last = M(misc[:, 2 * gate + half, 0:HALF], wrg[:, slot, gate * 128:(gate + 1) * 128], rhs, start=True, stop=True)
                    last.then_inc(gates_ready, 1)

                pe.wait_ge(s_o_t_ready, lay * 4 + 4 + 1)
                carry(pe)
                with pe.Fori(0, 2) as i:
                    for j in range(4):
                        if j % 2 == 0:
                            gates(i * 2 + j // 2, j // 2, 1)
                        stream_tile(lay, AT_GL, i, j, h_hi, h_lo)
                with pe.Fori(0, 2) as i:
                    for j in range(4):
                        if j % 2 == 0:
                            gates(i * 2 + (4 + j // 2), j // 2, 3)
                        stream_tile(lay, AT_RET, i, j, b_hi, b_lo, b_parts(o_split, lay * 8 + 1) if j == 0 else None)
                plain(lay, AT_MB, h_hi, h_lo)
                plain(lay, AT_LRU, b_hi, b_lo, b_parts(acc_free, lay * LAYER_TILES + (AT_MB + 2)))
                plain(lay, AT_OUT, b_hi, b_lo, b_parts(m_split, lay * 8))
                n = lay * ADA_GROUPS + ADA_FIRST
                ada_group(n, 0)
                mean_square(lay * 5 + 2)
                turn(n, 0)
                ada_group(n + 1, 1)
                turn(n + 1, 1)
                h2_parts = lambda k: pe.wait_ge(h_ready, lay * 16 + (k + 9))
                with pe.Fori(0, QUARTERS) as qt:
                    with pe.Fori(0, 2) as i:
                        for j in range(4):
                            stream_tile(lay, AT_MLP, qt * 4 + i, j, h_hi, h_lo, h2_parts if j == 0 else None)
                    with pe.Fori(0, 2) as i:
                        for j in range(4):
                            stream_tile(lay, AT_MLP + 8, qt * 4 + i, j, b_hi, b_lo, b_parts(u_split, lay * 32 + qt * 8) if j == 0 else None)
            mean_square(DEPTH * 5 + 1)


def constants():
    t = np.zeros((128, NCONST), np.float32)

    def put(name, value):
        a, b = _off[name]
        value = np.asarray(value, np.float32)
        t[:value.shape[0], a:b] = value.reshape(value.shape[0], -1)

    half = DK // 2
    inv = np.float32(10000.0) ** (-np.arange(half, dtype=np.float32) / np.float32(half))
    pos_p = np.arange(SEQ, dtype=np.float32).reshape(2, HALF_P)
    pos_s = np.tile(np.float32(PAST) + np.arange(DS, dtype=np.float32), DB).reshape(2, HALF_S)
    pos = np.concatenate([pos_p, pos_s], axis=1)
    ang = (pos[None] * inv[:, None, None]).astype(np.float32).astype(np.float64)
    put("cos", np.concatenate([np.cos(ang)] * 2))
    put("sin", np.concatenate([np.sin(ang), -np.sin(ang)]))
    log_g = np.log1p(-np.exp2(-5.0 - np.arange(HEADS)))
    idx, ids = np.arange(CHUNK), np.arange(DS)
    q = np.concatenate([np.exp((idx + 1.0)[None] * log_g[:, None]), np.exp((ids + 1.0)[None] * log_g[:, None])], axis=1)
    put("qdec", np.broadcast_to(q, (128,) + q.shape))
    diff = idx[None, :] - idx[:, None]
    m = np.where(diff[:, None] >= 0, np.exp(np.maximum(diff, 0)[:, None] * log_g[None, :, None]), 0.0)
    put("mask", m)
    tok = np.arange(NB_S)
    diff = tok[None, :] - tok[:, None]
    same = (tok[None, :] // DS == tok[:, None] // DS) & (diff >= 0)
    put("mask_s", np.where(same[:, None], np.exp(np.maximum(diff, 0)[:, None] * log_g[None, :, None]), 0.0))
    own = tok[:, None] // DS == np.arange(DB)[None, :]
    put("kdm", own[:, None, :] * np.exp((DS - 1.0 - tok % DS)[:, None, None] * log_g[None, :, None]))
    put("kdec", np.exp((CHUNK - 1.0 - idx)[:, None] * log_g[None]))
    put("cdec", np.broadcast_to(np.exp(CHUNK * log_g), (128, HEADS)))
    put("cdec_s", np.broadcast_to(np.exp(DS * log_g), (128, HEADS)))
    put("ident", np.eye(128))
    put("mean", np.full((128, 128), 1.0 / DM))
    return t


def tiles(w):
    return w.reshape(KT, 128, -1, 128).transpose(2, 1, 0, 3).reshape(-1, 128, 1024)


def ada_tiles(w):
    return w.reshape(4, 2, 128, ADA_GROUPS, 512).transpose(3, 0, 2, 1, 4).reshape(-1, 128, 1024)


def per_feature(a):
    a = np.moveaxis(a, -1, 0)
    return np.ascontiguousarray(np.moveaxis(a.reshape((KT, 128) + a.shape[1:]), 0, 1))


def kernel(**inputs):
    import concourse.bacc as bacc
    from concourse.bass_utils import run_bass_kernel_spmd as run

    a = {k: np.asarray(v) for k, v in inputs.items()}
    w = []
    for l in range(DEPTH):
        z = a["w_in"][l]
        cut = lambda lo, hi: tiles(z[:, lo:hi])
        w += [cut(0, 2048), cut(5120, 6144), cut(2048, 3072), cut(3072, 4096), cut(4096, 5120),
              tiles(a["w_proj_ret"][l]), cut(6144, 7168), tiles(a["w_proj_lru"][l]), tiles(a["w_out"][l])]
        w1, w2 = tiles(a["w_mlp1"][l]), a["w_mlp2"][l]
        for q in range(QUARTERS):
            w += [w1[q * 8:(q + 1) * 8], tiles(w2[q * 1024:(q + 1) * 1024])]
    w.append(w[0][:STREAM - DEPTH * LAYER_TILES])
    w_ada = np.concatenate([ada_tiles(a["w_ada"][l]) for l in range(DEPTH)])
    stream = np.concatenate(w)

    xp = per_feature(a["x_prompt"][0]).reshape(128, KT, 2, HALF_P)
    xs = per_feature(a["x_sample"].reshape(NB_S, DM)).reshape(128, KT, 2, HALF_S)
    small = np.concatenate([
        a["b_ada"].reshape(DEPTH, 48, 128), a["norm1_g"].reshape(DEPTH, KT, 128), a["norm2_g"].reshape(DEPTH, KT, 128),
        a["conv_w"].reshape(DEPTH, DEC_W * KT, 128)] + [a[n].reshape(DEPTH, KT, 128) for n in ("conv_b", "b_rg_a", "b_rg_x", "lru_lambda")], axis=1)
    w_rg = np.concatenate([a["w_rg_a"], a["w_rg_x"]], axis=3).reshape(DEPTH * KT, 128, 256)
    arrays = {
        "stream": stream,
        "ada_in": w_ada,
        "x_in": np.ascontiguousarray(np.concatenate([xp, xs], axis=3).reshape(128, KT, TOK)),
        "c_in": np.ascontiguousarray(per_feature(np.concatenate([a["c_prompt"], a["c_sample"]])).reshape(128, KT * GROUPS)),
        "small_in": np.ascontiguousarray(small.transpose(2, 0, 1)),
        "fg_in": np.ascontiguousarray(a["final_g"].reshape(KT, 128).T),
        "h0_in": np.ascontiguousarray(a["state_lru"].reshape(DEPTH, DB, KT, 128).transpose(3, 0, 2, 1).reshape(128, DEPTH * KT, DB)),
        "conv_in": np.ascontiguousarray(a["state_conv"].reshape(DEPTH, DB, 3, KT, 128).transpose(4, 0, 3, 1, 2).reshape(128, DEPTH * KT, DB, 3)),
        "wrg_in": np.concatenate([w_rg, w_rg[:2]]),
        "state_in": a["state_ret"],
        "const_in": constants(),
    }
    outs = {
        "y_out": (128, KT, TOK), "ret_p_out": (DEPTH * HEADS, DK, DV), "lru_out": (128, DEPTH * KT, GROUPS),
        "conv_out": (128, DEPTH * KT, GROUPS, 3), "ret_s_out": (DEPTH, DB, HEADS, DK, DV),
    }
    nc = bacc.Bacc("TRN2", target_bir_lowering=False, num_devices=1)
    ins = [nc.dram_tensor(n, v.shape, F32, kind="ExternalInput").ap() for n, v in arrays.items()]
    outs_ap = [nc.dram_tensor(n, s, F32, kind="ExternalOutput").ap() for n, s in outs.items()]
    build(nc, *ins, *outs_ap)
    r = run(nc, [arrays], core_ids=[0]).results[0]

    y = np.asarray(r["y_out"]).reshape(128, KT, 2, HALF)
    rows = lambda t: t.transpose(2, 3, 1, 0).reshape(-1, DM)
    lru = np.asarray(r["lru_out"]).reshape(128, DEPTH, KT, GROUPS).transpose(1, 3, 2, 0).reshape(DEPTH, GROUPS, DM)
    conv = np.asarray(r["conv_out"]).reshape(128, DEPTH, KT, GROUPS, 3).transpose(1, 3, 4, 2, 0).reshape(DEPTH, GROUPS, 3, DM)
    return (rows(y[..., :HALF_P]).reshape(1, SEQ, DM), rows(y[..., HALF_P:]).reshape(DB, DS, DM),
            np.asarray(r["ret_p_out"]).reshape(DEPTH, 1, HEADS, DK, DV), lru[:, :1], conv[:, :1],
            np.asarray(r["ret_s_out"]), lru[:, 1:], conv[:, 1:])
```
